# Optimizing a Trainium2 kernel written in Bass

```python
import math
import jax
import jax.numpy as jnp
from jax import lax
import numpy as np

D_MODEL = 2048
BATCH = 1
SEQ = 1024
DEPTH = 1
DEC_BATCH = 8
DEC_SEQ = 4
PAST_LEN = 512
PAGE_SIZE = 128

D_MIX = D_MODEL
D_ATT = D_MIX // 2
D_SSM = D_MIX // 4
D_MEM = D_MIX - D_ATT - D_SSM
HEAD_DIM = 128
N_HEADS = D_ATT // HEAD_DIM
N_KV_HEADS = 2
GQA = N_HEADS // N_KV_HEADS
N_IDX_HEADS = 16
IDX_DIM = 64
MAX_TOPK = 256
Q_BLOCK = 128
SSM_GROUP = 16
N_SSM_GROUPS = D_SSM // SSM_GROUP
SSM_STATE = 64
N_MEM = 256
N_MEM_HEADS = 4
MEM_HEAD_DIM = D_MEM // N_MEM_HEADS
EPS = 1e-6
SPLITS = (D_ATT, N_KV_HEADS * HEAD_DIM, N_KV_HEADS * HEAD_DIM, D_ATT, N_IDX_HEADS * IDX_DIM, IDX_DIM, N_IDX_HEADS, D_SSM, D_SSM, D_MEM, D_MEM)
D_IN = D_ATT * 2 + N_KV_HEADS * HEAD_DIM * 2 + N_IDX_HEADS * IDX_DIM + IDX_DIM + N_IDX_HEADS + D_SSM * 2 + D_MEM * 2

kernel_name = 'hymba_dsa_s5_memory_decoder_step'

def rmsnorm(x, g):
    xf = x.astype(jnp.float32)
    y = xf * lax.rsqrt(jnp.mean(xf * xf, axis=-1, keepdims=True) + EPS)
    return (y * g.astype(jnp.float32)).astype(x.dtype)

def alibi_slopes():
    return jnp.power(2.0, -8.0 * jnp.arange(1, N_HEADS + 1, dtype=jnp.float32) / N_HEADS)

def project(x, g_norm, w_in):
    h = rmsnorm(x, g_norm)
    z = h @ w_in
    offs = [int(o) for o in np.cumsum(SPLITS)[:-1]]
    return jnp.split(z, offs, axis=-1)

def dsa_attend(q, qi, wi, q_pos, k, v, ki, k_pos, topk):
    f32 = jnp.float32
    rel = jax.nn.relu(jnp.einsum('bthd,bsd->bths', qi.astype(f32), ki.astype(f32)) * (IDX_DIM ** -0.5))
    score = jnp.einsum('bth,bths->bts', wi.astype(f32) * (N_IDX_HEADS ** -0.5), rel)
    causal = k_pos[None, :] <= q_pos[:, None]
    score = jnp.where(causal[None], score, -jnp.inf)
    _, idx = lax.top_k(score, topk)
    sel_pos = k_pos[idx]
    valid = sel_pos <= q_pos[None, :, None]
    gather = jax.vmap(lambda rows, ii: rows[ii])
    k_sel = gather(k, idx).astype(f32)
    v_sel = gather(v, idx).astype(f32)
    b, t = q.shape[0], q.shape[1]
    qg = q.reshape(b, t, N_KV_HEADS, GQA, HEAD_DIM).astype(f32)
    s = jnp.einsum('btkgd,btskd->btkgs', qg, k_sel) * (HEAD_DIM ** -0.5)
    dist = (q_pos[None, :, None] - sel_pos).astype(f32)
    slopes = alibi_slopes().reshape(N_KV_HEADS, GQA)
    s = s - slopes[None, None, :, :, None] * dist[:, :, None, None, :]
    s = jnp.where(valid[:, :, None, None, :], s, -jnp.inf)
    p = jax.nn.softmax(s, axis=-1)
    o = jnp.einsum('btkgs,btskd->btkgd', p, v_sel)
    return o.reshape(b, t, N_HEADS * HEAD_DIM).astype(q.dtype)

def dsa_prompt(q, qi, wi, k, v, ki):
    b, L = q.shape[0], q.shape[1]
    nb = L // Q_BLOCK
    pos = jnp.arange(L, dtype=jnp.int32)
    topk = min(MAX_TOPK, L // 4)

    def blocks(a):
        return jnp.moveaxis(a.reshape((b, nb, Q_BLOCK) + a.shape[2:]), 1, 0)

    def step(args):
        qb, qib, wib, pb = args
        return dsa_attend(qb, qib, wib, pb, k, v, ki, pos, topk)

    o = lax.map(step, (blocks(q), blocks(qi), blocks(wi), pos.reshape(nb, Q_BLOCK)))
    return jnp.moveaxis(o, 0, 1).reshape(b, L, D_ATT)

def _complex_linear_combine(e1, e2):
    a1r, a1i, b1r, b1i = e1
    a2r, a2i, b2r, b2i = e2
    return (a1r * a2r - a1i * a2i, a1r * a2i + a1i * a2r,
            a2r * b1r - a2i * b1i + b2r, a2r * b1i + a2i * b1r + b2i)

def s5_branch(u, h0_re, h0_im, lam_re, lam_im, log_dt, b_re, b_im, c_re, c_im, d_skip, w_glu):
    f32 = jnp.float32
    b, t = u.shape[0], u.shape[1]
    uf = u.astype(f32).reshape(b, t, N_SSM_GROUPS, SSM_GROUP)
    lr, li = lam_re.astype(f32), lam_im.astype(f32)
    dt = jnp.exp(log_dt.astype(f32))[:, None]
    mag = jnp.exp(lr * dt)
    ar, ai = mag * jnp.cos(li * dt), mag * jnp.sin(li * dt)
    den = lr * lr + li * li
    cr = (lr * (ar - 1.0) + li * ai) / den
    ci = (lr * ai - li * (ar - 1.0)) / den
    br, bi = b_re.astype(f32), b_im.astype(f32)
    bbr = cr[..., None] * br - ci[..., None] * bi
    bbi = cr[..., None] * bi + ci[..., None] * br
    xr = jnp.einsum('btgc,gnc->btgn', uf, bbr)
    xi = jnp.einsum('btgc,gnc->btgn', uf, bbi)
    h0r, h0i = h0_re.astype(f32), h0_im.astype(f32)
    xr = xr.at[:, 0].add(ar * h0r - ai * h0i)
    xi = xi.at[:, 0].add(ar * h0i + ai * h0r)
    a_r = jnp.broadcast_to(ar, xr.shape)
    a_i = jnp.broadcast_to(ai, xr.shape)
    _, _, hr, hi = lax.associative_scan(_complex_linear_combine, (a_r, a_i, xr, xi), axis=1)
    y = (jnp.einsum('btgn,gcn->btgc', hr, c_re.astype(f32))
         - jnp.einsum('btgn,gcn->btgc', hi, c_im.astype(f32))
         + d_skip.astype(f32) * uf)
    y = jax.nn.gelu(y.reshape(b, t, D_SSM))
    a, g = jnp.split(y @ w_glu.astype(f32), 2, axis=-1)
    out = a * jax.nn.sigmoid(g)
    return out.astype(u.dtype), hr[:, -1].astype(h0_re.dtype), hi[:, -1].astype(h0_im.dtype)

def mem_kv(mem, g_mem, w_mem_kv):
    b = mem.shape[0]
    kv = rmsnorm(mem, g_mem) @ w_mem_kv
    mk, mv = jnp.split(kv, 2, axis=-1)
    return (mk.reshape(b, N_MEM, N_MEM_HEADS, MEM_HEAD_DIM),
            mv.reshape(b, N_MEM, N_MEM_HEADS, MEM_HEAD_DIM))

def mem_attend(qm, mk, mv):
    f32 = jnp.float32
    b, t = qm.shape[0], qm.shape[1]
    q = qm.reshape(b, t, N_MEM_HEADS, MEM_HEAD_DIM).astype(f32)
    s = jnp.einsum('bthd,bmhd->bhtm', q, mk.astype(f32)) * (MEM_HEAD_DIM ** -0.5)
    p = jax.nn.softmax(s, axis=-1)
    o = jnp.einsum('bhtm,bmhd->bthd', p, mv.astype(f32))
    return o.reshape(b, t, D_MEM).astype(qm.dtype)

def gather_pages(pool, page_table):
    pages = pool[page_table]
    db, n_pages = page_table.shape
    return pages.reshape((db, n_pages * pool.shape[1]) + pool.shape[2:])

def mixer_layer(x, past, h0_re, h0_im, mem_k, mem_v, g_norm, w_in, lam_re, lam_im, log_dt,
                b_re, b_im, c_re, c_im, d_skip, w_glu, w_out):
    b, t = x.shape[0], x.shape[1]
    q, k, v, gate_a, qi, ki, wi, u, gate_s, qm, gate_m = project(x, g_norm, w_in)
    q = q.reshape(b, t, N_HEADS, HEAD_DIM)
    k = k.reshape(b, t, N_KV_HEADS, HEAD_DIM)
    v = v.reshape(b, t, N_KV_HEADS, HEAD_DIM)
    qi = qi.reshape(b, t, N_IDX_HEADS, IDX_DIM)
    if past is None:
        o_a = dsa_prompt(q, qi, wi, k, v, ki)
    else:
        k_past, v_past, ki_past = past
        l_past = k_past.shape[1]
        k_all = jnp.concatenate([k_past, k.astype(k_past.dtype)], axis=1)
        v_all = jnp.concatenate([v_past, v.astype(v_past.dtype)], axis=1)
        ki_all = jnp.concatenate([ki_past, ki.astype(ki_past.dtype)], axis=1)
        q_pos = l_past + jnp.arange(t, dtype=jnp.int32)
        k_pos = jnp.arange(l_past + t, dtype=jnp.int32)
        topk = min(MAX_TOPK, (l_past + t) // 4)
        o_a = dsa_attend(q, qi, wi, q_pos, k_all, v_all, ki_all, k_pos, topk)
    o_s, h_re, h_im = s5_branch(u, h0_re, h0_im, lam_re, lam_im, log_dt, b_re, b_im, c_re, c_im, d_skip, w_glu)
    o_m = mem_attend(qm, mem_k, mem_v)
    mix = jnp.concatenate([o_a * jax.nn.silu(gate_a), o_s * jax.nn.silu(gate_s), o_m * jax.nn.silu(gate_m)], axis=-1)
    y = x + mix @ w_out
    return y, k, v, ki, h_re, h_im

def setup_inputs(seed: int = 0) -> dict:
    key = jax.random.key(seed)
    ks = jax.random.split(key, 32)
    f32 = jnp.float32
    n_pages = PAST_LEN // PAGE_SIZE
    n_used = DEC_BATCH * n_pages
    n_pool = n_used + max(1, n_used // 4)

    def nrm(k, shape, s=1.0):
        return s * jax.random.normal(k, shape, f32)

    page_table = jax.random.permutation(ks[0], n_pool)[:n_used].reshape(DEC_BATCH, n_pages).astype(jnp.int32)
    lam_im0 = math.pi * jnp.arange(SSM_STATE, dtype=f32)
    return {
        'x_prompt': nrm(ks[1], (BATCH, SEQ, D_MODEL)),
        'x_sample': nrm(ks[2], (DEC_BATCH, DEC_SEQ, D_MODEL)),
        'mem_prompt': nrm(ks[3], (BATCH, N_MEM, D_MODEL)),
        'cache_k': nrm(ks[4], (DEPTH, n_pool, PAGE_SIZE, N_KV_HEADS, HEAD_DIM)),
        'cache_v': nrm(ks[5], (DEPTH, n_pool, PAGE_SIZE, N_KV_HEADS, HEAD_DIM)),
        'cache_kidx': nrm(ks[6], (DEPTH, n_pool, PAGE_SIZE, IDX_DIM)),
        'cache_mem_k': nrm(ks[7], (DEPTH, DEC_BATCH, N_MEM, N_MEM_HEADS, MEM_HEAD_DIM)),
        'cache_mem_v': nrm(ks[8], (DEPTH, DEC_BATCH, N_MEM, N_MEM_HEADS, MEM_HEAD_DIM)),
        'state_ssm_re': nrm(ks[9], (DEPTH, DEC_BATCH, N_SSM_GROUPS, SSM_STATE), 0.3),
        'state_ssm_im': nrm(ks[10], (DEPTH, DEC_BATCH, N_SSM_GROUPS, SSM_STATE), 0.3),
        'page_table': page_table,
        'g_norm': 1.0 + nrm(ks[11], (DEPTH, D_MODEL), 0.02),
        'w_in': nrm(ks[12], (DEPTH, D_MODEL, D_IN), D_MODEL ** -0.5),
        'g_mem': 1.0 + nrm(ks[13], (DEPTH, D_MODEL), 0.02),
        'w_mem_kv': nrm(ks[14], (DEPTH, D_MODEL, 2 * D_MEM), D_MODEL ** -0.5),
        'lam_re': -0.5 + nrm(ks[15], (DEPTH, N_SSM_GROUPS, SSM_STATE), 0.01),
        'lam_im': lam_im0 + nrm(ks[16], (DEPTH, N_SSM_GROUPS, SSM_STATE), 0.01),
        'log_dt': jax.random.uniform(ks[17], (DEPTH, N_SSM_GROUPS), f32, math.log(1e-3), math.log(1e-1)),
        'b_re': nrm(ks[18], (DEPTH, N_SSM_GROUPS, SSM_STATE, SSM_GROUP), (2 * SSM_GROUP) ** -0.5),
        'b_im': nrm(ks[19], (DEPTH, N_SSM_GROUPS, SSM_STATE, SSM_GROUP), (2 * SSM_GROUP) ** -0.5),
        'c_re': nrm(ks[20], (DEPTH, N_SSM_GROUPS, SSM_GROUP, SSM_STATE), SSM_STATE ** -0.5),
        'c_im': nrm(ks[21], (DEPTH, N_SSM_GROUPS, SSM_GROUP, SSM_STATE), SSM_STATE ** -0.5),
        'd_skip': nrm(ks[22], (DEPTH, N_SSM_GROUPS, SSM_GROUP)),
        'w_glu': nrm(ks[23], (DEPTH, D_SSM, 2 * D_SSM), D_SSM ** -0.5),
        'w_out': nrm(ks[24], (DEPTH, D_MIX, D_MODEL), D_MIX ** -0.5),
        'g_final': 1.0 + nrm(ks[25], (D_MODEL,), 0.02),
    }

def reference(x_prompt, x_sample, mem_prompt, cache_k, cache_v, cache_kidx, cache_mem_k, cache_mem_v,
              state_ssm_re, state_ssm_im, page_table, g_norm, w_in, g_mem, w_mem_kv, lam_re, lam_im,
              log_dt, b_re, b_im, c_re, c_im, d_skip, w_glu, w_out, g_final):
    hp, hs = x_prompt, x_sample
    zeros_h = jnp.zeros((x_prompt.shape[0], N_SSM_GROUPS, SSM_STATE), state_ssm_re.dtype)
    kp_l, vp_l, kip_l, mkp_l, mvp_l, hrp_l, hip_l = [], [], [], [], [], [], []
    ks_l, vs_l, kis_l, hrs_l, his_l = [], [], [], [], []
    for l in range(DEPTH):
        ssm_w = (lam_re[l], lam_im[l], log_dt[l], b_re[l], b_im[l], c_re[l], c_im[l], d_skip[l], w_glu[l], w_out[l])
        mk_p, mv_p = mem_kv(mem_prompt, g_mem[l], w_mem_kv[l])
        hp, kp, vp, kip, hrp, hip = mixer_layer(hp, None, zeros_h, zeros_h, mk_p, mv_p, g_norm[l], w_in[l], *ssm_w)
        past = (gather_pages(cache_k[l], page_table), gather_pages(cache_v[l], page_table),
                gather_pages(cache_kidx[l], page_table))
        hs, ksn, vsn, kisn, hrs, his = mixer_layer(hs, past, state_ssm_re[l], state_ssm_im[l], cache_mem_k[l],
                                                 cache_mem_v[l], g_norm[l], w_in[l], *ssm_w)
        kp_l.append(kp); vp_l.append(vp); kip_l.append(kip); mkp_l.append(mk_p); mvp_l.append(mv_p)
        hrp_l.append(hrp); hip_l.append(hip)
        ks_l.append(ksn); vs_l.append(vsn); kis_l.append(kisn); hrs_l.append(hrs); his_l.append(his)
    y_prompt = rmsnorm(hp, g_final)
    y_sample = rmsnorm(hs, g_final)
    new_k_prompt = jnp.stack(kp_l)
    new_v_prompt = jnp.stack(vp_l)
    new_kidx_prompt = jnp.stack(kip_l)
    new_mem_k_prompt = jnp.stack(mkp_l)
    new_mem_v_prompt = jnp.stack(mvp_l)
    new_ssm_re_prompt = jnp.stack(hrp_l)
    new_ssm_im_prompt = jnp.stack(hip_l)
    new_k_sample = jnp.stack(ks_l)
    new_v_sample = jnp.stack(vs_l)
    new_kidx_sample = jnp.stack(kis_l)
    new_ssm_re_sample = jnp.stack(hrs_l)
    new_ssm_im_sample = jnp.stack(his_l)
    return (y_prompt, y_sample, new_k_prompt, new_v_prompt, new_kidx_prompt, new_mem_k_prompt, new_mem_v_prompt,
            new_ssm_re_prompt, new_ssm_im_prompt, new_k_sample, new_v_sample, new_kidx_sample,
            new_ssm_re_sample, new_ssm_im_sample)


_drawn_inputs = setup_inputs


def setup_inputs(seed=0):
    import zlib

    import numpy as np

    out = dict(_drawn_inputs(seed))
    spreads = {}
    factors = {'g_mem': 7.746, 'lam_re': 13.397, 'g_final': 7.345}
    for name, (base, spread) in spreads.items():
        noise = np.random.default_rng([zlib.crc32(name.encode()), seed]).standard_normal(out[name].shape)
        drawn = base * np.exp(spread * noise) if base else spread * noise
        out[name] = jnp.asarray(drawn.astype(out[name].dtype))
    for name, factor in factors.items():
        out[name] = (out[name] * factor).astype(out[name].dtype)
    return out
```

```python
import math
from contextlib import ExitStack

import numpy as np

import concourse.bass as bass
from concourse import mybir

F32 = mybir.dt.float32
F16 = mybir.dt.float16
BF16 = mybir.dt.bfloat16
I32 = mybir.dt.int32
ALU = mybir.AluOpType
ACT = mybir.ActivationFunctionType
AX_X = mybir.AxisListType.X

P = 128
D_MODEL, SEQ, DEC_BATCH, DEC_SEQ, PAST_LEN, PAGE = 2048, 1024, 8, 4, 512, 128
HEAD_DIM, N_HEADS, N_KV, GQA = 128, 8, 2, 4
N_IDX, IDX_DIM = 16, 64
GROUPS, GROUP, STATE = 32, 16, 64
N_MEM, N_MEM_HEADS = 256, 4
D_SSM = D_MEM = 512
EPS = 1e-6
TOPK = min(256, SEQ // 4)
TOPK_S = min(256, (PAST_LEN + DEC_SEQ) // 4)
KT = D_MODEL // P
NS = DEC_BATCH * DEC_SEQ
TOK = SEQ + NS
QT = SEQ // P
PIECES = [(TOK // 3 * n, TOK // 3) for n in range(3)]
STEPS = [(0, 512), (512, 512), (SEQ, NS)]
OFF_Q, OFF_K, OFF_V, OFF_GA = 0, 1024, 1280, 1536
OFF_QI, OFF_KI, OFF_U, OFF_GS, OFF_QM, OFF_GM = 2560, 3584, 3664, 4176, 4688, 5200
KIWI = IDX_DIM + N_IDX
SLAB = 256
CHUNK = 128
ROOT_H = 256.0
W_SHIFT = 2.0 ** -14
TINY = 1e-30
LOOPS = 4
KEPT = [OFF_Q + SLAB * s for s in range(6)] + [OFF_QM, OFF_QM + SLAB]
GATE = [OFF_GA + SLAB * s for s in range(4)] + [OFF_GS, OFF_GS + SLAB, OFF_GM, OFF_GM + SLAB]
LOOP_SLABS = [c for s in range(0, 8, 2) for c in (KEPT[s], GATE[s], KEPT[s + 1], GATE[s + 1])]


def stored(col):
    for n, c in enumerate(LOOP_SLABS):
        if c <= col < c + SLAB:
            return 2 * n + (col - c) // P
    raise ValueError(col)


TILES = 16
LO = 32
INVALID, PAD, REPLACED, CUT, FAR = -2e38, -2.2e38, -3e38, -2.5e38, -1e30
IDX_TILES = list(range(TOPK // P, QT))
IDX_OFF = {t: P * sum(x + 1 for x in IDX_TILES if x < t) for t in IDX_TILES}
IDX_COLS = P * sum(x + 1 for x in IDX_TILES)
ROUNDS = TOPK // 8
TWO_PI = 2 * np.pi
PI_A = 6.28125
PI_B = float(np.float32(np.round((TWO_PI - PI_A) * 2**20) / 2**20))
PI_C = float(np.float32(TWO_PI - PI_A - PI_B))
MAGIC = 1.5 * 2**23
PI_IN = float(np.nextafter(np.float32(np.pi), np.float32(0)))


class Link:

    def __init__(self, eng, sem, base=0):
        self.eng, self.sem, self.base, self.n = eng, sem, base, 0

    def __call__(self, ins):
        ins.then_inc(self.sem, 1)
        self.n += 1
        self.eng.wait_ge(self.sem, self.base + self.n)
        return ins


def build_program(nc, io):
    top = ExitStack()

    def sb_in(ctx, name, shape, dt=F32):
        return ctx.enter_context(nc.sbuf_tensor(name, shape, dt))

    def sem(name):
        return top.enter_context(nc.semaphore(name))

    with top:
        ps = top.enter_context(nc.psum_tensor("ps", [P, 8, 512], F32))
        z_dram = nc.dram_tensor("z_scratch", (len(LOOP_SLABS) * 2, P, TOK), F32, kind="Internal").ap()
        y_dram = nc.dram_tensor("y_scratch", (4, P, TOK), F32, kind="Internal").ap()

        ident = sb_in(top, "ident", [P, P])
        wis = sb_in(top, "wis", [P, QT + 1, N_IDX])
        cmin = sb_in(top, "cmin", [P, P])
        score = sb_in(top, "score", [P, IDX_COLS])
        ones = sb_in(top, "ones", [P, P])
        qi_s = sb_in(top, "qi_s", [P, N_IDX // 2, NS])
        kiT = sb_in(top, "kiT", [P, 2, TOK])

        mid = ExitStack()
        with mid:
            h16 = sb_in(mid, "h16", [P, 2, KT, TOK], F16)
            h_unit = sb_in(mid, "h_unit", [P, 1])
            par = sb_in(mid, "par", [P, 5, TILES])
            tabs = sb_in(mid, "tabs", [P, 2, TILES, 2, LO])
            bbar = sb_in(mid, "bbar", [P, 2, TILES, GROUP])
            cnat = sb_in(mid, "cnat", [P, 2, 4, STATE])
            dcol = sb_in(mid, "dcol", [P, 4])
            mask_c = sb_in(mid, "mask_c", [P, 8])
            mask_b = sb_in(mid, "mask_b", [P, 4, 8])
            h0 = sb_in(mid, "h0", [P, 2, DEC_BATCH, TILES])
            h_last = sb_in(mid, "h_last", [P, 2, 1 + DEC_BATCH, TILES])
            lam = sb_in(mid, "lam", [P, 3, TILES])
            bnat = sb_in(mid, "bnat", [P, 2, TILES, GROUP])
            pw = sb_in(mid, "pw", [P, 10])
            block_a(nc, io, locals(), sem, sb_in)
            block_b(nc, io, locals(), sem, sb_in)
        late = ExitStack()
        with late:
            mixT = sb_in(late, "mixT", [P, KT, TOK])
            with ExitStack() as heads:
                kT = sb_in(heads, "kT", [P, N_KV, TOK])
                with ExitStack() as by_token:
                    kv_tok = sb_in(by_token, "kv_tok", [P, QT + 1, 2 * N_KV * HEAD_DIM])
                    block_c(nc, io, locals(), sem, sb_in)
                    block_d(nc, io, locals(), sem, sb_in)
                block_e(nc, io, locals(), sem, sb_in)
            block_f(nc, io, locals(), sem, sb_in)


def block_a(nc, io, v, sem, sb_in):
    ident, cmin, h16, h_unit, par, tabs, bbar = (v[n] for n in ("ident", "cmin", "h16", "h_unit", "par", "tabs", "bbar"))
    cnat, dcol, mask_c, mask_b, h0, ps = (v[n] for n in ("cnat", "dcol", "mask_c", "mask_b", "h0", "ps"))
    lam, bnat, pw = (v[n] for n in ("lam", "bnat", "pw"))
    own = ExitStack()
    with own:
        sb = lambda name, shape: sb_in(own, name, shape)
        x_in = sb("x_in", [P, 2, D_MODEL])
        h_tok = sb("h_tok", [P, 2, D_MODEL])
        g_b = sb("g_b", [P, 2, D_MODEL])
        g_max = sb("g_max", [P, 2])
        memT = sb("memT", [P, KT, N_MEM])
        w_kv = sb("w_kv", [P, 4, 2 * D_MEM])
        kv_mem = sb("kv_mem", [P, 2, 2 * D_MEM])
        sq = v["score"][:, 0:D_MODEL]
        stat = sb("stat_a", [P, 3, QT + 3])
        rms = sb("rms_a", [P, QT + 3])
        lam_in = sb("lam_in", [TILES, 3, P])
        dt_in = sb("dt_in", [TILES, 2])
        d_in = sb("d_in", [4, P])
        st_in = sb("st_in", [DEC_BATCH * TILES, 2, P])

        x_loaded = [sem(f"x_loaded{b}") for b in range(2)]
        g_loaded = [sem("g_mem_loaded"), sem("g_norm_loaded")]
        w_kv_loaded = [sem(f"w_kv_loaded{b}") for b in range(4)]
        kv_step = sem("kv_step")
        kv_evac = sem("kv_evac")
        kv_stored = sem("kv_stored")
        params_loaded = sem("params_loaded")
        squares = sem("squares")
        mean_sq = sem("mean_sq")
        root = sem("root")
        h_ready = sem("h_ready")
        h_transposed = sem("h_transposed")
        evac_a = [sem("evac_even"), sem("evac_odd")]
        high_made = sem("high_made")
        ident_zero = sem("ident_zero")
        ident_ready = sem("ident_ready")
        pool_link = sem("pool_link_a")
        consts_ready = sem("consts_ready")
        lam_ready = sem("lam_ready")
        dt_spread = sem("dt_spread")
        st_transposed = sem("st_transposed")
        dve_link = sem("dve_link_a")

        MT = N_MEM // P
        ALL = MT + QT + 1

        def rows(t):
            return P if t < ALL - 1 else NS

        def source(t):
            if t < MT:
                return io["mem_prompt"][0, t * P:(t + 1) * P, :]
            if t < MT + QT:
                return io["x_prompt"][0, (t - MT) * P:(t - MT + 1) * P, :]
            return io["x_sample"].rearrange("b s d -> (b s) d")


        block = own.enter_context(nc.Block(name="setup"))

        @block.sync
        def _(sp):
            for t in range(ALL):
                b, n = t % 2, rows(t)
                if t < 2:
                    g = io["g_norm" if t else "g_mem"]
                    sp.dma_start(g_b[:, t, :], g[0].partition_broadcast(P)).then_inc(g_loaded[t], 16)
                if t >= 2:
                    sp.wait_ge(squares, t - 1)
                    sp.wait_ge(h_ready, t - 1)
                sp.dma_start(x_in[0:n, b, :], source(t)).then_inc(x_loaded[b], 16)
                for k in range(2 * (t - 1), 2 * t) if 1 <= t <= KT // 2 else ():
                    if k >= 4:
                        sp.wait_ge(kv_step, k - 3)
                    sp.dma_start(w_kv[:, k % 4, :], io["w_mem_kv"][0, k * P:(k + 1) * P, :]).then_inc(w_kv_loaded[k % 4], 16)

        @block.gpsimd
        def _(pool):
            link = Link(pool, pool_link)
            pool.dma_start(lam_in[:, 0, :], io["lam_re"][0].rearrange("(i a) n -> i (a n)", a=2)).then_inc(params_loaded, 16)
            pool.dma_start(lam_in[:, 1, :], io["lam_im"][0].rearrange("(i a) n -> i (a n)", a=2)).then_inc(params_loaded, 16)
            pool.dma_start(dt_in[:], io["log_dt"][0].rearrange("(i a) -> i a", a=2)).then_inc(params_loaded, 16)
            for n, name in enumerate(("b_re", "b_im")):
                pool.dma_start(bnat[:, n, :, :], io[name][0].rearrange("(i a) n c -> (a n) i c", a=2)).then_inc(params_loaded, 16)
            for n, name in enumerate(("c_re", "c_im")):
                src = io[name][0].rearrange("(j g) c n -> (g c) j n", j=4)
                pool.dma_start(cnat[:, n, :, :], src).then_inc(params_loaded, 16)
            for n, name in enumerate(("state_ssm_re", "state_ssm_im")):
                pool.dma_start(st_in[:, n, :], io[name][0].rearrange("b (i a) n -> (b i) (a n)", a=2)).then_inc(params_loaded, 16)
            pool.dma_start(d_in[:], io["d_skip"][0].rearrange("(j g) c -> j (g c)", j=4)).then_inc(params_loaded, 16)
            link(nc.gpsimd.memset(ident[:], 0.0))
            nc.gpsimd.affine_select(out=ident[:], in_=ident[:], compare_op=ALU.not_equal, fill=1.0, base=0,
                                    pattern=[[-1, P]], channel_multiplier=1).then_inc(ident_ready, 1)
            link(nc.gpsimd.memset(cmin[:], 3e38))
            link(nc.gpsimd.affine_select(out=cmin[:], in_=cmin[:], compare_op=ALU.is_ge, fill=INVALID, base=0,
                                         pattern=[[-1, P]], channel_multiplier=1))
            link(nc.gpsimd.memset(mask_c[:], 1.0))
            link(nc.gpsimd.affine_select(out=mask_c[:], in_=mask_c[:], compare_op=ALU.is_ge, fill=0.0, base=0,
                                         pattern=[[-GROUP, 8]], channel_multiplier=1))
            link(nc.gpsimd.affine_select(out=mask_c[:], in_=mask_c[:], compare_op=ALU.is_ge, fill=0.0, base=GROUP - 1,
                                         pattern=[[GROUP, 8]], channel_multiplier=-1))
            link(nc.gpsimd.memset(mask_b[:], 0.0))
            for r in range(4):
                for a in range(2):
                    link(nc.gpsimd.memset(mask_b[a * STATE:(a + 1) * STATE, r, 2 * r + a:2 * r + a + 1], 1.0))
            for k in range(10):
                link(nc.gpsimd.memset(pw[:, k:k + 1], float(2**k)))
            kiT = v["kiT"]
            link(nc.gpsimd.memset(kiT[IDX_DIM:P, 0, :], 0.0))
            link(nc.gpsimd.memset(kiT[0:IDX_DIM, 1, :], 0.0))
            nc.gpsimd.memset(v["ones"][:], 1.0).then_inc(consts_ready, 1)

        def evac(eng, copy, parity, t):
            n = rows(t)
            if t < MT:
                for q in range(parity, 4, 2):
                    eng.wait_ge(h_transposed, 4 * t + q + 1)
                    src = ps[:, q, :].rearrange("p (j n) -> p j n", j=4)[:, :, 0:n]
                    copy(memT[:, 4 * q:4 * q + 4, t * P:t * P + n], src).then_inc(evac_a[parity], 1)
                return
            at = (t - MT) * P
            for q in range(4):
                src = ps[:, q, :].rearrange("p (j n) -> p j n", j=4)[:, :, 0:n]
                high = h16[:, 0, 4 * q:4 * q + 4, at:at + n]
                if parity == 0:
                    eng.wait_ge(h_transposed, 4 * t + q + 1)
                    copy(high, src).then_inc(high_made, 1)
                else:
                    eng.wait_ge(high_made, 4 * (t - MT) + q + 1)
                    nc.vector.tensor_tensor(h16[:, 1, 4 * q:4 * q + 4, at:at + n], src, high, ALU.subtract).then_inc(evac_a[q % 2], 1)

        @block.scalar
        def _(act):
            for t in range(ALL + 1):
                if t < ALL:
                    b, n = t % 2, rows(t)
                    act.wait_ge(x_loaded[b], 16 * (t // 2 + 1))
                    nc.scalar.activation(sq[0:n, :], x_in[0:n, b, :], ACT.Square,
                                         accum_out=stat[0:n, 0, t:t + 1]).then_inc(squares, 1)
                    act.wait_ge(mean_sq, t + 1)
                    nc.scalar.activation(rms[0:n, t:t + 1], stat[0:n, 1, t:t + 1], ACT.Sqrt).then_inc(root, 1)
                if t >= 1:
                    evac(act, nc.scalar.copy, 0, t - 1)
            for a in range(MT):
                act.wait_ge(kv_step, KT)
                src = ps[:, 4 + 2 * a:6 + 2 * a, :].rearrange("p a n -> p (a n)")
                nc.scalar.activation(kv_mem[:, a, :], src, ACT.Copy).then_inc(kv_evac, 1)
            act.wait_ge(kv_evac, MT)
            for n, name in enumerate(("out_mk", "out_mv")):
                dst = io[name][0, 0].rearrange("(a p) h d -> p a (h d)", p=P)
                act.dma_start(dst, kv_mem[:, :, n * D_MEM:(n + 1) * D_MEM]).then_inc(kv_stored, 16)
            act.wait_ge(kv_stored, 32)

        @block.vector
        def _(dve):
            link = Link(dve, dve_link)
            dve_copy = nc.vector.tensor_copy
            for t in range(ALL + 1):
                if t < ALL:
                    b, n = t % 2, rows(t)
                    dve.wait_ge(squares, t + 1)
                    nc.vector.tensor_scalar(stat[0:n, 1, t:t + 1], stat[0:n, 0, t:t + 1], 1.0 / D_MODEL, EPS,
                                            ALU.mult, ALU.add).then_inc(mean_sq, 1)
                    dve.wait_ge(root, t + 1)
                    link(nc.vector.reciprocal(stat[0:n, 2, t:t + 1], rms[0:n, t:t + 1]))
                    if t == 0:
                        dve.wait_ge(g_loaded[0], 16)
                        dve.wait_ge(g_loaded[1], 16)
                        g = g_b[:, 1, :]
                        nc.vector.tensor_reduce(g_max[:, 0:1], g, AX_X, ALU.max)
                        link(nc.vector.tensor_reduce(g_max[:, 1:2], g, AX_X, ALU.min))
                        link(nc.vector.tensor_scalar(g_max[:, 1:2], g_max[:, 1:2], -1.0, TINY, ALU.mult, ALU.max))
                        link(nc.vector.tensor_tensor(g_max[:, 0:1], g_max[:, 0:1], g_max[:, 1:2], ALU.max))
                        link(nc.vector.tensor_scalar(h_unit[:], g_max[:, 0:1], 1.0 / ROOT_H, None, ALU.mult))
                        link(nc.vector.reciprocal(g_max[:, 1:2], h_unit[:]))
                        link(nc.vector.tensor_scalar(g, g, g_max[:, 1:2], None, ALU.mult))
                    if t >= 2:
                        dve.wait_ge(h_transposed, 4 * (t - 1))
                    nc.vector.scalar_tensor_tensor(out=h_tok[0:n, b, :], in0=x_in[0:n, b, :], scalar=stat[0:n, 2, t:t + 1],
                                                   in1=g_b[0:n, int(t >= MT), :], op0=ALU.mult, op1=ALU.mult).then_inc(h_ready, 1)
                if t >= 1:
                    evac(dve, dve_copy, 1, t - 1)
            dve.wait_ge(params_loaded, 10 * 16)
            dve_copy(lam_in[:, 2, :].rearrange("i (a n) -> i a n", a=2),
                     dt_in[:].unsqueeze(2).to_broadcast([TILES, 2, STATE])).then_inc(dt_spread, 1)
            dve.wait_ge(st_transposed, 1)
            dve_copy(lam[:], ps[:, 5, 0:3 * TILES].rearrange("p (a i) -> p a i", a=3)).then_inc(lam_ready, 1)
            dve_copy(dcol[:], ps[:, 5, 64:68])
            src = ps[:, 4, 0:2 * TILES * DEC_BATCH].rearrange("p (a b i) -> p a b i", a=2, i=TILES)
            dve_copy(h0[:], src)

        @block.tensor
        def _(pe):
            pe.wait_ge(ident_ready, 1)
            for t in range(ALL):
                b, n = t % 2, rows(t)
                pe.wait_ge(h_ready, t + 1)
                for q in range(4):
                    if t >= 1:
                        pe.wait_ge(evac_a[q % 2], 2 * (t - 1) + q // 2 + 1)
                    for j in range(4):
                        c = 4 * q + j
                        last = nc.tensor.transpose(ps[:, q, j * P:j * P + n], h_tok[0:n, b, c * P:(c + 1) * P],
                                                   ident[0:n, 0:n])
                    last.then_inc(h_transposed, 1)
                if t >= MT and 2 * (t - MT) < KT:
                    if t == MT:
                        for parity in range(2):
                            pe.wait_ge(evac_a[parity], 2 * MT)
                    for k in range(2 * (t - MT), 2 * (t - MT) + 2):
                        pe.wait_ge(w_kv_loaded[k % 4], 16 * (k // 4 + 1))
                        for a in range(MT):
                            for half in range(2):
                                last = nc.tensor.matmul(ps[:, 4 + 2 * a + half, :], memT[:, k, a * P:(a + 1) * P],
                                                        w_kv[:, k % 4, half * 512:(half + 1) * 512],
                                                        start=(k == 0), stop=(k == KT - 1))
                        last.then_inc(kv_step, 1)
            pe.wait_ge(params_loaded, 10 * 16)
            pe.wait_ge(kv_evac, MT)
            for a in range(2):
                last = nc.tensor.transpose(ps[:, 4, a * P:(a + 1) * P], st_in[:, a, :], ident[:])
            nc.tensor.transpose(ps[:, 5, 64:68], d_in[:], ident[0:4, 0:4])
            pe.wait_ge(dt_spread, 1)
            for a in range(3):
                last = nc.tensor.transpose(ps[:, 5, a * TILES:(a + 1) * TILES], lam_in[:, a, :], ident[0:TILES, 0:TILES])
            last.then_inc(st_transposed, 1)



def block_b(nc, io, v, sem, sb_in):
    ident, cmin, h16, h_unit, par, tabs, bbar = (v[n] for n in ("ident", "cmin", "h16", "h_unit", "par", "tabs", "bbar"))
    cnat, dcol, mask_c, mask_b, h0, ps = (v[n] for n in ("cnat", "dcol", "mask_c", "mask_b", "h0", "ps"))
    wis, score, qi_s, kiT, h_last, ones = (v[n] for n in ("wis", "score", "qi_s", "kiT", "h_last", "ones"))
    z_dram, y_dram = v["z_dram"], v["y_dram"]
    lam, bnat, pw = (v[n] for n in ("lam", "bnat", "pw"))
    own = ExitStack()
    with own:
        sb = lambda name, shape, dt=F32: sb_in(own, name, shape, dt)
        wb = sb("wb", [P, 2, KT, CHUNK])
        w16 = sb("w16", [P, 2, 2, KT, CHUNK], F16)
        absolute = sb("absolute", [P, 4, CHUNK], BF16)
        size = sb("size", [P, 2, 4])
        unit = sb("unit", [P, 4, 3])
        uT = sb("uT", [P, 4, TOK])
        room = sb("room", [P, 8 * TOK])
        qiT = room[:].rearrange("p (c n) -> p c n", c=8)
        at = 0

        def part(n):
            nonlocal at
            at += n
            return room[:, at - n:at]

        tab = part(2 * SEQ).rearrange("p (a n) -> p a n", a=2)
        g_ = part(2 * SEQ).rearrange("p (a n) -> p a n", a=2)
        h_ = part(2 * TOK).rearrange("p (a n) -> p a n", a=2)
        pt = part(SEQ)
        dt_ = part(512)
        xy = part(4 * P).rearrange("p (a n) -> p a n", a=4)
        xs = part(2 * NS).rearrange("p (a n) -> p a n", a=2)
        tt = score[:, 0:2 * TILES * LO].rearrange("p (s i a b) -> p s i a b", s=2, i=TILES, a=2)
        bt = score[:, 2 * TILES * LO:2 * TILES * (LO + GROUP)].rearrange("p (s i c) -> p s i c", s=2, i=TILES)
        w1 = score[:, 2048:2048 + 16 * TILES].rearrange("p (s i) -> p s i", i=TILES)
        ang = score[:, 2304:2304 + 60 * TILES].rearrange("p (s i k) -> p s i k", s=6, k=10)
        kw_f = sb("kw_f", [P, TOK])
        yacc = kw_f
        zst = sb("zst", [P, 2, TOK])
        rel = zst[:].rearrange("p a n -> p (a n)")[:, 0:2 * SEQ].rearrange("p (a n) -> p a n", a=2)
        stat = sb("stat_b", [P, 4, P])
        ki_out = uT[:, 0, 0:(QT + 1) * IDX_DIM].rearrange("p (t d) -> p t d", t=QT + 1)
        m8 = sb("m8", [P, 8])
        st_out = stat

        w_loaded = [sem(f"w_loaded{b}") for b in range(2)]
        w_summed, w_sized, unit_ready, w_high, w_split, act_link = (
            sem(n) for n in ("w_summed", "w_sized", "unit_ready", "w_high", "w_split", "act_link"))
        z_ready = sem("z_ready")
        z_evac = sem("z_evac")
        z_stored = [sem(f"z_stored{b}") for b in range(2)]
        turned = sem("turned")
        dve_read = sem("dve_read")
        act_read = sem("act_read")
        index_mm = sem("index_mm")
        acc_done = sem("acc_done")
        pool_link = sem("pool_link_b")
        ang_ready = sem("ang_ready")
        sin_ready = sem("sin_ready")
        xy_ready = sem("xy_ready")
        x_mm = sem("x_mm")
        g_ready = sem("g_ready")
        h_rotated = sem("h_rotated")
        y_mm = sem("y_mm")
        y_done = sem("y_done")
        gelu_done = sem("gelu_done")
        y_stored = sem("y_stored")
        dve_link = sem("dve_link_b")
        loop_link = sem("loop_link")
        last_turned = sem("last_turned")
        last_copied = sem("last_copied")
        out_stored = sem("out_stored_b")

        w_rows = io["w_in"][0].rearrange("(k p) n -> p k n", p=P)
        slabs = [OFF_QI + SLAB * s for s in range(4)] + [OFF_U + SLAB * s for s in range(2)] + LOOP_SLABS
        chunks = [(OFF_KI, KIWI)] + [(c + d, CHUNK) for c in slabs for d in (0, CHUNK)]
        chunks += chunks[-1:]
        KW_READS = 4
        HEADS = len(IDX_TILES) * N_IDX
        FIRST_U, FIRST_LOOP = 9, 13
        LAST = len(chunks) - 1

        block = own.enter_context(nc.Block(name="project"))

        @block.sync
        def _(sp):
            for c, (col, w) in enumerate(chunks):
                if c >= 2:
                    sp.wait_ge(w_split, c - 1)
                sp.dma_start(wb[:, c % 2, :, 0:w], w_rows[:, :, col:col + w]).then_inc(w_loaded[c % 2], 16)
            for n, (name, who) in enumerate((("out_ssm_re_p", 0), ("out_ssm_im_p", 0), ("out_ssm_re_s", 1), ("out_ssm_im_s", 1))):
                sp.wait_ge(last_copied, n + 1)
                if who == 0:
                    dst = io[name][0, 0].rearrange("(i a) n -> i (a n)", a=2)
                    sp.dma_start(dst, st_out[0:TILES, n, :]).then_inc(out_stored, 16)
                else:
                    dst = io[name][0].rearrange("b (i a) n -> (b i) (a n)", a=2)
                    sp.dma_start(dst, st_out[:, n, :]).then_inc(out_stored, 16)
            sp.wait_ge(out_stored, 4 * 16)

        def group(pe, b, m, n, c):
            t0, w = PIECES[n]
            if n == 0:
                pe.wait_ge(w_split, c + 1)
            if not isinstance(c, int) or c >= 1:
                pe.wait_ge(z_evac, 3 * c + (n + 1 - 3))
            for k in range(KT):
                for i, (pw_, ph) in enumerate(((0, 0), (0, 1), (1, 0))):
                    last = nc.tensor.matmul(ps[0:m, n, 0:w], w16[:, b, pw_, k, 0:m], h16[:, ph, k, t0:t0 + w],
                                            start=(k == 0 and i == 0), stop=(k == KT - 1 and i == 2))
            last.then_inc(z_ready, 1)
            return last

        def sum_sizes(pe, c, b, out):
            pe.wait_ge(w_summed, 4 * c + 4)
            return nc.tensor.matmul(out, ones[:], size[:, b, :], start=True, stop=True)

        @block.tensor
        def _(pe):
            def chunk_before_loop(c, b, m):
                group(pe, b, m, 0, c)
                sum_sizes(pe, c + 1, 1 - b, ps[:, 7, 0:4]).then_inc(w_sized, 1)
                for n in (1, 2):
                    group(pe, b, m, n, c)

            sum_sizes(pe, 0, 0, ps[:, 7, 0:4]).then_inc(w_sized, 1)
            chunk_before_loop(0, 0, KIWI)
            with pe.Fori(0, 2) as it:
                for u in range(4):
                    chunk_before_loop(it * 4 + (1 + u), 1 - u % 2, P)
            pe.wait_ge(z_evac, 3)
            for t in range(QT + 1):
                n = P if t < QT else NS
                last = nc.tensor.transpose(ps[0:n, 3 + t // 5, (t % 5) * KIWI:(t % 5 + 1) * KIWI],
                                           kw_f[0:KIWI, t * P:t * P + n], ident[0:KIWI, 0:KIWI])
            last.then_inc(turned, 1)
            pe.wait_ge(dve_read, KW_READS)
            pe.wait_ge(z_evac, 27)
            for ti, t in enumerate(IDX_TILES):
                for h in range(N_IDX):
                    m = ti * N_IDX + h
                    bank = 3 + 2 * (m % 2)
                    if m >= 2:
                        pe.wait_ge(act_read, m - 1)
                    for x0 in range(0, (t + 1) * P, 512):
                        w = min(512, (t + 1) * P - x0)
                        last = nc.tensor.matmul(ps[:, bank + x0 // 512, 0:w], qiT[:, h // 2, t * P:(t + 1) * P],
                                                kiT[:, h % 2, x0:x0 + w], start=True, stop=True)
                    last.then_inc(index_mm, 1)
            for c in range(FIRST_U, FIRST_LOOP):
                chunk_before_loop(c, c % 2, P)
            pe.wait_ge(z_evac, 3 * FIRST_LOOP)
            with pe.Fori(0, LOOPS) as it:
                for x in range(4):
                    tile = it * 4 + x
                    chunk = it * 8 + (FIRST_LOOP + 2 * x)
                    pe.wait_ge(w_split, chunk + 1)
                    pe.wait_ge(xy_ready, tile + 1)
                    pe.wait_ge(act_read, tile + HEADS)
                    for a in range(4):
                        last = nc.tensor.transpose(ps[:, 3, a * P:(a + 1) * P], xy[:, a, :], ident[:])
                    last.then_inc(turned, 1)
                    group(pe, 1, P, 0, chunk)
                    pe.wait_ge(act_read, tile + HEADS + 1)
                    pe.wait_ge(dve_read, tile * 6 + KW_READS)
                    for n, (t0, w) in enumerate(STEPS):
                        for a in range(2):
                            out = ps[:, 4 + 2 * n + a, 0:w] if n < 2 else ps[:, 3, a * NS:(a + 1) * NS]
                            last = nc.tensor.matmul(out, stat[:, a, :], uT[:, bass.ds(it, 1), t0:t0 + w], start=True, stop=True)
                        if n == 2:
                            last = sum_sizes(pe, chunk + 1, 0, ps[:, 3, 2 * NS:2 * NS + 4])
                        last.then_inc(x_mm, 1)
                    group(pe, 1, P, 1, chunk)
                    group(pe, 1, P, 2, chunk)
                    group(pe, 0, P, 0, chunk + 1)
                    pe.wait_ge(dve_read, tile * 6 + (KW_READS + 1))
                    sum_sizes(pe, chunk + 2, 1, ps[:, 3, 0:4]).then_inc(w_sized, 1)
                    group(pe, 0, P, 1, chunk + 1)
                    group(pe, 0, P, 2, chunk + 1)
                    pe.wait_ge(h_rotated, tile + 1)
                    for n, (t0, w) in enumerate(STEPS):
                        for a in range(2):
                            last = nc.tensor.matmul(ps[:, (6, 7, 4)[n], 0:w], stat[:, 2 + a, :], h_[:, a, t0:t0 + w],
                                                    start=(a == 0), stop=(a == 1))
                        last.then_inc(y_mm, 1)
            pe.wait_ge(y_done, LOOPS)
            pe.wait_ge(dve_read, 6 * TILES + KW_READS)
            for n in range(2):
                nc.tensor.transpose(ps[0:TILES, 3, n * P:(n + 1) * P], h_last[:, n, 0, :], ident[:])
            for n in range(2):
                last = nc.tensor.transpose(ps[:, 5, n * P:(n + 1) * P],
                                           h_last[:, n, 1:1 + DEC_BATCH, :].rearrange("p b i -> p (b i)"), ident[:])
            last.then_inc(last_turned, 1)

        @block.scalar
        def _(act):
            def sum_absolutes(c, b, w=CHUNK):
                act.wait_ge(w_loaded[b], loads(c, b))
                for k in range(4):
                    if not isinstance(c, int) or c or k:
                        act.wait_ge(w_summed, 4 * c + k)
                    nc.scalar.activation(absolute[:, :, 0:w], wb[:, b, 4 * k:4 * k + 4, 0:w], ACT.Abs,
                                         accum_out=size[:, b, k:k + 1]).then_inc(w_summed, 1)

            def split_high(c, b, slot, w=CHUNK):
                act.wait_ge(unit_ready, c + 1)
                src, high = wb[:, b, :, 0:w], w16[:, b, 0, :, 0:w]
                nc.scalar.activation(src, src, ACT.Copy, scale=unit[:, slot, 1:2]).then_inc(act_link, 1)
                if not isinstance(c, int) or c >= 2:
                    act.wait_ge(z_ready, 3 * (c - 1))
                act.wait_ge(act_link, c + 1)
                nc.scalar.activation(high, src, ACT.Copy).then_inc(w_high, 1)

            def loads(c, b):
                return 16 * (c // 2 + 1) if isinstance(c, int) else c * 8 + (16 - 8 * b)

            def evac(c, n, outs, func=ACT.Copy, slot=None):
                slot = c % 4 if slot is None else slot
                t0, w = PIECES[n]
                act.wait_ge(z_ready, 3 * c + (n + 1))
                for rows, out in outs:
                    whole = out.shape[-1] == TOK
                    last = nc.scalar.activation(out[:, t0:t0 + w] if whole else out, ps[rows, n, 0 if whole else w - NS:w], func,
                                                scale=unit[rows, slot, 2:3])
                last.then_inc(z_evac, 1)

            sum_absolutes(0, 0, KIWI)
            split_high(0, 0, 0, KIWI)
            sum_absolutes(1, 1)
            for n in range(3):
                if n == 1:
                    split_high(1, 1, 1)
                evac(0, n, [(slice(0, KIWI), kw_f[0:KIWI, :]), (slice(0, IDX_DIM), kiT[0:IDX_DIM, 0, :]),
                            (slice(0, IDX_DIM), kiT[IDX_DIM:P, 1, :])])
            act.wait_ge(ang_ready, 1)
            nc.scalar.activation(ang[:, 2, :, :], ang[:, 0, :, :], ACT.Sin).then_inc(sin_ready, 1)
            nc.scalar.activation(ang[:, 3, :, :], ang[:, 1, :, :], ACT.Sin).then_inc(sin_ready, 1)
            for c in range(8):
                sum_absolutes(c + 2, c % 2)
                for n in range(3):
                    if n == 1:
                        split_high(c + 2, c % 2, (c + 2) % 4)
                    evac(1 + c, n, [(slice(0, P), qiT[:, c, :])] + ([(slice(0, P), qi_s[:, c, :])] if n == 2 else []))
            act.wait_ge(dve_read, KW_READS)
            act.dma_start(io["out_kidx_p"][0, 0].rearrange("(t p) d -> p t d", p=P), ki_out[:, 0:QT, :]).then_inc(z_stored[0], 16)
            act.dma_start(io["out_kidx_s"][0].rearrange("b s d -> (b s) d"), ki_out[0:NS, QT, :]).then_inc(z_stored[1], 16)
            for ti, t in enumerate(IDX_TILES):
                for h in range(N_IDX):
                    m = ti * N_IDX + h
                    act.wait_ge(index_mm, m + 1)
                    if m >= 2:
                        act.wait_ge(acc_done, m - 1)
                    src = ps[:, 3 + 2 * (m % 2):5 + 2 * (m % 2), :].rearrange("p a n -> p (a n)")[:, 0:(t + 1) * P]
                    nc.scalar.activation(rel[:, m % 2, 0:(t + 1) * P], src, ACT.Relu, scale=IDX_DIM ** -0.5).then_inc(act_read, 1)
            for b in range(2):
                act.wait_ge(z_stored[b], 16)
            for c in range(4):
                after = FIRST_U + c + 1
                sum_absolutes(after, after % 2)
                for n in range(3):
                    if n == 1:
                        split_high(after, after % 2, after % 4)
                    evac(FIRST_U + c, n, [(slice(0, P), uT[:, c, :])])
            act.wait_ge(acc_done, HEADS)
            with act.Fori(0, LOOPS) as it:
                for x in range(4):
                    act.wait_ge(turned, it * 4 + (x + 2))
                    nc.scalar.activation(stat[:], ps[:, 3, :].rearrange("p (a n) -> p a n", a=4), ACT.Copy).then_inc(act_read, 1)
                    for sub in range(2):
                        act.wait_ge(z_stored[sub], it * 64 + 16 * (x + 1))
                        c = it * 8 + (FIRST_LOOP + 2 * x + sub)
                        k = FIRST_LOOP + 2 * x + sub
                        sum_absolutes(c + 1, (k + 1) % 2)
                        for n in range(3):
                            if n == 1:
                                split_high(c + 1, (k + 1) % 2, (k + 1) % 4)
                            evac(c, n, [(slice(0, P), zst[:, sub, :])], ACT.Silu if x % 2 else ACT.Copy, k % 4)
                        act.wait_ge(z_evac, 3 * c + 3)
                        act.dma_start(z_dram[bass.ds(it * 8 + (2 * x + sub), 1)].rearrange("a p n -> (a p) n"), zst[:, sub, :]).then_inc(z_stored[sub], 16)
                act.wait_ge(y_done, it + 1)
                nc.scalar.activation(yacc[:], yacc[:], ACT.Gelu_apprx_tanh).then_inc(gelu_done, 1)
                act.wait_ge(gelu_done, it + 1)
                act.dma_start(y_dram[bass.ds(it, 1)].rearrange("a p n -> (a p) n"), yacc[:]).then_inc(y_stored, 16)
                act.wait_ge(y_stored, it * 16 + 16)
            for b in range(2):
                act.wait_ge(z_stored[b], 16 * (1 + len(LOOP_SLABS)))

        @block.gpsimd
        def _(pool):
            def split_low(c, b, w=CHUNK):
                pool.wait_ge(w_high, c + 1)
                nc.gpsimd.tensor_tensor(w16[:, b, 1, :, 0:w], wb[:, b, :, 0:w], w16[:, b, 0, :, 0:w], ALU.subtract).then_inc(w_split, 1)

            split_low(0, 0, KIWI)
            for c in range(1, FIRST_LOOP + 1):
                split_low(c, c % 2)
            pool.wait_ge(act_read, HEADS)
            TT = nc.gpsimd.tensor_tensor
            PER_TILE = 5
            with pool.Fori(0, LOOPS) as it:
                for x in range(4):
                    tile = it * 4 + x
                    base = it * (4 * PER_TILE) + x * PER_TILE
                    pool.wait_ge(turned, tile + 1)
                    mb = mask_b[:, x, :].unsqueeze(2).to_broadcast([P, 8, GROUP])
                    for a in range(2):
                        src = bbar[:, a, bass.ds(tile, 1), :].to_broadcast([P, 8, GROUP])
                        TT(xy[:, a, :].rearrange("p (g c) -> p g c", g=8), src, mb, ALU.mult)
                    mc = mask_c[:, 2 * x:2 * x + 2].unsqueeze(2).to_broadcast([P, 2, STATE])
                    for a in range(2):
                        src = cnat[:, a, bass.ds(it, 1), :].to_broadcast([P, 2, STATE])
                        last = TT(xy[:, 2 + a, :].rearrange("p (a n) -> p a n", a=2), src, mc, ALU.mult)
                    last.then_inc(xy_ready, 1)
                    split_low(it * 8 + (FIRST_LOOP + 2 * x + 1), 0)
                    pool.wait_ge(g_ready, tile + 1)
                    c_, s_ = tab[:, 0, :], tab[:, 1, :]
                    hr, hi = h_[:, 0, 0:SEQ], h_[:, 1, 0:SEQ]
                    TT(hr, g_[:, 0, :], c_, ALU.mult).then_inc(pool_link, 1)
                    TT(pt, g_[:, 1, :], s_, ALU.mult).then_inc(pool_link, 1)
                    pool.wait_ge(pool_link, base + 2)
                    TT(hr, hr, pt, ALU.subtract).then_inc(pool_link, 1)
                    TT(hi, g_[:, 0, :], s_, ALU.mult).then_inc(pool_link, 1)
                    pool.wait_ge(pool_link, base + 4)
                    TT(pt, g_[:, 1, :], c_, ALU.mult).then_inc(pool_link, 1)
                    pool.wait_ge(pool_link, base + 5)
                    TT(hi, hi, pt, ALU.add).then_inc(h_rotated, 1)
                    split_low(it * 8 + (FIRST_LOOP + 2 * x + 2), 1)

        @block.vector
        def _(dve):
            link = Link(dve, dve_link)
            TSC, TT, STT = nc.vector.tensor_scalar, nc.vector.tensor_tensor, nc.vector.scalar_tensor_tensor
            copy = nc.vector.tensor_copy

            def set_unit(link, src, slot):
                u = [unit[:, slot, i:i + 1] for i in range(3)]
                link(nc.vector.tensor_reduce(u[0], src, AX_X, ALU.add))
                link(TSC(u[0], u[0], W_SHIFT, TINY, ALU.mult, ALU.max))
                nc.vector.reciprocal(u[1], u[0])
                TT(u[2], u[0], h_unit[:], ALU.mult).then_inc(unit_ready, 1)

            def early_unit(c):
                dve.wait_ge(w_sized, c + 1)
                set_unit(link, ps[:, 7, 0:4], c % 4)

            early_unit(0)
            lr, li = lam[:, 0, :], lam[:, 1, :]
            dt, lrd, th, k_, r_ = (w1[:, i, :] for i in range(5))

            def exponential(out, x, y):
                link(TSC(y, x, 1 / 16, None, ALU.mult))
                link(TSC(out, y, 1 / math.factorial(9), None, ALU.mult))
                for n in range(8, 0, -1):
                    link(STT(out=out, in0=out, scalar=1 / math.factorial(n), in1=y, op0=ALU.add, op1=ALU.mult))
                link(TSC(out, out, 1.0, None, ALU.add))
                for _ in range(4):
                    link(TT(out, out, out, ALU.mult))

            exponential(dt, lam[:, 2, :], k_)
            link(TT(lrd, lr, dt, ALU.mult))
            exponential(par[:, 0, :], lrd, k_)
            early_unit(1)
            link(TT(th, li, dt, ALU.mult))

            def reduce_angle(out, x, k):
                link(TSC(k, x, 1.0 / TWO_PI, MAGIC, ALU.mult, ALU.add))
                link(TSC(k, k, MAGIC, None, ALU.subtract))
                link(STT(out=out, in0=k, scalar=-PI_A, in1=x, op0=ALU.mult, op1=ALU.add))
                link(STT(out=out, in0=k, scalar=-PI_B, in1=out, op0=ALU.mult, op1=ALU.add))
                link(STT(out=out, in0=k, scalar=-PI_C, in1=out, op0=ALU.mult, op1=ALU.add))
                link(TSC(out, out, PI_IN, -PI_IN, ALU.min, ALU.max))

            reduce_angle(r_, th, k_)
            link(TT(ang[:, 4, :, :], r_.unsqueeze(2).to_broadcast([P, TILES, 10]),
                    pw[:].unsqueeze(1).to_broadcast([P, TILES, 10]), ALU.mult))
            reduce_angle(ang[:, 0, :, :], ang[:, 4, :, :], ang[:, 5, :, :])
            link(STT(out=ang[:, 1, :, :], in0=ang[:, 0, :, :], scalar=-1.0, in1=ang[:, 0, :, :],
                     op0=ALU.mult, op1=ALU.max))
            TSC(ang[:, 1, :, :], ang[:, 1, :, :], -1.0, np.pi / 2, ALU.mult, ALU.add).then_inc(ang_ready, 1)
            early_unit(2)
            dve.wait_ge(sin_ready, 2)
            sin_p, cos_p = ang[:, 2, :, :], ang[:, 3, :, :]
            mag, ar, ai, nai = (par[:, i, :] for i in range(4))
            link(TT(ar, mag, cos_p[:, :, 0], ALU.mult))
            link(TT(ai, mag, sin_p[:, :, 0], ALU.mult))
            link(TSC(nai, ai, -1.0, None, ALU.mult))
            den, am1, t1, t2, cr, ci = (w1[:, i, :] for i in range(5, 11))
            link(TT(t1, lr, lr, ALU.mult))
            link(TT(t2, li, li, ALU.mult))
            link(TT(den, t1, t2, ALU.add))
            link(nc.vector.reciprocal(den, den))
            link(TSC(am1, ar, -1.0, None, ALU.add))
            link(TT(t1, lr, am1, ALU.mult))
            link(TT(t2, li, ai, ALU.mult))
            link(TT(cr, t1, t2, ALU.add))
            link(TT(cr, cr, den, ALU.mult))
            link(TT(t1, lr, ai, ALU.mult))
            link(TT(t2, li, am1, ALU.mult))
            link(TT(ci, t1, t2, ALU.subtract))
            link(TT(ci, ci, den, ALU.mult))
            crb = cr.unsqueeze(2).to_broadcast([P, TILES, GROUP])
            cib = ci.unsqueeze(2).to_broadcast([P, TILES, GROUP])
            link(TT(bbar[:, 0, :, :], bnat[:, 0, :, :], crb, ALU.mult))
            link(TT(bt[:, 0, :, :], bnat[:, 1, :, :], cib, ALU.mult))
            link(TT(bbar[:, 0, :, :], bbar[:, 0, :, :], bt[:, 0, :, :], ALU.subtract))
            link(TT(bbar[:, 1, :, :], bnat[:, 1, :, :], crb, ALU.mult))
            link(TT(bt[:, 1, :, :], bnat[:, 0, :, :], cib, ALU.mult))
            link(TT(bbar[:, 1, :, :], bbar[:, 1, :, :], bt[:, 1, :, :], ALU.add))
            link(TSC(cnat[:, 1, :, :], cnat[:, 1, :, :], -1.0, None, ALU.mult))
            link(nc.vector.memset(tabs[:, 0, :, :, 0:1], 1.0))
            link(nc.vector.memset(tabs[:, 1, :, :, 0:1], 0.0))
            for lev in range(5):
                d = 1 << lev
                shape = [P, TILES, 2, d]
                pc = cos_p.rearrange("p i (a k) -> p i a k", a=2)[:, :, :, lev:lev + 1].to_broadcast(shape)
                psn = sin_p.rearrange("p i (a k) -> p i a k", a=2)[:, :, :, lev:lev + 1].to_broadcast(shape)
                c_, s_ = tabs[:, 0, :, :, 0:d], tabs[:, 1, :, :, 0:d]
                co, so = tabs[:, 0, :, :, d:2 * d], tabs[:, 1, :, :, d:2 * d]
                u1, u2 = tt[:, 0, :, :, 0:d], tt[:, 1, :, :, 0:d]
                link(TT(co, c_, pc, ALU.mult))
                link(TT(u1, s_, psn, ALU.mult))
                link(TT(co, co, u1, ALU.subtract))
                link(TT(so, s_, pc, ALU.mult))
                link(TT(u2, c_, psn, ALU.mult))
                link(TT(so, so, u2, ALU.add))
            for c in range(3, FIRST_U + 1):
                early_unit(c)
            dve.wait_ge(turned, 1)
            first = ps[:, 3, 0:5 * KIWI].rearrange("p (t c) -> p t c", t=5)
            copy(ki_out[:, 0:5, :], first[:, :, 0:IDX_DIM]).then_inc(dve_read, 1)
            TSC(wis[:, 0:5, :], first[:, :, IDX_DIM:KIWI], N_IDX ** -0.5, None, ALU.mult)
            second = ps[:, 4, 0:3 * KIWI].rearrange("p (t c) -> p t c", t=3)
            copy(ki_out[:, 5:8, :], second[:, :, 0:IDX_DIM]).then_inc(dve_read, 1)
            TSC(wis[:, 5:8, :], second[:, :, IDX_DIM:KIWI], N_IDX ** -0.5, None, ALU.mult)
            third = ps[0:NS, 4, 3 * KIWI:4 * KIWI]
            copy(ki_out[0:NS, 8, :], third[:, 0:IDX_DIM]).then_inc(dve_read, 1)
            TSC(wis[0:NS, 8, :], third[:, IDX_DIM:KIWI], N_IDX ** -0.5, None, ALU.mult).then_inc(dve_read, 1)
            dve.wait_ge(dve_read, KW_READS)
            for ti, t in enumerate(IDX_TILES):
                sc = score[:, IDX_OFF[t]:IDX_OFF[t] + (t + 1) * P]
                for h in range(N_IDX):
                    m = ti * N_IDX + h
                    dve.wait_ge(act_read, m + 1)
                    wi = wis[:, t, h:h + 1]
                    r = rel[:, m % 2, 0:(t + 1) * P]
                    if h == 0:
                        TSC(sc, r, wi, None, ALU.mult).then_inc(acc_done, 1)
                    else:
                        dve.wait_ge(acc_done, m)
                        STT(out=sc, in0=r, scalar=wi, in1=sc, op0=ALU.mult, op1=ALU.add).then_inc(acc_done, 1)
                dve.wait_ge(acc_done, (ti + 1) * N_IDX)
                diag = sc[:, t * P:(t + 1) * P]
                link(TT(diag, diag, cmin[:], ALU.min))
            for c in range(FIRST_U + 1, FIRST_LOOP + 1):
                early_unit(c)

            with dve.Fori(0, LOOPS) as it:
                dve.sem_clear(loop_link)
                link = Link(dve, loop_link)

                def keep_eight(t):
                    sc = score[:, IDX_OFF[t]:IDX_OFF[t] + (t + 1) * P]
                    link(nc.vector.max(out=m8[:], in_=sc))
                    link(nc.vector.match_replace(out=sc, in_to_replace=m8[:], in_values=sc, imm_value=REPLACED))

                plan = {0: [7] * 8, 1: [6] * 8, 2: [5, 2] * 8, 3: [4, 3] * 8}
                for x in range(4):
                    tile = it * 4 + x
                    rounds = plan[x]
                    view = lambda a: tab[:, a, :].rearrange("p (a b) -> p a b", a=LO)
                    shape = [P, LO, LO]
                    low = lambda a: tabs[:, a, bass.ds(tile, 1), 0, :].to_broadcast(shape)
                    high = lambda a: tabs[:, a, bass.ds(tile, 1), 1, :].rearrange("p i a -> p a i").to_broadcast(shape)
                    g2 = g_[:, 0, :].rearrange("p (a b) -> p a b", a=LO)
                    g3 = g_[:, 1, :].rearrange("p (a b) -> p a b", a=LO)
                    TT(view(0), high(0), low(0), ALU.mult)
                    TT(g2, high(1), low(1), ALU.mult)
                    TT(view(1), high(0), low(1), ALU.mult)
                    link(TT(g3, high(1), low(0), ALU.mult))
                    TT(view(0), view(0), g2, ALU.subtract)
                    link(TT(view(1), view(1), g3, ALU.add))
                    early, later = len(rounds) // 4, 5 * len(rounds) // 8
                    for t in rounds[:early]:
                        keep_eight(t)
                    dve.wait_ge(x_mm, it * 12 + (3 * x + 3))
                    set_unit(link, ps[:, 3, 2 * NS:2 * NS + 4], (FIRST_LOOP + 2 * x + 1) % 4)
                    copy(xs, ps[:, 3, 0:2 * NS].rearrange("p (a n) -> p a n", a=2)).then_inc(dve_read, 1)
                    for n in range(2):
                        sl = slice(512 * n, 512 * n + 512)
                        xr, xi = ps[:, 4 + 2 * n, :], ps[:, 5 + 2 * n, :]
                        gr, gi = g_[:, 0, sl], g_[:, 1, sl]
                        c_, s_ = tab[:, 0, sl], tab[:, 1, sl]
                        TT(gr, xr, c_, ALU.mult)
                        link(TT(dt_, xi, s_, ALU.mult))
                        TT(gr, gr, dt_, ALU.add)
                        link(TT(gi, xi, c_, ALU.mult))
                        TT(dt_, xr, s_, ALU.mult).then_inc(dve_read, 1)
                        dve.wait_ge(dve_read, it * 24 + (KW_READS + 6 * x + n + 2))
                        link(TT(gi, gi, dt_, ALU.subtract))
                    ar, ai, nai = (par[:, k, bass.ds(tile, 1)] for k in (1, 2, 3))
                    for q in range(DEC_SEQ):
                        if q == 0:
                            pr, pi = (h0[:, a, :, bass.ds(tile, 1)].rearrange("p b i -> p (b i)") for a in range(2))
                        else:
                            pr, pi = (h_[:, a, SEQ + q - 1:TOK:DEC_SEQ] for a in range(2))
                        xr, xi = (xs[:, a, q:NS:DEC_SEQ] for a in range(2))
                        nr, ni = (h_[:, a, SEQ + q:TOK:DEC_SEQ] for a in range(2))
                        STT(out=nr, in0=pr, scalar=ar, in1=xr, op0=ALU.mult, op1=ALU.add)
                        link(STT(out=ni, in0=pi, scalar=ar, in1=xi, op0=ALU.mult, op1=ALU.add))
                        STT(out=nr, in0=pi, scalar=nai, in1=nr, op0=ALU.mult, op1=ALU.add)
                        link(STT(out=ni, in0=pr, scalar=ai, in1=ni, op0=ALU.mult, op1=ALU.add))
                    mag = par[:, 0, bass.ds(tile, 1)].to_broadcast([P, SEQ])
                    for a in range(2):
                        last = nc.vector.tensor_tensor_scan(out=g_[:, a, :], data0=mag, data1=g_[:, a, :], initial=0.0,
                                                            op0=ALU.mult, op1=ALU.add)
                        last.then_inc(g_ready, 1) if a == 1 else link(last)
                    for t in rounds[early:later]:
                        keep_eight(t)
                    dve.wait_ge(w_sized, it * 4 + (FIRST_LOOP + 2 + x))
                    set_unit(link, ps[:, 3, 0:4], (FIRST_LOOP + 2 * x + 2) % 4)
                    for t in rounds[later:]:
                        keep_eight(t)
                    for n, (t0, w) in enumerate(STEPS):
                        dve.wait_ge(y_mm, it * 12 + (3 * x + n + 1))
                        y, src = yacc[:, t0:t0 + w], ps[:, (6, 7, 4)[n], 0:w]
                        if x == 0:
                            last = STT(out=y, in0=uT[:, bass.ds(it, 1), t0:t0 + w].rearrange("p a n -> p (a n)"),
                                       scalar=dcol[:, bass.ds(it, 1)], in1=src, op0=ALU.mult, op1=ALU.add)
                        else:
                            last = TT(y, y, src, ALU.add)
                        last.then_inc(dve_read, 1)
                    dve.wait_ge(dve_read, it * 24 + (KW_READS + 6 * x + 6))
                    for a in range(2):
                        last = copy(h_last[:, a, :, bass.ds(tile, 1)].rearrange("p b i -> p (b i)"), h_[:, a, SEQ - 1:TOK:DEC_SEQ])
                    if x == 3:
                        last.then_inc(y_done, 1)
            dve.wait_ge(last_turned, 1)
            for n in range(2):
                copy(st_out[0:TILES, n, :], ps[0:TILES, 3, n * P:(n + 1) * P]).then_inc(last_copied, 1)
            for n in range(2):
                copy(st_out[:, 2 + n, :], ps[:, 5, n * P:(n + 1) * P]).then_inc(last_copied, 1)


def block_c(nc, io, v, sem, sb_in):
    ident, ps, z_dram, y_dram, mixT, kT, kv_tok = (v[n] for n in ("ident", "ps", "z_dram", "y_dram", "mixT", "kT", "kv_tok"))
    own = ExitStack()
    with own:
        sb = lambda name, shape: sb_in(own, name, shape)
        w_glu = sb("w_glu_sb", [P, 4, 2 * D_SSM])
        yT = sb("yT", [P, 4, TOK])
        vT = sb("vT", [P, 2, TOK])
        qmT = sb("qmT", [P, 4, TOK])
        sg = sb("sg", [P, 2, 512])
        ag = sb("ag", [P, 512])
        mem_kv = sb("mem_kv", [P, 2, 2, D_MEM])
        mkT = sb("mkT", [P, 4, N_MEM])
        pm = w_glu[:, 0:2, :].rearrange("p b (h n) -> p b h n", h=4)
        pmT = w_glu[:, 2:4, :].rearrange("p b (k h n) -> p b k h n", k=2, h=4)
        nmx = sb("nmx_c", [P, QT, 4])
        nb = sb("nb_c", [P, QT, 4])
        rs = sb("rs_c", [P, QT, 4])
        rinv = sb("rinv_c", [P, QT, 4])

        glu_loaded, kv_loaded, mem_loaded, gate_s_loaded, gate_m_loaded, gate_a_loaded = (
            sem(n) for n in ("glu_loaded", "kv_loaded", "mem_loaded", "gate_s_loaded", "gate_m_loaded", "gate_a_loaded"))
        glu_mm, glu_sig, glu_used = sem("glu_mm"), sem("glu_sig"), sem("glu_used")
        kv_turned, kv_copied, kv_stored = sem("kv_turned"), sem("kv_copied"), sem("kv_stored_c")
        mk_turned, mk_copied = sem("mk_turned"), sem("mk_copied")
        s_mm, nb_ready, exp_done, p_ready = sem("s_mm_c"), sem("nb_ready_c"), sem("exp_done_c"), sem("p_ready_c")
        p_turned, p_copied = sem("p_turned_c"), [sem(f"p_copied_c{k}") for k in range(2)]
        o_mm, o_used, dve_link = sem("o_mm_c"), sem("o_used_c"), sem("dve_link_c")
        SCALE = HEAD_DIM ** -0.5
        GLU = [(c, n) for c in range(4) for n in range(3)]

        def pair(col):
            return z_dram[stored(col):stored(col) + 2].rearrange("c p n -> p c n")

        block = own.enter_context(nc.Block(name="mix_a"))

        @block.sync
        def _(sp):
            sp.dma_start(w_glu[:], io["w_glu"][0].rearrange("(k p) n -> p k n", p=P)).then_inc(glu_loaded, 16)
            sp.dma_start(yT[:], y_dram.rearrange("c p n -> p c n")).then_inc(glu_loaded, 16)
            for s in range(2):
                sp.dma_start(mixT[:, 8 + 2 * s:10 + 2 * s, :], pair(OFF_GS + SLAB * s)).then_inc(gate_s_loaded, 16)
            sp.dma_start(kT[:], pair(OFF_K)).then_inc(kv_loaded, 16)
            sp.dma_start(vT[:], pair(OFF_V)).then_inc(kv_loaded, 16)
            for n, name in enumerate(("out_mk", "out_mv")):
                src = io[name][0, 0].rearrange("(a p) h d -> p a (h d)", p=P)
                sp.dma_start(mem_kv[:, n, :, :], src).then_inc(mem_loaded, 16)
            for s in range(2):
                sp.dma_start(qmT[:, 2 * s:2 * s + 2, :], pair(OFF_QM + SLAB * s)).then_inc(mem_loaded, 16)
            for s in range(2):
                sp.dma_start(mixT[:, 12 + 2 * s:14 + 2 * s, :], pair(OFF_GM + SLAB * s)).then_inc(gate_m_loaded, 16)
            for s in range(4):
                sp.dma_start(mixT[:, 2 * s:2 * s + 2, :], pair(OFF_GA + SLAB * s)).then_inc(gate_a_loaded, 16)
            sp.wait_ge(gate_a_loaded, 64)
            sp.wait_ge(kv_copied, QT + 1)
            for n, name in enumerate(("out_k", "out_v")):
                part = slice(n * 256, n * 256 + 256)
                dst = io[name + "_p"][0, 0].rearrange("(t p) h d -> p t (h d)", p=P)
                sp.dma_start(dst, kv_tok[:, 0:QT, part]).then_inc(kv_stored, 16)
                dst = io[name + "_s"][0].rearrange("b s h d -> (b s) (h d)")
                sp.dma_start(dst, kv_tok[0:NS, QT, part]).then_inc(kv_stored, 16)
            sp.wait_ge(kv_stored, 64)

        @block.tensor
        def _(pe):
            pe.wait_ge(glu_loaded, 32)
            for i, (c, n) in enumerate(GLU):
                t0, w = PIECES[n]
                if i >= 2:
                    pe.wait_ge(glu_used, i - 1)
                for a in range(2):
                    for k in range(4):
                        last = nc.tensor.matmul(ps[:, 2 * (i % 2) + a, 0:w], w_glu[:, k, a * D_SSM + c * P:a * D_SSM + (c + 1) * P],
                                                yT[:, k, t0:t0 + w], start=(k == 0), stop=(k == 3))
                last.then_inc(glu_mm, 1)
            pe.wait_ge(kv_loaded, 32)
            for t in range(QT + 1):
                n = P if t < QT else NS
                if t >= 2:
                    pe.wait_ge(kv_copied, t - 1)
                for a, src in enumerate((kT, kT, vT, vT)):
                    last = nc.tensor.transpose(ps[0:n, 4 + t % 2, a * P:(a + 1) * P], src[:, a % 2, t * P:t * P + n], ident[:])
                last.then_inc(kv_turned, 1)
            pe.wait_ge(mem_loaded, 64)
            for h in range(N_MEM_HEADS):
                for k in range(2):
                    last = nc.tensor.transpose(ps[:, 6 + h // 2, (2 * (h % 2) + k) * P:(2 * (h % 2) + k + 1) * P],
                                               mem_kv[:, 0, k, h * P:(h + 1) * P], ident[:])
            last.then_inc(mk_turned, 1)
            pe.wait_ge(mk_copied, 1)
            pe.wait_ge(glu_used, len(GLU))
            pe.wait_ge(kv_copied, QT + 1)
            for s in range(QT + 2):
                if s < QT:
                    if s >= 2:
                        pe.wait_ge(exp_done, 4 * (s - 1))
                    for h in range(N_MEM_HEADS):
                        last = nc.tensor.matmul(ps[:, 2 * (s % 2) + h // 2, (h % 2) * N_MEM:(h % 2 + 1) * N_MEM],
                                                qmT[:, h, s * P:(s + 1) * P], mkT[:, h, :], start=True, stop=True)
                    last.then_inc(s_mm, 1)
                if s >= 2:
                    u = s - 2
                    for k in range(2):
                        pe.wait_ge(p_copied[k], u + 1)
                    if u >= 2:
                        pe.wait_ge(o_used, u - 1)
                    for h in range(N_MEM_HEADS):
                        for k in range(2):
                            last = nc.tensor.matmul(ps[:, 6 + u % 2, h * P:(h + 1) * P], mem_kv[:, 1, k, h * P:(h + 1) * P],
                                                    pmT[:, u % 2, k, h, :], start=(k == 0), stop=(k == 1))
                    last.then_inc(o_mm, 1)
                if 1 <= s <= QT:
                    u = s - 1
                    pe.wait_ge(p_ready, u + 1)
                    for k in range(2):
                        if u >= 1:
                            pe.wait_ge(p_copied[k], u)
                        for h in range(N_MEM_HEADS):
                            last = nc.tensor.transpose(ps[:, 4 + k, h * P:(h + 1) * P], pm[:, u % 2, h, k * P:(k + 1) * P], ident[:])
                        last.then_inc(p_turned, 1)

        @block.scalar
        def _(act):
            for i, (c, n) in enumerate(GLU):
                w = PIECES[n][1]
                act.wait_ge(glu_mm, i + 1)
                if i >= 2:
                    act.wait_ge(glu_used, i - 1)
                nc.scalar.activation(sg[:, i % 2, 0:w], ps[:, 2 * (i % 2) + 1, 0:w], ACT.Sigmoid).then_inc(glu_sig, 1)
            for t in range(QT + 1):
                n = P if t < QT else NS
                act.wait_ge(kv_turned, t + 1)
                nc.scalar.activation(kv_tok[0:n, t, :], ps[0:n, 4 + t % 2, :], ACT.Copy).then_inc(kv_copied, 1)
            act.wait_ge(mk_turned, 1)
            nc.scalar.activation(mkT[:].rearrange("p h n -> p (h n)"), ps[:, 6:8, :].rearrange("p a n -> p (a n)"), ACT.Copy).then_inc(mk_copied, 1)
            for s in range(QT + 1):
                if s < QT:
                    act.wait_ge(nb_ready, s + 1)
                    if s >= 2:
                        act.wait_ge(p_turned, 2 * (s - 1))
                    for h in range(N_MEM_HEADS):
                        nc.scalar.activation(pm[:, s % 2, h, :], ps[:, 2 * (s % 2) + h // 2, (h % 2) * N_MEM:(h % 2 + 1) * N_MEM],
                                             ACT.Exp, bias=nb[:, s, h:h + 1], scale=SCALE, accum_out=rs[:, s, h:h + 1]).then_inc(exp_done, 1)
                if s >= 1:
                    u = s - 1
                    act.wait_ge(p_turned, 2 * u + 1)
                    if u >= 2:
                        act.wait_ge(o_mm, u - 1)
                    nc.scalar.activation(pmT[:, u % 2, 0, :, :].rearrange("p h n -> p (h n)"), ps[:, 4, :], ACT.Copy).then_inc(p_copied[0], 1)

        @block.vector
        def _(dve):
            link = Link(dve, dve_link)
            TSC, TT = nc.vector.tensor_scalar, nc.vector.tensor_tensor
            dve.wait_ge(gate_s_loaded, 32)
            for i, (c, n) in enumerate(GLU):
                t0, w = PIECES[n]
                dve.wait_ge(glu_sig, i + 1)
                TT(ag[:, 0:w], ps[:, 2 * (i % 2), 0:w], sg[:, i % 2, 0:w], ALU.mult).then_inc(glu_used, 1)
                dve.wait_ge(glu_used, i + 1)
                o = mixT[:, 8 + c, t0:t0 + w]
                link(TT(o, o, ag[:, 0:w], ALU.mult))
            dve.wait_ge(gate_m_loaded, 32)
            for s in range(QT + 2):
                if s < QT:
                    dve.wait_ge(s_mm, s + 1)
                    src = ps[:, 2 * (s % 2):2 * (s % 2) + 2, :].rearrange("p a (h n) -> p (a h) n", h=2)
                    link(nc.vector.tensor_reduce(nmx[:, s, :], src, AX_X, ALU.max, negate=True))
                    TSC(nb[:, s, :], nmx[:, s, :], SCALE, None, ALU.mult).then_inc(nb_ready, 1)
                if 1 <= s <= QT:
                    u = s - 1
                    dve.wait_ge(exp_done, 4 * (u + 1))
                    link(nc.vector.reciprocal(rinv[:, u, :], rs[:, u, :]))
                    TT(pm[:, u % 2, :, :], pm[:, u % 2, :, :], rinv[:, u, :].unsqueeze(2).to_broadcast([P, 4, N_MEM]),
                       ALU.mult).then_inc(p_ready, 1)
                if s >= 2:
                    u = s - 2
                    dve.wait_ge(o_mm, u + 1)
                    o = mixT[:, 12:16, u * P:(u + 1) * P]
                    TT(o, o, ps[:, 6 + u % 2, :].rearrange("p (h n) -> p h n", h=4), ALU.mult).then_inc(o_used, 1)
                if 1 <= s <= QT:
                    u = s - 1
                    dve.wait_ge(p_turned, 2 * u + 2)
                    nc.vector.tensor_copy(pmT[:, u % 2, 1, :, :].rearrange("p h n -> p (h n)"), ps[:, 5, :]).then_inc(p_copied[1], 1)


def block_d(nc, io, v, sem, sb_in):
    ident, ps, z_dram, mixT, kT, kv_tok, score = (v[n] for n in ("ident", "ps", "z_dram", "mixT", "kT", "kv_tok", "score"))
    own = ExitStack()
    with own:
        sb = lambda name, shape: sb_in(own, name, shape)
        kmq = sb("kmq", [P, SEQ])
        dist = sb("dist", [P, 2, SEQ])
        q_t = sb("q_t", [P, 2, N_HEADS, P])
        lg = sb("lg", [P, 2, SEQ])
        pr = sb("pr", [P, 2, GQA, SEQ])
        prT = sb("prT", [P, 2, GQA, P])
        inv_d = sb("inv_d", [P, 2, GQA, P])
        HEADS = QT * N_HEADS
        nmx = sb("nmx_d", [P, HEADS])
        rs = sb("rs_d", [P, HEADS])
        rinv = sb("rinv_d", [P, HEADS])

        q_loaded = [sem(f"q_loaded{b}") for b in range(2)]
        q_scaled, dist_ready, pool_link = sem("q_scaled"), sem("dist_ready"), sem("pool_link_d")
        s_mm, s_read, nm_ready = sem("s_mm_d"), sem("s_read_d"), sem("nm_ready_d")
        exp_done, rinv_ready, p_ready = sem("exp_done_d"), sem("rinv_ready_d"), sem("p_ready_d")
        p_turned, p_copied = sem("p_turned_d"), [sem(f"p_copied_d{k}") for k in range(2)]
        o_mm, o_used, dve_link = sem("o_mm_d"), sem("o_used_d"), sem("dve_link_d")
        SCALE = HEAD_DIM ** -0.5
        UNITS = [(t, g) for t in range(QT) for g in range(N_KV)]
        first_key_block = [sum(t + 1 for t, _ in UNITS[:u]) for u in range(len(UNITS) + 1)]

        def steps(u):
            kb = UNITS[u][0] + 1
            todo = []
            for k in range(kb):
                todo.append(("turn", k))
                if k:
                    todo.append(("value", k - 1))
            todo.append(("value", kb - 1))
            cut = [len(todo) * j // 4 for j in range(5)]
            return [todo[cut[j]:cut[j + 1]] for j in range(4)]

        block = own.enter_context(nc.Block(name="attend"))

        @block.sync
        def _(sp):
            for t in range(QT):
                if t >= 2:
                    sp.wait_ge(s_mm, N_HEADS * (t - 1))
                for s in range(N_HEADS // 2):
                    at = stored(OFF_Q + SLAB * s)
                    src = z_dram[at:at + 2, :, t * P:(t + 1) * P].rearrange("c p n -> p c n")
                    sp.dma_start(q_t[:, t % 2, 2 * s:2 * s + 2, :], src).then_inc(q_loaded[t % 2], 16)

        @block.gpsimd
        def _(pool):
            link = Link(pool, pool_link)
            link(nc.gpsimd.iota(kmq[:], pattern=[[1, SEQ]], base=-(SEQ - P), channel_multiplier=-1,
                                allow_small_or_imprecise_dtypes=True))
            link(nc.gpsimd.affine_select(out=kmq[:], in_=kmq[:], compare_op=ALU.is_ge, fill=FAR, base=SEQ - P,
                                         pattern=[[-1, SEQ]], channel_multiplier=1))

            def prepare(t):
                n = (t + 1) * P
                pool.wait_ge(q_loaded[t % 2], 64 * (t // 2 + 1))
                q = q_t[:, t % 2, :, :]
                nc.gpsimd.tensor_scalar(q, q, SCALE, None, ALU.mult).then_inc(q_scaled, 1)
                if t >= 2:
                    pool.wait_ge(s_read, N_HEADS * (t - 1))
                if t in IDX_TILES:
                    d = dist[:, t % 2, 0:n]
                    link(nc.gpsimd.tensor_scalar(d, score[:, IDX_OFF[t]:IDX_OFF[t] + n], CUT, FAR, ALU.is_ge, ALU.mult))
                    nc.gpsimd.tensor_tensor(d, d, kmq[:, SEQ - n:SEQ], ALU.add).then_inc(dist_ready, 1)
                else:
                    nc.gpsimd.tensor_copy(dist[:, t % 2, 0:n], kmq[:, SEQ - n:SEQ]).then_inc(dist_ready, 1)

            prepare(0)
            prepare(1)
            for u, (t, g) in enumerate(UNITS):
                if u >= 2:
                    pool.wait_ge(p_turned, first_key_block[u - 1])
                for j in range(GQA):
                    hh = GQA * u + j
                    pool.wait_ge(rinv_ready, hh + 1)
                    nc.gpsimd.tensor_scalar(inv_d[:, u % 2, j, :], ident[:], rinv[:, hh:hh + 1], None, ALU.mult).then_inc(p_ready, 1)
                if g == 1 and t + 2 < QT:
                    prepare(t + 2)

        @block.tensor
        def _(pe):
            def turn(u, k):
                gk = first_key_block[u] + k
                if gk >= 2:
                    pe.wait_ge(p_copied[gk % 2], gk // 2)
                for j in range(GQA):
                    last = nc.tensor.matmul(ps[:, 4 + gk % 2, j * P:(j + 1) * P], pr[:, u % 2, j, k * P:(k + 1) * P],
                                            inv_d[:, u % 2, j, :], start=True, stop=True)
                last.then_inc(p_turned, 1)

            def value(u, k):
                t, g = UNITS[u]
                gk = first_key_block[u] + k
                pe.wait_ge(p_copied[gk % 2], gk // 2 + 1)
                if k == 0 and u >= 2:
                    pe.wait_ge(o_used, u - 1)
                v_ = kv_tok[:, k, 256 + g * P:256 + (g + 1) * P]
                nc.tensor.matmul(ps[:, 6 + u % 2, :], v_, prT[:, gk % 2, :, :].rearrange("p j n -> p (j n)"),
                                 start=(k == 0), stop=(k == t)).then_inc(o_mm, 1)

            for s in range(len(UNITS) + 1):
                todo = steps(s - 1) if s else [[]] * 4
                for j in range(GQA):
                    if s < len(UNITS):
                        t, g = UNITS[s]
                        hh = GQA * s + j
                        if g == 0 and j == 0:
                            pe.wait_ge(q_scaled, t + 1)
                        if hh >= 2:
                            pe.wait_ge(s_read, hh - 1)
                        for x0 in range(0, (t + 1) * P, 512):
                            w = min(512, (t + 1) * P - x0)
                            last = nc.tensor.matmul(ps[:, 2 * (hh % 2) + x0 // 512, 0:w], q_t[:, t % 2, GQA * g + j, :],
                                                    kT[:, g, x0:x0 + w], start=True, stop=True)
                        last.then_inc(s_mm, 1)
                    if s and j == 0:
                        pe.wait_ge(p_ready, GQA * s)
                    for kind, k in todo[j]:
                        (turn if kind == "turn" else value)(s - 1, k)

        def copy_turned(eng, copy, u, todo, parity):
            for kind, k in todo:
                gk = first_key_block[u] + k
                if kind == "turn" and gk % 2 == parity:
                    eng.wait_ge(p_turned, gk + 1)
                    if gk >= 2:
                        eng.wait_ge(o_mm, gk - 1)
                    copy(prT[:, parity, :, :].rearrange("p j n -> p (j n)"), ps[:, 4 + parity, :]).then_inc(p_copied[parity], 1)

        @block.scalar
        def _(act):
            for s in range(len(UNITS) + 1):
                todo = steps(s - 1) if s else [[]] * 4
                for j in range(GQA):
                    if s < len(UNITS):
                        n = (UNITS[s][0] + 1) * P
                        hh = GQA * s + j
                        act.wait_ge(nm_ready, hh + 1)
                        if j == 0 and s >= 2:
                            act.wait_ge(p_turned, first_key_block[s - 1])
                        nc.scalar.activation(pr[:, s % 2, j, 0:n], lg[:, hh % 2, 0:n], ACT.Exp, bias=nmx[:, hh:hh + 1],
                                             accum_out=rs[:, hh:hh + 1]).then_inc(exp_done, 1)
                    copy_turned(act, nc.scalar.copy, s - 1, todo[j], 0)

        @block.vector
        def _(dve):
            link = Link(dve, dve_link)

            def invert(hh):
                dve.wait_ge(exp_done, hh + 1)
                nc.vector.reciprocal(rinv[:, hh:hh + 1], rs[:, hh:hh + 1]).then_inc(rinv_ready, 1)

            for s in range(len(UNITS) + 1):
                todo = steps(s - 1) if s else [[]] * 4
                for j in range(GQA):
                    if s < len(UNITS):
                        t, g = UNITS[s]
                        n = (t + 1) * P
                        hh = GQA * s + j
                        if g == 0 and j == 0:
                            dve.wait_ge(dist_ready, t + 1)
                        dve.wait_ge(s_mm, hh + 1)
                        src = ps[:, 2 * (hh % 2):2 * (hh % 2) + 2, :].rearrange("p a n -> p (a n)")[:, 0:n]
                        if hh >= 2:
                            dve.wait_ge(exp_done, hh - 1)
                        nc.vector.scalar_tensor_tensor(out=lg[:, hh % 2, 0:n], in0=dist[:, t % 2, 0:n],
                                                       scalar=2.0 ** (-8.0 * (GQA * g + j + 1) / N_HEADS), in1=src,
                                                       op0=ALU.mult, op1=ALU.add).then_inc(s_read, 1)
                        dve.wait_ge(s_read, hh + 1)
                        nc.vector.tensor_reduce(nmx[:, hh:hh + 1], lg[:, hh % 2, 0:n], AX_X, ALU.max, negate=True).then_inc(nm_ready, 1)
                        if j:
                            invert(hh - 1)
                    copy_turned(dve, nc.vector.tensor_copy, s - 1, todo[j], 1)
                if s < len(UNITS):
                    invert(GQA * s + 3)
                if s:
                    u = s - 1
                    t, g = UNITS[u]
                    dve.wait_ge(o_mm, first_key_block[u + 1])
                    o = mixT[:, GQA * g:GQA * (g + 1), t * P:(t + 1) * P]
                    nc.vector.tensor_tensor(o, o, ps[:, 6 + u % 2, :].rearrange("p (j n) -> p j n", j=GQA), ALU.mult).then_inc(o_used, 1)


def block_e(nc, io, v, sem, sb_in):
    ident, ps, z_dram, mixT, kT = (v[n] for n in ("ident", "ps", "z_dram", "mixT", "kT"))
    wis, qi_s, kiT, score = (v[n] for n in ("wis", "qi_s", "kiT", "score"))
    B, S = DEC_BATCH, DEC_SEQ
    PAGES = PAST_LEN // PAGE
    KEYS = PAST_LEN + S
    BLOCKS = PAGES + 1
    own = ExitStack()
    with own:
        sb = lambda name, shape, dt=F32: sb_in(own, name, shape, dt)
        pages = sb("pages", [1, B * PAGES], I32)
        k_in = score[:, 0:2048].rearrange("p (b n d) -> p b n d", b=2, n=PAGES)
        mk_in = score[:, 2048:4096].rearrange("p (b n d) -> p b n d", b=2, n=2)
        ki_in = sb("ki_in", [P, 2, PAGES, IDX_DIM])
        v_all = sb("v_all", [P, B, PAGES, 256])
        v_new = sb("v_new", [S, B, 256])
        mv_all = sb("mv_all", [P, B, 2, D_MEM])
        key_room = sb("key_room", [P, 3 * PAST_LEN])
        kbT = key_room[:, 0:N_KV * PAST_LEN].rearrange("p (g n) -> p g n", g=N_KV)
        kibT = key_room[:, N_KV * PAST_LEN:]
        mkbT = sb("mkbT", [P, 4, N_MEM])
        q_s = sb("q_s", [P, N_HEADS, NS])
        qm_s = sb("qm_s", [P, 4, NS])
        wi_all = sb("wi_all", [P, B, S, N_IDX])
        wi_b = sb("wi_b", [P, B, 2, N_IDX // 2, S])
        r_ = sb("r_", [P, BLOCKS, 2 * N_IDX // 2, S])
        sT = sb("sT", [P, BLOCKS, B, S])
        lateT = sb("lateT", [S, B, S])
        SEL = KEYS + 8
        sel = sb("sel", [NS, SEL])
        m8 = sb("m8_e", [NS, 8])
        qrow = sb("qrow", [1, NS])
        qcol = sb("qcol", [NS, 1])
        rm32 = sb("rm32", [NS, B])
        spread = sb("spread", [NS, 4, NS])
        rmask = sb("rmask", [P, B])
        slope = sb("slope", [P, N_KV])
        dist = sb("dist_e", [P, KEYS])
        acc = sb("acc_e", [P, N_KV, KEYS])
        acc_m = sb("acc_m", [P, N_MEM])
        pT = key_room[:, 0:N_KV * BLOCKS * P].rearrange("p (g n j b q) -> p g n j b q", g=N_KV, n=BLOCKS, j=4, b=B)
        pmT = sb("pmT_e", [P, 2, 4, B, S])
        sm = sb("sm_e", [P, 3, 4])

        pages_loaded, const_ready, pool_link = sem("pages_loaded"), sem("const_ready_e"), sem("pool_link_e")
        small_loaded, wi_written, wi_loaded = sem("small_loaded"), sem("wi_written"), sem("wi_loaded")
        k_loaded = [sem(f"k_loaded{b}") for b in range(2)]
        v_loaded = sem("v_loaded_e")
        k_turned, k_copied = sem("k_turned_e"), sem("k_copied_e")
        i_mm, i_read, s_mm, s_read = sem("i_mm"), sem("i_read"), sem("s_mm_e"), sem("s_read_e")
        dve_link, rows_made, rows_used = sem("dve_link_e"), sem("rows_made"), sem("rows_used")
        score_turned, score_in, chosen, spread_done = sem("score_turned"), sem("score_in"), sem("chosen"), sem("spread_done")
        scores_sT, logits, exp_done, p_ready = sem("scores_sT"), sem("logits_e"), sem("exp_done_e"), sem("p_ready_e")
        p_turned, p_copied, o_mm = sem("p_turned_e"), sem("p_copied_e"), sem("o_mm_e")
        SCALE = HEAD_DIM ** -0.5
        wi_dram = nc.dram_tensor("wi_scratch", (NS, N_IDX), F32, kind="Internal").ap()

        block = own.enter_context(nc.Block(name="sample"))

        @block.sync
        def _(sp):
            sp.dma_start(pages[:], io["page_table"].rearrange("b n -> (b n)").unsqueeze(0)).then_inc(pages_loaded, 16)
            sp.dma_start(wi_dram, wis[0:NS, QT, :]).then_inc(wi_written, 16)
            for s in range(4):
                at = stored(OFF_Q + SLAB * s)
                sp.dma_start(q_s[:, 2 * s:2 * s + 2, :], z_dram[at:at + 2, :, SEQ:TOK].rearrange("c p n -> p c n")).then_inc(small_loaded, 16)
            for s in range(2):
                at = stored(OFF_QM + SLAB * s)
                sp.dma_start(qm_s[:, 2 * s:2 * s + 2, :], z_dram[at:at + 2, :, SEQ:TOK].rearrange("c p n -> p c n")).then_inc(small_loaded, 16)
            sp.dma_start(v_new[:], io["out_v_s"][0].rearrange("b s h d -> s b (h d)")).then_inc(small_loaded, 16)
            sp.wait_ge(wi_written, 16)
            sp.dma_start(wi_all[:].rearrange("p b s h -> p (b s h)"), wi_dram.rearrange("t h -> (t h)").partition_broadcast(P)).then_inc(wi_loaded, 16)
            sp.wait_ge(pages_loaded, 16)
            for b in range(B):
                if b >= 2:
                    sp.wait_ge(k_turned, 3 * (b - 1))
                for n in range(PAGES):
                    page = sp.value_load(pages[0:1, b * PAGES + n:b * PAGES + n + 1], min_val=0, max_val=io["cache_k"].shape[1] - 1)
                    row = lambda name: io[name][0, bass.ds(page, 1)]
                    sp.dma_start(k_in[:, b % 2, n, :], row("cache_k").rearrange("a p h d -> (a p) (h d)")).then_inc(k_loaded[b % 2], 16)
                    sp.dma_start(ki_in[:, b % 2, n, :], row("cache_kidx").rearrange("a p d -> (a p) d")).then_inc(k_loaded[b % 2], 16)
                    sp.dma_start(v_all[:, b, n, :], row("cache_v").rearrange("a p h d -> (a p) (h d)")).then_inc(v_loaded, 16)
                sp.dma_start(mk_in[:, b % 2, :, :], io["cache_mem_k"][0, b].rearrange("(a p) h d -> p a (h d)", p=P)).then_inc(k_loaded[b % 2], 16)
                sp.dma_start(mv_all[:, b, :, :], io["cache_mem_v"][0, b].rearrange("(a p) h d -> p a (h d)", p=P)).then_inc(v_loaded, 16)

        @block.gpsimd
        def _(pool):
            link = Link(pool, pool_link)
            A = nc.gpsimd.affine_select
            link(nc.gpsimd.iota(qrow[:].rearrange("p (b q) -> p b q", q=S), pattern=[[0, B], [1, S]], base=0,
                                channel_multiplier=0, allow_small_or_imprecise_dtypes=True))
            link(nc.gpsimd.memset(lateT[:], 3e38))
            link(A(out=lateT[:], in_=lateT[:], compare_op=ALU.is_ge, fill=INVALID, base=0, pattern=[[0, B], [1, S]], channel_multiplier=-1))
            link(nc.gpsimd.memset(rm32[:], 1.0))
            link(A(out=rm32[:], in_=rm32[:], compare_op=ALU.is_ge, fill=0.0, base=0, pattern=[[-S, B]], channel_multiplier=1))
            link(A(out=rm32[:], in_=rm32[:], compare_op=ALU.is_ge, fill=0.0, base=S - 1, pattern=[[S, B]], channel_multiplier=-1))
            for j in range(4):
                link(nc.gpsimd.tensor_copy(spread[:, j, :], ident[0:NS, 0:NS]))
                for g in range(N_KV):
                    link(nc.gpsimd.memset(slope[NS * j:NS * (j + 1), g:g + 1], 2.0 ** (-8.0 * (GQA * g + j + 1) / N_HEADS)))
            link(nc.gpsimd.iota(dist[:], pattern=[[1, KEYS]], base=-PAST_LEN, channel_multiplier=0, allow_small_or_imprecise_dtypes=True))
            pool.wait_ge(small_loaded, 7 * 16)
            for q in (q_s, qm_s):
                last = nc.gpsimd.tensor_scalar(q[:], q[:], SCALE, None, ALU.mult)
            last.then_inc(const_ready, 1)

        @block.tensor
        def _(pe):
            pe.wait_ge(const_ready, 1)
            nc.tensor.transpose(ps[0:NS, 7, 0:1], qrow[:], ident[0:1, 0:1])
            nc.tensor.matmul(ps[:, 7, 8:8 + B], spread[:].rearrange("k j n -> k (j n)"), rm32[:], start=True, stop=True).then_inc(rows_made, 1)
            pe.wait_ge(rows_used, 1)
            for b in range(B):
                pe.wait_ge(k_loaded[b % 2], (2 * PAGES + 1) * 16 * (b // 2 + 1))
                if b:
                    pe.wait_ge(k_copied, 3 * b)
                for n in range(PAGES):
                    last = nc.tensor.transpose(ps[0:IDX_DIM, 0, n * P:(n + 1) * P], ki_in[:, b % 2, n, :], ident[:])
                last.then_inc(k_turned, 1)
                for g in range(N_KV):
                    if b:
                        pe.wait_ge(s_read, 4 * b)
                    for n in range(PAGES):
                        last = nc.tensor.transpose(ps[:, 1 + g, n * P:(n + 1) * P], k_in[:, b % 2, n, g * P:(g + 1) * P], ident[:])
                last.then_inc(k_turned, 1)
                for h in range(4):
                    for n in range(2):
                        last = nc.tensor.transpose(ps[:, 3 + h // 2, (2 * (h % 2) + n) * P:(2 * (h % 2) + n + 1) * P],
                                                   mk_in[:, b % 2, n, h * P:(h + 1) * P], ident[:])
                last.then_inc(k_turned, 1)
                pe.wait_ge(k_copied, 3 * b + 1)
                if b:
                    pe.wait_ge(i_read, 2 * b)
                for n in range(BLOCKS):
                    for a in range(2):
                        half = slice(a * IDX_DIM, (a + 1) * IDX_DIM)
                        keys = kibT[half, n * P:(n + 1) * P] if n < PAGES else kiT[half, a, SEQ + S * b:SEQ + S * (b + 1)]
                        m = P if n < PAGES else S
                        col = 64 + 32 * n
                        last = nc.tensor.matmul(ps[0:m, 5 + a, col:col + 32], keys, qi_s[half, :, S * b:S * (b + 1)], start=True, stop=True)
                last.then_inc(i_mm, 1)
                pe.wait_ge(k_copied, 3 * b + 3)
                for g in range(N_KV):
                    q = q_s[:, GQA * g:GQA * (g + 1), :].rearrange("p j n -> p (j n)")
                    nc.tensor.matmul(ps[:, 1 + g, :], q, kbT[:, g, :], start=True, stop=True)
                    last = nc.tensor.matmul(ps[:, 4, g * S:(g + 1) * S], q, kT[:, g, SEQ + S * b:SEQ + S * (b + 1)], start=True, stop=True)
                for h in range(4):
                    last = nc.tensor.matmul(ps[NS * h:NS * (h + 1), 7, 0:N_MEM], qm_s[:, h, :], mkbT[:, h, :], start=True, stop=True)
                last.then_inc(s_mm, 1)
            pe.wait_ge(scores_sT, 1)
            pe.wait_ge(s_read, 4 * B)
            for n in range(BLOCKS):
                m = P if n < PAGES else S
                out = ps[0:NS, 0, n * P:(n + 1) * P] if n < PAGES else ps[0:NS, 1, 0:S]
                last = nc.tensor.transpose(out, sT[0:m, n, :, :].rearrange("p b q -> p (b q)"), ident[0:m, 0:m])
            last.then_inc(score_turned, 1)
            pe.wait_ge(p_ready, 1)
            for n in range(2):
                last = nc.tensor.transpose(ps[:, 6, n * P:(n + 1) * P], acc_m[:, n * P:(n + 1) * P], ident[:])
            last.then_inc(p_turned, 1)
            pe.wait_ge(v_loaded, (PAGES + 1) * B * 16)
            pe.wait_ge(p_copied, 1)
            for h in range(4):
                for b in range(B):
                    for n in range(2):
                        last = nc.tensor.matmul(ps[:, 7, h * NS + S * b:h * NS + S * (b + 1)], mv_all[:, b, n, h * P:(h + 1) * P],
                                                pmT[:, n, h, b, :], start=(n == 0), stop=(n == 1))
            last.then_inc(o_mm, 1)
            pe.wait_ge(chosen, 1)
            rows = spread[:].rearrange("k j n -> k (j n)")
            nc.tensor.matmul(ps[:, 2, :], rows, sel[:, 0:PAST_LEN], start=True, stop=True)
            nc.tensor.matmul(ps[:, 3, 0:S], rows, sel[:, PAST_LEN:KEYS], start=True, stop=True).then_inc(spread_done, 1)
            for g in range(N_KV):
                pe.wait_ge(p_ready, 2 + g)
                for n in range(BLOCKS):
                    w = P if n < PAGES else S
                    out = ps[:, 4 + 2 * g, n * P:(n + 1) * P] if n < PAGES else ps[0:S, 5 - 4 * g, 0:P]
                    last = nc.tensor.transpose(out, acc[:, g, n * P:n * P + w], ident[:])
                last.then_inc(p_turned, 1)
            pe.wait_ge(p_copied, 3)
            for g in range(N_KV):
                for b in range(B):
                    out = ps[:, 0, g * P:(g + 1) * P].rearrange("p (j b q) -> p j b q", j=4, b=B)[:, :, b, :]
                    for n in range(BLOCKS):
                        m = P if n < PAGES else S
                        vals = v_all[:, b, n, g * P:(g + 1) * P] if n < PAGES else v_new[:, b, g * P:(g + 1) * P]
                        last = nc.tensor.matmul(out, vals, pT[0:m, g, n, :, b, :], start=(n == 0), stop=(n == BLOCKS - 1))
            last.then_inc(o_mm, 1)

        @block.scalar
        def _(act):
            for b in range(B):
                act.wait_ge(k_turned, 3 * b + 1)
                if b:
                    act.wait_ge(i_mm, b)
                nc.scalar.copy(kibT[0:IDX_DIM, :], ps[0:IDX_DIM, 0, :])
                nc.scalar.copy(kibT[IDX_DIM:P, :], ps[0:IDX_DIM, 0, :]).then_inc(k_copied, 1)
                act.wait_ge(k_turned, 3 * b + 2)
                if b:
                    act.wait_ge(s_mm, b)
                nc.scalar.copy(key_room[:, 0:N_KV * PAST_LEN], ps[:, 1:3, :].rearrange("p g n -> p (g n)")).then_inc(k_copied, 1)
                act.wait_ge(k_turned, 3 * b + 3)
                nc.scalar.copy(mkbT[:].rearrange("p h n -> p (h n)"), ps[:, 3:5, :].rearrange("p g n -> p (g n)")).then_inc(k_copied, 1)
            act.wait_ge(logits, 1)
            nc.scalar.activation(acc_m[:], acc_m[:], ACT.Exp, bias=sm[:, 0, 2:3], accum_out=sm[:, 1, 2:3]).then_inc(exp_done, 1)
            act.wait_ge(p_turned, 1)
            nc.scalar.copy(pmT[:].rearrange("p n h b q -> p (n h b q)"), ps[:, 6, 0:2 * P]).then_inc(p_copied, 1)
            for g in range(N_KV):
                act.wait_ge(logits, 2 + g)
                nc.scalar.activation(acc[:, g, :], acc[:, g, :], ACT.Exp, bias=sm[:, 0, g:g + 1], accum_out=sm[:, 1, g:g + 1]).then_inc(exp_done, 1)
            for g in range(N_KV):
                act.wait_ge(p_turned, 2 + g)
                nc.scalar.copy(pT[:, g, 0:PAGES, :, :, :].rearrange("p n j b q -> p (n j b q)"), ps[:, 4 + 2 * g, :])
                nc.scalar.copy(pT[0:S, g, PAGES, :, :, :].rearrange("p j b q -> p (j b q)"), ps[0:S, 5 - 4 * g, 0:P]).then_inc(p_copied, 1)

        @block.vector
        def _(dve):
            link = Link(dve, dve_link)
            TSC, TT, STT = nc.vector.tensor_scalar, nc.vector.tensor_tensor, nc.vector.scalar_tensor_tensor
            copy = nc.vector.tensor_copy
            dve.wait_ge(rows_made, 1)
            link(copy(qcol[:], ps[0:NS, 7, 0:1]))
            copy(rmask[:], ps[:, 7, 8:8 + B]).then_inc(rows_used, 1)
            dve.wait_ge(rows_used, 1)
            dve.wait_ge(wi_loaded, 16)
            for a in range(2):
                src = wi_all[:].rearrange("p b s (c a) -> p b s c a", a=2)
                for c in range(N_IDX // 2):
                    last = copy(wi_b[:, :, a, c, :], src[:, :, :, c, a])
            link(last)
            for b in range(B):
                dve.wait_ge(i_mm, b + 1)
                for rows, blocks in ((slice(0, P), slice(0, PAGES)), (slice(0, S), slice(PAGES, BLOCKS))):
                    n = blocks.stop - blocks.start
                    src = ps[rows, 5:7, 64 + blocks.start * 32:64 + blocks.stop * 32].rearrange("p a (n x) -> p a n x", n=n)
                    r = r_[rows, blocks, :, :]
                    last = TSC(r.rearrange("p n (a c) q -> p a n (c q)", a=2), src, IDX_DIM ** -0.5, 0.0, ALU.mult, ALU.max)
                    last.then_inc(i_read, 1)
                    dve.wait_ge(i_read, 2 * b + (1 if n > 1 else 2))
                    wb_ = wi_b[rows, b, :, :, :].rearrange("p a c q -> p (a c) q").unsqueeze(1).to_broadcast([rows.stop, n, N_IDX, S])
                    link(TT(r, r, wb_, ALU.mult))
                    link(nc.vector.tensor_reduce(sT[rows, blocks, b, :], r.rearrange("p n c q -> p n q c"), AX_X, ALU.add))
                dve.wait_ge(s_mm, b + 1)
                rm = rmask[:, b:b + 1]
                for out, src in ((acc[:, :, 0:PAST_LEN], ps[:, 1:3, :]), (acc[:, :, PAST_LEN:KEYS], ps[:, 4, 0:2 * S].rearrange("p (g n) -> p g n", g=2)),
                                 (acc_m[:], ps[:, 7, 0:N_MEM])):
                    if b == 0:
                        last = TSC(out, src, rm, None, ALU.mult)
                    else:
                        last = STT(out=out, in0=src, scalar=rm, in1=out, op0=ALU.mult, op1=ALU.add)
                    last.then_inc(s_read, 1)
                copy(sm[:, 2, 3:4], rm).then_inc(s_read, 1)
                dve.wait_ge(s_read, 4 * b + 4)
            TT(sT[0:S, PAGES, :, :], sT[0:S, PAGES, :, :], lateT[:], ALU.min).then_inc(scores_sT, 1)

            def invert(k, group, p):
                dve.wait_ge(exp_done, k + 1)
                link(nc.vector.reciprocal(sm[:, 2, group:group + 1], sm[:, 1, group:group + 1]))
                TSC(p, p, sm[:, 2, group:group + 1], None, ALU.mult).then_inc(p_ready, 1)

            nc.vector.tensor_reduce(sm[:, 0, 2:3], acc_m[:], AX_X, ALU.max, negate=True).then_inc(logits, 1)
            dve.wait_ge(score_turned, 1)
            link(nc.vector.memset(sel[:, KEYS:SEL], PAD))
            link(copy(sel[:, 0:PAST_LEN], ps[0:NS, 0, :]))
            link(copy(sel[:, PAST_LEN:KEYS], ps[0:NS, 1, 0:S]))
            invert(0, 2, acc_m[:])
            for n in range(TOPK_S // 8 + 1):
                link(nc.vector.max(out=m8[:], in_=sel[:]))
                if n == TOPK_S // 8:
                    link(nc.vector.memset(m8[:, TOPK_S % 8:8], PAD))
                link(nc.vector.match_replace(out=sel[:], in_to_replace=m8[:], in_values=sel[:], imm_value=REPLACED))
            s_ = sel[:, 0:KEYS]
            link(TSC(s_, s_, CUT, FAR, ALU.is_ge, ALU.mult))
            link(TT(s_, s_, dist[0:NS, :], ALU.add))
            TSC(s_, s_, qcol[:], None, ALU.subtract).then_inc(chosen, 1)
            dve.wait_ge(spread_done, 1)
            link(copy(dist[:, 0:PAST_LEN], ps[:, 2, :]))
            link(copy(dist[:, PAST_LEN:KEYS], ps[:, 3, 0:S]))
            for g in range(N_KV):
                link(STT(out=acc[:, g, :], in0=dist[:], scalar=slope[:, g:g + 1], in1=acc[:, g, :], op0=ALU.mult, op1=ALU.add))
                nc.vector.tensor_reduce(sm[:, 0, g:g + 1], acc[:, g, :], AX_X, ALU.max, negate=True).then_inc(logits, 1)
            for g in range(N_KV):
                invert(1 + g, g, acc[:, g, :])
            dve.wait_ge(o_mm, 1)
            o = mixT[:, 12:16, SEQ:TOK]
            TT(o, o, ps[:, 7, 0:P].rearrange("p (h n) -> p h n", h=4), ALU.mult)
            dve.wait_ge(o_mm, 2)
            o = mixT[:, 0:8, SEQ:TOK]
            TT(o, o, ps[:, 0, 0:2 * P].rearrange("p (h n) -> p h n", h=8), ALU.mult)


def block_f(nc, io, v, sem, sb_in):
    ps, mixT = v["ps"], v["mixT"]
    own = ExitStack()
    with own:
        sb = lambda name, shape: sb_in(own, name, shape)
        w_o = sb("w_o", [P, 2, KT, SLAB])
        y = sb("y_f", [P, QT + 1, D_MODEL])
        g_b = sb("g_f", [P, D_MODEL])
        sq = v["score"][:, 0:2 * SLAB].rearrange("p (a n) -> p a n", a=2)
        NSLAB = D_MODEL // SLAB
        ss = sb("ss_f", [P, QT + 1, NSLAB])
        st = sb("st_f", [P, QT + 1, 4])

        w_loaded = [sem(f"w_o_loaded{b}") for b in range(2)]
        x_loaded, g_loaded = sem("x_again"), sem("g_f_loaded")
        y_mm, banks_free, y_sq, ms_ready, rt_ready, fin = (sem(n) for n in ("yo_mm", "banks_free", "yo_sq", "ms_f", "rt_f", "fin_f"))
        dve_link, stored_y = sem("dve_link_f"), sem("stored_y")

        RING = 6

        def rows(t):
            return P if t < QT else NS

        block = own.enter_context(nc.Block(name="out"))

        @block.sync
        def _(sp):
            w_rows = io["w_out"][0].rearrange("(k p) n -> p k n", p=P)
            for s in range(NSLAB):
                if s >= 2:
                    sp.wait_ge(y_mm, (QT + 1) * (s - 1))
                sp.dma_start(w_o[:, s % 2, :, :], w_rows[:, :, s * SLAB:(s + 1) * SLAB]).then_inc(w_loaded[s % 2], 16)
                if s == 0:
                    for t in range(QT + 1):
                        src = io["x_prompt"][0, t * P:(t + 1) * P, :] if t < QT else io["x_sample"].rearrange("b s d -> (b s) d")
                        sp.dma_start(y[0:rows(t), t, :], src).then_inc(x_loaded, 16)
                    sp.dma_start(g_b[:], io["g_final"].partition_broadcast(P)).then_inc(g_loaded, 16)
            for t in range(QT + 1):
                sp.wait_ge(fin, t + 1)
                dst = io["out_y_p"][0, t * P:(t + 1) * P, :] if t < QT else io["out_y_s"].rearrange("b s d -> (b s) d")
                sp.dma_start(dst, y[0:rows(t), t, :]).then_inc(stored_y, 16)
            sp.wait_ge(stored_y, 16 * (QT + 1))

        @block.tensor
        def _(pe):
            with pe.Fori(0, NSLAB // 2) as it:
                for b in range(2):
                    pe.wait_ge(w_loaded[b], it * 16 + 16)
                    for t in range(QT + 1):
                        i = (QT + 1) * b + t
                        pe.wait_ge(banks_free, it * (2 * (QT + 1)) + (i + 1))
                        for k in range(KT):
                            last = nc.tensor.matmul(ps[0:rows(t), i % RING, 0:SLAB], mixT[:, k, t * P:t * P + rows(t)],
                                                    w_o[:, b, k, :], start=(k == 0), stop=(k == KT - 1))
                        last.then_inc(y_mm, 1)

        def slab(ap, it, b):
            return ap.rearrange("p (s n) -> p s n", n=SLAB)[:, bass.ds(it * 2 + b, 1), :].rearrange("p a n -> p (a n)")

        @block.vector
        def _(dve):
            link = Link(dve, dve_link)
            TSC, TT = nc.vector.tensor_scalar, nc.vector.tensor_tensor
            dve.sem_inc(banks_free, RING)
            dve.wait_ge(x_loaded, 16 * (QT + 1))

            def add(it, b, t):
                i = (QT + 1) * b + t
                dve.wait_ge(y_mm, it * (2 * (QT + 1)) + (i + 1))
                o = slab(y[0:rows(t), t, :], it, b)
                TT(o, o, ps[0:rows(t), i % RING, 0:SLAB], ALU.add).then_inc(banks_free, 1)

            def finish(t):
                n = rows(t)
                dve.wait_ge(y_sq, 2 + (QT + 1) * (NSLAB - 1) + t + 1)
                link(nc.vector.tensor_reduce(st[0:n, t, 0:1], ss[0:n, t, :], AX_X, ALU.add))
                TSC(st[0:n, t, 1:2], st[0:n, t, 0:1], 1.0 / D_MODEL, EPS, ALU.mult, ALU.add).then_inc(ms_ready, 1)
                dve.wait_ge(rt_ready, t + 1)
                link(nc.vector.reciprocal(st[0:n, t, 3:4], st[0:n, t, 2:3]))
                nc.vector.scalar_tensor_tensor(out=y[0:n, t, :], in0=y[0:n, t, :], scalar=st[0:n, t, 3:4], in1=g_b[0:n, :],
                                               op0=ALU.mult, op1=ALU.mult).then_inc(fin, 1)

            with dve.Fori(0, NSLAB // 2 - 1) as it:
                for b in range(2):
                    for t in range(QT + 1):
                        add(it, b, t)
            dve.wait_ge(g_loaded, 16)
            for b in range(2):
                for t in range(QT + 1):
                    add(NSLAB // 2 - 1, b, t)
                    if b and t:
                        finish(t - 1)
            finish(QT)

        @block.scalar
        def _(act):
            act.sem_inc(y_sq, 2)

            def square(it, b, t):
                i = (QT + 1) * b + t
                act.wait_ge(banks_free, it * (2 * (QT + 1)) + (i + 1 + RING))
                act.wait_ge(y_sq, it * (2 * (QT + 1)) + (i + 1))
                n = rows(t)
                nc.scalar.activation(sq[0:n, i % 2, :], slab(y[0:n, t, :], it, b), ACT.Square,
                                     accum_out=ss[0:n, t, bass.ds(it * 2 + b, 1)]).then_inc(y_sq, 1)

            with act.Fori(0, NSLAB // 2 - 1) as it:
                for b in range(2):
                    for t in range(QT + 1):
                        square(it, b, t)
            for b in range(2):
                for t in range(QT + 1):
                    square(NSLAB // 2 - 1, b, t)
                    if b:
                        act.wait_ge(ms_ready, t + 1)
                        n = rows(t)
                        nc.scalar.activation(st[0:n, t, 2:3], st[0:n, t, 1:2], ACT.Sqrt).then_inc(rt_ready, 1)


_INS = ["x_prompt", "x_sample", "mem_prompt", "cache_k", "cache_v", "cache_kidx", "cache_mem_k", "cache_mem_v",
        "state_ssm_re", "state_ssm_im", "page_table", "g_norm", "w_in", "g_mem", "w_mem_kv", "lam_re", "lam_im",
        "log_dt", "b_re", "b_im", "c_re", "c_im", "d_skip", "w_glu", "w_out", "g_final"]
_OUTS = {
    "out_y_p": (1, SEQ, D_MODEL), "out_y_s": (DEC_BATCH, DEC_SEQ, D_MODEL),
    "out_k_p": (1, 1, SEQ, N_KV, HEAD_DIM), "out_v_p": (1, 1, SEQ, N_KV, HEAD_DIM), "out_kidx_p": (1, 1, SEQ, IDX_DIM),
    "out_mk": (1, 1, N_MEM, N_MEM_HEADS, HEAD_DIM), "out_mv": (1, 1, N_MEM, N_MEM_HEADS, HEAD_DIM),
    "out_ssm_re_p": (1, 1, GROUPS, STATE), "out_ssm_im_p": (1, 1, GROUPS, STATE),
    "out_k_s": (1, DEC_BATCH, DEC_SEQ, N_KV, HEAD_DIM), "out_v_s": (1, DEC_BATCH, DEC_SEQ, N_KV, HEAD_DIM),
    "out_kidx_s": (1, DEC_BATCH, DEC_SEQ, IDX_DIM),
    "out_ssm_re_s": (1, DEC_BATCH, GROUPS, STATE), "out_ssm_im_s": (1, DEC_BATCH, GROUPS, STATE),
}


def kernel(**inputs):
    import numpy as _np
    import concourse.bacc as _bacc
    from concourse import mybir as _mybir
    from concourse.bass_utils import run_bass_kernel_spmd as _run

    nc = _bacc.Bacc("TRN2", target_bir_lowering=False, num_devices=1)
    arrays, io = {}, {}
    for name in _INS:
        a = _np.ascontiguousarray(inputs[name])
        arrays[f"in_{name}_dram"] = a
        io[name] = nc.dram_tensor(f"in_{name}_dram", a.shape, _mybir.dt.from_np(a.dtype), kind="ExternalInput").ap()
    for name, shape in _OUTS.items():
        io[name] = nc.dram_tensor(f"{name}_dram", shape, F32, kind="ExternalOutput").ap()
    build_program(nc, io)
    r = _run(nc, [arrays], core_ids=[0])
    return tuple(r.results[0][f"{name}_dram"] for name in _OUTS)
```

```python
import math
from contextlib import ExitStack

import numpy as np

import concourse.bass as bass
from concourse import mybir

F32 = mybir.dt.float32
F16 = mybir.dt.float16
BF16 = mybir.dt.bfloat16
I32 = mybir.dt.int32
ALU = mybir.AluOpType
ACT = mybir.ActivationFunctionType
AX_X = mybir.AxisListType.X

P = 128
D_MODEL, SEQ, DEC_BATCH, DEC_SEQ, PAST_LEN, PAGE = 2048, 1024, 8, 4, 512, 128
HEAD_DIM, N_HEADS, N_KV, GQA = 128, 8, 2, 4
N_IDX, IDX_DIM = 16, 64
GROUPS, GROUP, STATE = 32, 16, 64
N_MEM, N_MEM_HEADS = 256, 4
D_SSM = D_MEM = 512
EPS = 1e-6
TOPK = min(256, SEQ // 4)
TOPK_S = min(256, (PAST_LEN + DEC_SEQ) // 4)
KT = D_MODEL // P
NS = DEC_BATCH * DEC_SEQ
TOK = SEQ + NS
QT = SEQ // P
PIECES = [(TOK // 3 * n, TOK // 3) for n in range(3)]
STEPS = [(0, 512), (512, 512), (SEQ, NS)]
OFF_Q, OFF_K, OFF_V, OFF_GA = 0, 1024, 1280, 1536
OFF_QI, OFF_KI, OFF_U, OFF_GS, OFF_QM, OFF_GM = 2560, 3584, 3664, 4176, 4688, 5200
KIWI = IDX_DIM + N_IDX
SLAB = 256
CHUNK = 128
ROOT_H = 256.0
W_SHIFT = 2.0 ** -14
M_SHIFT = 2.0 ** -15
TINY = 1e-30
LOOPS = 4
KEPT = [OFF_Q + SLAB * s for s in range(6)] + [OFF_QM, OFF_QM + SLAB]
GATE = [OFF_GA + SLAB * s for s in range(4)] + [OFF_GS, OFF_GS + SLAB, OFF_GM, OFF_GM + SLAB]
LOOP_SLABS = [c for s in range(0, 8, 2) for c in (KEPT[s], GATE[s], KEPT[s + 1], GATE[s + 1])]


def stored(col):
    for n, c in enumerate(LOOP_SLABS):
        if c <= col < c + SLAB:
            return 2 * n + (col - c) // P
    raise ValueError(col)


_pieces = [OFF_QI + SLAB * s for s in range(4)] + [OFF_U + SLAB * s for s in range(2)] + LOOP_SLABS
CHUNKS = [(OFF_KI, KIWI)] + [(c + d, CHUNK) for c in _pieces for d in (0, CHUNK)]
CHUNKS += CHUNKS[-1:]


def load_chunk(eng, io, wb, w_loaded, c):
    col, w = CHUNKS[c]
    src = io["w_in"][0].rearrange("(k p) n -> p k n", p=P)[:, :, col:col + w]
    eng.dma_start(wb[:, c % 2, :, 0:w], src).then_inc(w_loaded[c % 2], 16)


TILES = 16
LO = 32
INVALID, PAD, REPLACED, CUT, FAR = -2e38, -2.2e38, -3e38, -2.5e38, -1e30
IDX_TILES = list(range(TOPK // P, QT))
IDX_OFF = {t: P * sum(x + 1 for x in IDX_TILES if x < t) for t in IDX_TILES}
IDX_COLS = P * sum(x + 1 for x in IDX_TILES)
ROUNDS = TOPK // 8
TWO_PI = 2 * np.pi
PI_A = 6.28125
PI_B = float(np.float32(np.round((TWO_PI - PI_A) * 2**20) / 2**20))
PI_C = float(np.float32(TWO_PI - PI_A - PI_B))
MAGIC = 1.5 * 2**23
PI_IN = float(np.nextafter(np.float32(np.pi), np.float32(0)))


class Link:

    def __init__(self, eng, sem, base=0):
        self.eng, self.sem, self.base, self.n = eng, sem, base, 0

    def __call__(self, ins):
        ins.then_inc(self.sem, 1)
        self.n += 1
        self.eng.wait_ge(self.sem, self.base + self.n)
        return ins


def build_program(nc, io):
    top = ExitStack()

    def sb_in(ctx, name, shape, dt=F32):
        return ctx.enter_context(nc.sbuf_tensor(name, shape, dt))

    def sem(name):
        return top.enter_context(nc.semaphore(name))

    with top:
        ps = top.enter_context(nc.psum_tensor("ps", [P, 8, 512], F32))
        z_dram = nc.dram_tensor("z_scratch", (len(LOOP_SLABS) * 2, P, TOK), F32, kind="Internal").ap()
        y_dram = nc.dram_tensor("y_scratch", (4, P, TOK), F32, kind="Internal").ap()

        ident = sb_in(top, "ident", [P, P])
        wis = sb_in(top, "wis", [P, QT + 1, N_IDX])
        cmin = sb_in(top, "cmin", [P, P])
        score = sb_in(top, "score", [P, IDX_COLS])
        ones = sb_in(top, "ones", [P, P])
        qi_s = sb_in(top, "qi_s", [P, N_IDX // 2, NS])
        kiT = sb_in(top, "kiT", [P, 2, TOK])

        mid = ExitStack()
        with mid:
            h16 = sb_in(mid, "h16", [P, 2, KT, TOK], F16)
            h_unit = sb_in(mid, "h_unit", [P, 1])
            par = sb_in(mid, "par", [P, 5, TILES])
            tabs = sb_in(mid, "tabs", [P, 2, TILES, 2, LO])
            bbar = sb_in(mid, "bbar", [P, 2, TILES, GROUP])
            cnat = sb_in(mid, "cnat", [P, 2, 4, STATE])
            dcol = sb_in(mid, "dcol", [P, 4])
            mask_c = sb_in(mid, "mask_c", [P, 8])
            mask_b = sb_in(mid, "mask_b", [P, 4, 8])
            h0 = sb_in(mid, "h0", [P, 2, DEC_BATCH, TILES])
            h_last = sb_in(mid, "h_last", [P, 2, 1 + DEC_BATCH, TILES])
            lam = sb_in(mid, "lam", [P, 3, TILES])
            bnat = sb_in(mid, "bnat", [P, 2, TILES, GROUP])
            pw = sb_in(mid, "pw", [P, 10])
            wb = sb_in(mid, "wb", [P, 2, KT, CHUNK])
            w_loaded = [sem(f"w_loaded{b}") for b in range(2)]
            kv_stored = sem("kv_stored")
            block_a(nc, io, locals(), sem, sb_in)
            block_b(nc, io, locals(), sem, sb_in)
        late = ExitStack()
        with late:
            y_room = sb_in(late, "y_room", [P, (QT + 1) * D_MODEL])
            mixT = y_room[:, 0:KT * TOK].rearrange("p (k n) -> p k n", k=KT)
            mix_size = sb_in(late, "mix_size", [P, KT + 2])
            w_first = top.enter_context(nc.semaphore("w_first"))
            with ExitStack() as heads:
                kT = sb_in(heads, "kT", [P, N_KV, TOK])
                pages = sb_in(heads, "pages", [1, DEC_BATCH * (PAST_LEN // PAGE)], I32)
                ki_in = sb_in(heads, "ki_in", [P, 2, PAST_LEN // PAGE, IDX_DIM])
                lateT = sb_in(heads, "lateT", [DEC_SEQ, DEC_BATCH, DEC_SEQ])
                qrow = sb_in(heads, "qrow", [1, NS])
                rm32 = sb_in(heads, "rm32", [NS, DEC_BATCH])
                spread = sb_in(heads, "spread", [NS, 4, NS])
                slope = sb_in(heads, "slope", [P, N_KV])
                dist_e = sb_in(heads, "dist_e", [P, PAST_LEN + DEC_SEQ])
                pages_loaded = sem("pages_loaded")
                k_loaded = [sem(f"k_loaded{b}") for b in range(2)]
                with ExitStack() as by_token:
                    kv_tok = sb_in(by_token, "kv_tok", [P, QT + 1, 2 * N_KV * HEAD_DIM])
                    v_or_q = sb_in(by_token, "v_or_q", [P, N_KV * TOK])
                    kmq = sb_in(by_token, "kmq", [P, SEQ])
                    q_loaded = [sem(f"q_loaded{b}") for b in range(2)]
                    pool_link = sem("pool_link_c")
                    block_c(nc, io, locals(), sem, sb_in)
                    block_d(nc, io, locals(), sem, sb_in)
                block_e(nc, io, locals(), sem, sb_in)
            block_f(nc, io, locals(), sem, sb_in)


def block_a(nc, io, v, sem, sb_in):
    ident, cmin, h16, h_unit, par, tabs, bbar = (v[n] for n in ("ident", "cmin", "h16", "h_unit", "par", "tabs", "bbar"))
    cnat, dcol, mask_c, mask_b, h0, ps = (v[n] for n in ("cnat", "dcol", "mask_c", "mask_b", "h0", "ps"))
    lam, bnat, pw = (v[n] for n in ("lam", "bnat", "pw"))
    own = ExitStack()
    with own:
        sb = lambda name, shape: sb_in(own, name, shape)
        x_in = sb("x_in", [P, 2, D_MODEL])
        h_tok = sb("h_tok", [P, 2, D_MODEL])
        g_b = sb("g_b", [P, 2, D_MODEL])
        g_max = sb("g_max", [P, 2])
        memT = sb("memT", [P, KT, N_MEM])
        w_kv = sb("w_kv", [P, 4, 2 * D_MEM])
        kv_mem = v["score"][:, D_MODEL:D_MODEL + 4 * D_MEM].rearrange("p (a n) -> p a n", a=2)
        sq = v["score"][:, 0:D_MODEL]
        stat = sb("stat_a", [P, 3, QT + 3])
        rms = sb("rms_a", [P, QT + 3])
        lam_in = v["wb"][0:TILES, 1, 0:3, :]
        st_in = v["wb"][:, 1, 4:6, :]
        dt_in = sb("dt_in", [TILES, 2])
        d_in = sb("d_in", [4, P])

        x_loaded = [sem(f"x_loaded{b}") for b in range(2)]
        g_loaded = [sem("g_mem_loaded"), sem("g_norm_loaded")]
        w_kv_loaded = [sem(f"w_kv_loaded{b}") for b in range(4)]
        kv_step = sem("kv_step")
        kv_evac = sem("kv_evac")
        kv_stored = v["kv_stored"]
        params_loaded = sem("params_loaded")
        squares = sem("squares")
        mean_sq = sem("mean_sq")
        root = sem("root")
        h_ready = sem("h_ready")
        h_transposed = sem("h_transposed")
        evac_a = [sem("evac_even"), sem("evac_odd")]
        high_made = sem("high_made")
        ident_ready = sem("ident_ready")
        pool_link = sem("pool_link_a")
        consts_ready = sem("consts_ready")
        lam_ready = sem("lam_ready")
        dt_spread = sem("dt_spread")
        st_transposed = sem("st_transposed")
        dve_link = sem("dve_link_a")

        MT = N_MEM // P
        ALL = MT + QT + 1

        def rows(t):
            return P if t < ALL - 1 else NS

        def source(t):
            if t < MT:
                return io["mem_prompt"][0, t * P:(t + 1) * P, :]
            if t < MT + QT:
                return io["x_prompt"][0, (t - MT) * P:(t - MT + 1) * P, :]
            return io["x_sample"].rearrange("b s d -> (b s) d")


        block = own.enter_context(nc.Block(name="setup"))

        @block.sync
        def _(sp):
            for t in range(ALL):
                b, n = t % 2, rows(t)
                if t < 2:
                    g = io["g_norm" if t else "g_mem"]
                    sp.dma_start(g_b[:, t, :], g[0].partition_broadcast(P)).then_inc(g_loaded[t], 16)
                if t >= 2:
                    sp.wait_ge(squares, t - 1)
                    sp.wait_ge(h_ready, t - 1)
                sp.dma_start(x_in[0:n, b, :], source(t)).then_inc(x_loaded[b], 16)
            load_chunk(sp, io, v["wb"], v["w_loaded"], 0)

        @block.gpsimd
        def _(pool):
            link = Link(pool, pool_link)
            pool.dma_start(lam_in[:, 0, :], io["lam_re"][0].rearrange("(i a) n -> i (a n)", a=2)).then_inc(params_loaded, 16)
            pool.dma_start(lam_in[:, 1, :], io["lam_im"][0].rearrange("(i a) n -> i (a n)", a=2)).then_inc(params_loaded, 16)
            pool.dma_start(dt_in[:], io["log_dt"][0].rearrange("(i a) -> i a", a=2)).then_inc(params_loaded, 16)
            for n, name in enumerate(("b_re", "b_im")):
                pool.dma_start(bnat[:, n, :, :], io[name][0].rearrange("(i a) n c -> (a n) i c", a=2)).then_inc(params_loaded, 16)
            for n, name in enumerate(("c_re", "c_im")):
                src = io[name][0].rearrange("(j g) c n -> (g c) j n", j=4)
                pool.dma_start(cnat[:, n, :, :], src).then_inc(params_loaded, 16)
            for n, name in enumerate(("state_ssm_re", "state_ssm_im")):
                pool.dma_start(st_in[:, n, :], io[name][0].rearrange("b (i a) n -> (b i) (a n)", a=2)).then_inc(params_loaded, 16)
            pool.dma_start(d_in[:], io["d_skip"][0].rearrange("(j g) c -> j (g c)", j=4)).then_inc(params_loaded, 16)
            link(nc.gpsimd.memset(ident[:], 0.0))
            nc.gpsimd.affine_select(out=ident[:], in_=ident[:], compare_op=ALU.not_equal, fill=1.0, base=0,
                                    pattern=[[-1, P]], channel_multiplier=1).then_inc(ident_ready, 1)
            link(nc.gpsimd.memset(cmin[:], 3e38))
            link(nc.gpsimd.affine_select(out=cmin[:], in_=cmin[:], compare_op=ALU.is_ge, fill=INVALID, base=0,
                                         pattern=[[-1, P]], channel_multiplier=1))
            link(nc.gpsimd.memset(mask_c[:], 1.0))
            link(nc.gpsimd.affine_select(out=mask_c[:], in_=mask_c[:], compare_op=ALU.is_ge, fill=0.0, base=0,
                                         pattern=[[-GROUP, 8]], channel_multiplier=1))
            link(nc.gpsimd.affine_select(out=mask_c[:], in_=mask_c[:], compare_op=ALU.is_ge, fill=0.0, base=GROUP - 1,
                                         pattern=[[GROUP, 8]], channel_multiplier=-1))
            link(nc.gpsimd.memset(mask_b[:], 0.0))
            for r in range(4):
                for a in range(2):
                    link(nc.gpsimd.memset(mask_b[a * STATE:(a + 1) * STATE, r, 2 * r + a:2 * r + a + 1], 1.0))
            for k in range(10):
                link(nc.gpsimd.memset(pw[:, k:k + 1], float(2**k)))
            kiT = v["kiT"]
            link(nc.gpsimd.memset(kiT[IDX_DIM:P, 0, :], 0.0))
            link(nc.gpsimd.memset(kiT[0:IDX_DIM, 1, :], 0.0))
            nc.gpsimd.memset(v["ones"][:], 1.0).then_inc(consts_ready, 1)
            for k in range(KT):
                if k >= 4:
                    pool.wait_ge(kv_step, k - 3)
                pool.dma_start(w_kv[:, k % 4, :], io["w_mem_kv"][0, k * P:(k + 1) * P, :]).then_inc(w_kv_loaded[k % 4], 16)


        def evac(eng, copy, parity, t):
            n = rows(t)
            if t < MT:
                for q in range(parity, 4, 2):
                    eng.wait_ge(h_transposed, 4 * t + q + 1)
                    src = ps[:, q, :].rearrange("p (j n) -> p j n", j=4)[:, :, 0:n]
                    copy(memT[:, 4 * q:4 * q + 4, t * P:t * P + n], src).then_inc(evac_a[parity], 1)
                return
            at = (t - MT) * P
            for q in range(4):
                src = ps[:, q, :].rearrange("p (j n) -> p j n", j=4)[:, :, 0:n]
                high = h16[:, 0, 4 * q:4 * q + 4, at:at + n]
                if parity == 0:
                    eng.wait_ge(h_transposed, 4 * t + q + 1)
                    copy(high, src).then_inc(high_made, 1)
                else:
                    eng.wait_ge(high_made, 4 * (t - MT) + q + 1)
                    nc.vector.tensor_tensor(h16[:, 1, 4 * q:4 * q + 4, at:at + n], src, high, ALU.subtract).then_inc(evac_a[q % 2], 1)

        @block.scalar
        def _(act):
            for t in range(ALL + 1):
                if t < ALL:
                    b, n = t % 2, rows(t)
                    act.wait_ge(x_loaded[b], 16 * (t // 2 + 1))
                    nc.scalar.activation(sq[0:n, :], x_in[0:n, b, :], ACT.Square,
                                         accum_out=stat[0:n, 0, t:t + 1]).then_inc(squares, 1)
                    act.wait_ge(mean_sq, t + 1)
                    nc.scalar.activation(rms[0:n, t:t + 1], stat[0:n, 1, t:t + 1], ACT.Sqrt).then_inc(root, 1)
                if t >= 1:
                    evac(act, nc.scalar.copy, 0, t - 1)
            for a in range(MT):
                act.wait_ge(kv_step, KT)
                src = ps[:, 4 + 2 * a:6 + 2 * a, :].rearrange("p a n -> p (a n)")
                nc.scalar.activation(kv_mem[:, a, :], src, ACT.Copy).then_inc(kv_evac, 1)
            act.wait_ge(kv_evac, MT)
            for n, name in enumerate(("out_mk", "out_mv")):
                dst = io[name][0, 0].rearrange("(a p) h d -> p a (h d)", p=P)
                act.dma_start(dst, kv_mem[:, :, n * D_MEM:(n + 1) * D_MEM]).then_inc(kv_stored, 16)

        @block.vector
        def _(dve):
            link = Link(dve, dve_link)
            dve_copy = nc.vector.tensor_copy
            for t in range(ALL + 1):
                if t < ALL:
                    b, n = t % 2, rows(t)
                    dve.wait_ge(squares, t + 1)
                    nc.vector.tensor_scalar(stat[0:n, 1, t:t + 1], stat[0:n, 0, t:t + 1], 1.0 / D_MODEL, EPS,
                                            ALU.mult, ALU.add).then_inc(mean_sq, 1)
                    dve.wait_ge(root, t + 1)
                    link(nc.vector.reciprocal(stat[0:n, 2, t:t + 1], rms[0:n, t:t + 1]))
                    if t == 0:
                        dve.wait_ge(g_loaded[0], 16)
                        dve.wait_ge(g_loaded[1], 16)
                        g = g_b[:, 1, :]
                        nc.vector.tensor_reduce(g_max[:, 0:1], g, AX_X, ALU.max)
                        link(nc.vector.tensor_reduce(g_max[:, 1:2], g, AX_X, ALU.min))
                        link(nc.vector.tensor_scalar(g_max[:, 1:2], g_max[:, 1:2], -1.0, TINY, ALU.mult, ALU.max))
                        link(nc.vector.tensor_tensor(g_max[:, 0:1], g_max[:, 0:1], g_max[:, 1:2], ALU.max))
                        link(nc.vector.tensor_scalar(h_unit[:], g_max[:, 0:1], 1.0 / ROOT_H, None, ALU.mult))
                        link(nc.vector.reciprocal(g_max[:, 1:2], h_unit[:]))
                        link(nc.vector.tensor_scalar(g, g, g_max[:, 1:2], None, ALU.mult))
                    if t >= 2:
                        dve.wait_ge(h_transposed, 4 * (t - 1))
                    nc.vector.scalar_tensor_tensor(out=h_tok[0:n, b, :], in0=x_in[0:n, b, :], scalar=stat[0:n, 2, t:t + 1],
                                                   in1=g_b[0:n, int(t >= MT), :], op0=ALU.mult, op1=ALU.mult).then_inc(h_ready, 1)
                if t >= 1:
                    evac(dve, dve_copy, 1, t - 1)
            dve.wait_ge(params_loaded, 10 * 16)
            dve_copy(lam_in[:, 2, :].rearrange("i (a n) -> i a n", a=2),
                     dt_in[:].unsqueeze(2).to_broadcast([TILES, 2, STATE])).then_inc(dt_spread, 1)
            dve.wait_ge(st_transposed, 1)
            dve_copy(lam[:], ps[:, 5, 0:3 * TILES].rearrange("p (a i) -> p a i", a=3)).then_inc(lam_ready, 1)
            dve_copy(dcol[:], ps[:, 5, 64:68])
            src = ps[:, 4, 0:2 * TILES * DEC_BATCH].rearrange("p (a b i) -> p a b i", a=2, i=TILES)
            dve_copy(h0[:], src)

        @block.tensor
        def _(pe):
            pe.wait_ge(ident_ready, 1)
            for t in range(ALL):
                b, n = t % 2, rows(t)
                pe.wait_ge(h_ready, t + 1)
                for q in range(4):
                    if t >= 1:
                        pe.wait_ge(evac_a[q % 2], 2 * (t - 1) + q // 2 + 1)
                    for j in range(4):
                        c = 4 * q + j
                        last = nc.tensor.transpose(ps[:, q, j * P:j * P + n], h_tok[0:n, b, c * P:(c + 1) * P],
                                                   ident[0:n, 0:n])
                    last.then_inc(h_transposed, 1)
                if t >= MT and 2 * (t - MT) < KT:
                    if t == MT:
                        for parity in range(2):
                            pe.wait_ge(evac_a[parity], 2 * MT)
                    for k in range(2 * (t - MT), 2 * (t - MT) + 2):
                        pe.wait_ge(w_kv_loaded[k % 4], 16 * (k // 4 + 1))
                        for a in range(MT):
                            for half in range(2):
                                last = nc.tensor.matmul(ps[:, 4 + 2 * a + half, :], memT[:, k, a * P:(a + 1) * P],
                                                        w_kv[:, k % 4, half * 512:(half + 1) * 512],
                                                        start=(k == 0), stop=(k == KT - 1))
                        last.then_inc(kv_step, 1)
            pe.wait_ge(params_loaded, 10 * 16)
            pe.wait_ge(kv_evac, MT)
            for a in range(2):
                last = nc.tensor.transpose(ps[:, 4, a * P:(a + 1) * P], st_in[:, a, :], ident[:])
            nc.tensor.transpose(ps[:, 5, 64:68], d_in[:], ident[0:4, 0:4])
            pe.wait_ge(dt_spread, 1)
            for a in range(3):
                last = nc.tensor.transpose(ps[:, 5, a * TILES:(a + 1) * TILES], lam_in[:, a, :], ident[0:TILES, 0:TILES])
            last.then_inc(st_transposed, 1)



def block_b(nc, io, v, sem, sb_in):
    ident, cmin, h16, h_unit, par, tabs, bbar = (v[n] for n in ("ident", "cmin", "h16", "h_unit", "par", "tabs", "bbar"))
    cnat, dcol, mask_c, mask_b, h0, ps = (v[n] for n in ("cnat", "dcol", "mask_c", "mask_b", "h0", "ps"))
    wis, score, qi_s, kiT, h_last, ones = (v[n] for n in ("wis", "score", "qi_s", "kiT", "h_last", "ones"))
    z_dram, y_dram = v["z_dram"], v["y_dram"]
    lam, bnat, pw = (v[n] for n in ("lam", "bnat", "pw"))
    own = ExitStack()
    with own:
        sb = lambda name, shape, dt=F32: sb_in(own, name, shape, dt)
        wb, w_loaded = v["wb"], v["w_loaded"]
        w16 = sb("w16", [P, 2, 2, KT, CHUNK], F16)
        absolute = sb("absolute", [P, 4, CHUNK], BF16)
        size = sb("size", [P, 2, 4])
        unit = sb("unit", [P, 4, 3])
        uT = sb("uT", [P, 4, TOK])
        room = sb("room", [P, 8 * TOK])
        qiT = room[:].rearrange("p (c n) -> p c n", c=8)
        at = 0

        def part(n):
            nonlocal at
            at += n
            return room[:, at - n:at]

        tab = part(2 * SEQ).rearrange("p (a n) -> p a n", a=2)
        g_ = part(2 * SEQ).rearrange("p (a n) -> p a n", a=2)
        h_ = part(2 * TOK).rearrange("p (a n) -> p a n", a=2)
        pt = part(SEQ)
        dt_ = part(512)
        xy = part(4 * P).rearrange("p (a n) -> p a n", a=4)
        xs = part(2 * NS).rearrange("p (a n) -> p a n", a=2)
        tt = score[:, 0:2 * TILES * LO].rearrange("p (s i a b) -> p s i a b", s=2, i=TILES, a=2)
        bt = score[:, 2 * TILES * LO:2 * TILES * (LO + GROUP)].rearrange("p (s i c) -> p s i c", s=2, i=TILES)
        w1 = score[:, 2048:2048 + 16 * TILES].rearrange("p (s i) -> p s i", i=TILES)
        ang = score[:, 2304:2304 + 60 * TILES].rearrange("p (s i k) -> p s i k", s=6, k=10)
        kw_f = sb("kw_f", [P, TOK])
        yacc = kw_f
        zst = sb("zst", [P, 2, TOK])
        rel = zst[:].rearrange("p a n -> p (a n)")[:, 0:2 * SEQ].rearrange("p (a n) -> p a n", a=2)
        stat = sb("stat_b", [P, 4, P])
        ki_out = uT[:, 0, 0:(QT + 1) * IDX_DIM].rearrange("p (t d) -> p t d", t=QT + 1)
        m8 = sb("m8", [P, 8])
        st_out = stat

        w_summed, w_sized, unit_ready, w_high, w_split, act_link = (
            sem(n) for n in ("w_summed", "w_sized", "unit_ready", "w_high", "w_split", "act_link"))
        z_ready = sem("z_ready")
        z_evac = sem("z_evac")
        z_stored = [sem(f"z_stored{b}") for b in range(2)]
        turned = sem("turned")
        dve_read = sem("dve_read")
        act_read = sem("act_read")
        index_mm = sem("index_mm")
        acc_done = sem("acc_done")
        pool_link = sem("pool_link_b")
        ang_ready = sem("ang_ready")
        sin_ready = sem("sin_ready")
        xy_ready = sem("xy_ready")
        x_mm = sem("x_mm")
        g_ready = sem("g_ready")
        h_rotated = sem("h_rotated")
        y_mm = sem("y_mm")
        y_done = sem("y_done")
        gelu_done = sem("gelu_done")
        y_stored = sem("y_stored")
        dve_link = sem("dve_link_b")
        loop_link = sem("loop_link")
        last_turned = sem("last_turned")
        last_copied = sem("last_copied")
        out_stored = sem("out_stored_b")

        chunks = CHUNKS
        KW_READS = 4
        HEADS = len(IDX_TILES) * N_IDX
        FIRST_U, FIRST_LOOP = 9, 13

        block = own.enter_context(nc.Block(name="project"))

        @block.sync
        def _(sp):
            for c in range(1, len(chunks)):
                if c >= 2:
                    sp.wait_ge(w_split, c - 1)
                load_chunk(sp, io, wb, w_loaded, c)
            for n, (name, who) in enumerate((("out_ssm_re_p", 0), ("out_ssm_im_p", 0), ("out_ssm_re_s", 1), ("out_ssm_im_s", 1))):
                sp.wait_ge(last_copied, n + 1)
                if who == 0:
                    dst = io[name][0, 0].rearrange("(i a) n -> i (a n)", a=2)
                    sp.dma_start(dst, st_out[0:TILES, n, :]).then_inc(out_stored, 16)
                else:
                    dst = io[name][0].rearrange("b (i a) n -> (b i) (a n)", a=2)
                    sp.dma_start(dst, st_out[:, n, :]).then_inc(out_stored, 16)
            sp.wait_ge(out_stored, 4 * 16)

        def group(pe, b, m, n, c):
            t0, w = PIECES[n]
            if n == 0:
                pe.wait_ge(w_split, c + 1)
            if not isinstance(c, int) or c >= 1:
                pe.wait_ge(z_evac, 3 * c + (n + 1 - 3))
            for k in range(KT):
                for i, (pw_, ph) in enumerate(((0, 0), (0, 1), (1, 0))):
                    last = nc.tensor.matmul(ps[0:m, n, 0:w], w16[:, b, pw_, k, 0:m], h16[:, ph, k, t0:t0 + w],
                                            start=(k == 0 and i == 0), stop=(k == KT - 1 and i == 2))
            last.then_inc(z_ready, 1)
            return last

        def sum_sizes(pe, c, b, out):
            pe.wait_ge(w_summed, 4 * c + 4)
            return nc.tensor.matmul(out, ones[:], size[:, b, :], start=True, stop=True)

        @block.tensor
        def _(pe):
            def chunk_before_loop(c, b, m):
                group(pe, b, m, 0, c)
                sum_sizes(pe, c + 1, 1 - b, ps[:, 7, 0:4]).then_inc(w_sized, 1)
                for n in (1, 2):
                    group(pe, b, m, n, c)

            sum_sizes(pe, 0, 0, ps[:, 7, 0:4]).then_inc(w_sized, 1)
            chunk_before_loop(0, 0, KIWI)
            with pe.Fori(0, 2) as it:
                for u in range(4):
                    chunk_before_loop(it * 4 + (1 + u), 1 - u % 2, P)
            pe.wait_ge(z_evac, 3)
            for t in range(QT + 1):
                n = P if t < QT else NS
                last = nc.tensor.transpose(ps[0:n, 3 + t // 5, (t % 5) * KIWI:(t % 5 + 1) * KIWI],
                                           kw_f[0:KIWI, t * P:t * P + n], ident[0:KIWI, 0:KIWI])
            last.then_inc(turned, 1)
            pe.wait_ge(dve_read, KW_READS)
            pe.wait_ge(z_evac, 27)
            for ti, t in enumerate(IDX_TILES):
                for h in range(N_IDX):
                    m = ti * N_IDX + h
                    bank = 3 + 2 * (m % 2)
                    if m >= 2:
                        pe.wait_ge(act_read, m - 1)
                    for x0 in range(0, (t + 1) * P, 512):
                        w = min(512, (t + 1) * P - x0)
                        last = nc.tensor.matmul(ps[:, bank + x0 // 512, 0:w], qiT[:, h // 2, t * P:(t + 1) * P],
                                                kiT[:, h % 2, x0:x0 + w], start=True, stop=True)
                    last.then_inc(index_mm, 1)
            for c in range(FIRST_U, FIRST_LOOP):
                chunk_before_loop(c, c % 2, P)
            pe.wait_ge(z_evac, 3 * FIRST_LOOP)
            with pe.Fori(0, LOOPS) as it:
                for x in range(4):
                    tile = it * 4 + x
                    chunk = it * 8 + (FIRST_LOOP + 2 * x)
                    pe.wait_ge(w_split, chunk + 1)
                    pe.wait_ge(xy_ready, tile + 1)
                    pe.wait_ge(act_read, tile + HEADS)
                    for a in range(4):
                        last = nc.tensor.transpose(ps[:, 3, a * P:(a + 1) * P], xy[:, a, :], ident[:])
                    last.then_inc(turned, 1)
                    group(pe, 1, P, 0, chunk)
                    pe.wait_ge(act_read, tile + HEADS + 1)
                    pe.wait_ge(dve_read, tile * 6 + KW_READS)
                    for n, (t0, w) in enumerate(STEPS):
                        for a in range(2):
                            out = ps[:, 4 + 2 * n + a, 0:w] if n < 2 else ps[:, 3, a * NS:(a + 1) * NS]
                            last = nc.tensor.matmul(out, stat[:, a, :], uT[:, bass.ds(it, 1), t0:t0 + w], start=True, stop=True)
                        if n == 2:
                            last = sum_sizes(pe, chunk + 1, 0, ps[:, 3, 2 * NS:2 * NS + 4])
                        last.then_inc(x_mm, 1)
                    group(pe, 1, P, 1, chunk)
                    group(pe, 1, P, 2, chunk)
                    group(pe, 0, P, 0, chunk + 1)
                    pe.wait_ge(dve_read, tile * 6 + (KW_READS + 1))
                    sum_sizes(pe, chunk + 2, 1, ps[:, 3, 0:4]).then_inc(w_sized, 1)
                    group(pe, 0, P, 1, chunk + 1)
                    group(pe, 0, P, 2, chunk + 1)
                    pe.wait_ge(h_rotated, tile + 1)
                    for n, (t0, w) in enumerate(STEPS):
                        for a in range(2):
                            last = nc.tensor.matmul(ps[:, (6, 7, 4)[n], 0:w], stat[:, 2 + a, :], h_[:, a, t0:t0 + w],
                                                    start=(a == 0), stop=(a == 1))
                        last.then_inc(y_mm, 1)
            pe.wait_ge(y_done, LOOPS)
            pe.wait_ge(dve_read, 6 * TILES + KW_READS)
            for n in range(2):
                nc.tensor.transpose(ps[0:TILES, 3, n * P:(n + 1) * P], h_last[:, n, 0, :], ident[:])
            for n in range(2):
                last = nc.tensor.transpose(ps[:, 5, n * P:(n + 1) * P],
                                           h_last[:, n, 1:1 + DEC_BATCH, :].rearrange("p b i -> p (b i)"), ident[:])
            last.then_inc(last_turned, 1)

        @block.scalar
        def _(act):
            def sum_absolutes(c, b, w=CHUNK):
                act.wait_ge(w_loaded[b], loads(c, b))
                for k in range(4):
                    if not isinstance(c, int) or c or k:
                        act.wait_ge(w_summed, 4 * c + k)
                    nc.scalar.activation(absolute[:, :, 0:w], wb[:, b, 4 * k:4 * k + 4, 0:w], ACT.Abs,
                                         accum_out=size[:, b, k:k + 1]).then_inc(w_summed, 1)

            def split_high(c, b, slot, w=CHUNK):
                act.wait_ge(unit_ready, c + 1)
                src, high = wb[:, b, :, 0:w], w16[:, b, 0, :, 0:w]
                nc.scalar.activation(src, src, ACT.Copy, scale=unit[:, slot, 1:2]).then_inc(act_link, 1)
                if not isinstance(c, int) or c >= 2:
                    act.wait_ge(z_ready, 3 * (c - 1))
                act.wait_ge(act_link, c + 1)
                nc.scalar.activation(high, src, ACT.Copy).then_inc(w_high, 1)

            def loads(c, b):
                return 16 * (c // 2 + 1) if isinstance(c, int) else c * 8 + (16 - 8 * b)

            def evac(c, n, outs, func=ACT.Copy, slot=None):
                slot = c % 4 if slot is None else slot
                t0, w = PIECES[n]
                act.wait_ge(z_ready, 3 * c + (n + 1))
                for rows, out in outs:
                    whole = out.shape[-1] == TOK
                    last = nc.scalar.activation(out[:, t0:t0 + w] if whole else out, ps[rows, n, 0 if whole else w - NS:w], func,
                                                scale=unit[rows, slot, 2:3])
                last.then_inc(z_evac, 1)

            sum_absolutes(0, 0, KIWI)
            split_high(0, 0, 0, KIWI)
            sum_absolutes(1, 1)
            for n in range(3):
                if n == 1:
                    split_high(1, 1, 1)
                evac(0, n, [(slice(0, KIWI), kw_f[0:KIWI, :]), (slice(0, IDX_DIM), kiT[0:IDX_DIM, 0, :]),
                            (slice(0, IDX_DIM), kiT[IDX_DIM:P, 1, :])])
            act.wait_ge(ang_ready, 1)
            nc.scalar.activation(ang[:, 2, :, :], ang[:, 0, :, :], ACT.Sin).then_inc(sin_ready, 1)
            nc.scalar.activation(ang[:, 3, :, :], ang[:, 1, :, :], ACT.Sin).then_inc(sin_ready, 1)
            for c in range(8):
                sum_absolutes(c + 2, c % 2)
                for n in range(3):
                    if n == 1:
                        split_high(c + 2, c % 2, (c + 2) % 4)
                    evac(1 + c, n, [(slice(0, P), qiT[:, c, :])] + ([(slice(0, P), qi_s[:, c, :])] if n == 2 else []))
            act.wait_ge(dve_read, KW_READS)
            act.dma_start(io["out_kidx_p"][0, 0].rearrange("(t p) d -> p t d", p=P), ki_out[:, 0:QT, :]).then_inc(z_stored[0], 16)
            act.dma_start(io["out_kidx_s"][0].rearrange("b s d -> (b s) d"), ki_out[0:NS, QT, :]).then_inc(z_stored[1], 16)
            for ti, t in enumerate(IDX_TILES):
                for h in range(N_IDX):
                    m = ti * N_IDX + h
                    act.wait_ge(index_mm, m + 1)
                    if m >= 2:
                        act.wait_ge(acc_done, m - 1)
                    src = ps[:, 3 + 2 * (m % 2):5 + 2 * (m % 2), :].rearrange("p a n -> p (a n)")[:, 0:(t + 1) * P]
                    nc.scalar.activation(rel[:, m % 2, 0:(t + 1) * P], src, ACT.Relu, scale=IDX_DIM ** -0.5).then_inc(act_read, 1)
            for b in range(2):
                act.wait_ge(z_stored[b], 16)
            for c in range(4):
                after = FIRST_U + c + 1
                sum_absolutes(after, after % 2)
                for n in range(3):
                    if n == 1:
                        split_high(after, after % 2, after % 4)
                    evac(FIRST_U + c, n, [(slice(0, P), uT[:, c, :])])
            act.wait_ge(acc_done, HEADS)
            with act.Fori(0, LOOPS) as it:
                for x in range(4):
                    act.wait_ge(turned, it * 4 + (x + 2))
                    nc.scalar.activation(stat[:], ps[:, 3, :].rearrange("p (a n) -> p a n", a=4), ACT.Copy).then_inc(act_read, 1)
                    for sub in range(2):
                        act.wait_ge(z_stored[sub], it * 64 + 16 * (x + 1))
                        c = it * 8 + (FIRST_LOOP + 2 * x + sub)
                        k = FIRST_LOOP + 2 * x + sub
                        sum_absolutes(c + 1, (k + 1) % 2)
                        for n in range(3):
                            if n == 1:
                                split_high(c + 1, (k + 1) % 2, (k + 1) % 4)
                            evac(c, n, [(slice(0, P), zst[:, sub, :])], ACT.Silu if x % 2 else ACT.Copy, k % 4)
                        act.wait_ge(z_evac, 3 * c + 3)
                        act.dma_start(z_dram[bass.ds(it * 8 + (2 * x + sub), 1)].rearrange("a p n -> (a p) n"), zst[:, sub, :]).then_inc(z_stored[sub], 16)
                act.wait_ge(y_done, it + 1)
                nc.scalar.activation(yacc[:], yacc[:], ACT.Gelu_apprx_tanh).then_inc(gelu_done, 1)
                act.wait_ge(gelu_done, it + 1)
                act.dma_start(y_dram[bass.ds(it, 1)].rearrange("a p n -> (a p) n"), yacc[:]).then_inc(y_stored, 16)
                act.wait_ge(y_stored, it * 16 + 16)
            for b in range(2):
                act.wait_ge(z_stored[b], 16 * (1 + len(LOOP_SLABS)))

        @block.gpsimd
        def _(pool):
            def split_low(c, b, w=CHUNK):
                pool.wait_ge(w_high, c + 1)
                nc.gpsimd.tensor_tensor(w16[:, b, 1, :, 0:w], wb[:, b, :, 0:w], w16[:, b, 0, :, 0:w], ALU.subtract).then_inc(w_split, 1)

            split_low(0, 0, KIWI)
            for c in range(1, FIRST_LOOP + 1):
                split_low(c, c % 2)
            pool.wait_ge(act_read, HEADS)
            TT = nc.gpsimd.tensor_tensor
            PER_TILE = 5
            with pool.Fori(0, LOOPS) as it:
                for x in range(4):
                    tile = it * 4 + x
                    base = it * (4 * PER_TILE) + x * PER_TILE
                    pool.wait_ge(turned, tile + 1)
                    mb = mask_b[:, x, :].unsqueeze(2).to_broadcast([P, 8, GROUP])
                    for a in range(2):
                        src = bbar[:, a, bass.ds(tile, 1), :].to_broadcast([P, 8, GROUP])
                        TT(xy[:, a, :].rearrange("p (g c) -> p g c", g=8), src, mb, ALU.mult)
                    mc = mask_c[:, 2 * x:2 * x + 2].unsqueeze(2).to_broadcast([P, 2, STATE])
                    for a in range(2):
                        src = cnat[:, a, bass.ds(it, 1), :].to_broadcast([P, 2, STATE])
                        last = TT(xy[:, 2 + a, :].rearrange("p (a n) -> p a n", a=2), src, mc, ALU.mult)
                    last.then_inc(xy_ready, 1)
                    split_low(it * 8 + (FIRST_LOOP + 2 * x + 1), 0)
                    pool.wait_ge(g_ready, tile + 1)
                    c_, s_ = tab[:, 0, :], tab[:, 1, :]
                    hr, hi = h_[:, 0, 0:SEQ], h_[:, 1, 0:SEQ]
                    TT(hr, g_[:, 0, :], c_, ALU.mult).then_inc(pool_link, 1)
                    TT(pt, g_[:, 1, :], s_, ALU.mult).then_inc(pool_link, 1)
                    pool.wait_ge(pool_link, base + 2)
                    TT(hr, hr, pt, ALU.subtract).then_inc(pool_link, 1)
                    TT(hi, g_[:, 0, :], s_, ALU.mult).then_inc(pool_link, 1)
                    pool.wait_ge(pool_link, base + 4)
                    TT(pt, g_[:, 1, :], c_, ALU.mult).then_inc(pool_link, 1)
                    pool.wait_ge(pool_link, base + 5)
                    TT(hi, hi, pt, ALU.add).then_inc(h_rotated, 1)
                    split_low(it * 8 + (FIRST_LOOP + 2 * x + 2), 1)

        @block.vector
        def _(dve):
            link = Link(dve, dve_link)
            TSC, TT, STT = nc.vector.tensor_scalar, nc.vector.tensor_tensor, nc.vector.scalar_tensor_tensor
            copy = nc.vector.tensor_copy

            def set_unit(link, src, slot):
                u = [unit[:, slot, i:i + 1] for i in range(3)]
                link(nc.vector.tensor_reduce(u[0], src, AX_X, ALU.add))
                link(TSC(u[0], u[0], W_SHIFT, TINY, ALU.mult, ALU.max))
                nc.vector.reciprocal(u[1], u[0])
                TT(u[2], u[0], h_unit[:], ALU.mult).then_inc(unit_ready, 1)

            def early_unit(c):
                dve.wait_ge(w_sized, c + 1)
                set_unit(link, ps[:, 7, 0:4], c % 4)

            early_unit(0)
            dve.wait_ge(v["kv_stored"], 32)
            lr, li = lam[:, 0, :], lam[:, 1, :]
            dt, lrd, th, k_, r_ = (w1[:, i, :] for i in range(5))

            def exponential(out, x, y):
                link(TSC(y, x, 1 / 16, None, ALU.mult))
                link(TSC(out, y, 1 / math.factorial(9), None, ALU.mult))
                for n in range(8, 0, -1):
                    link(STT(out=out, in0=out, scalar=1 / math.factorial(n), in1=y, op0=ALU.add, op1=ALU.mult))
                link(TSC(out, out, 1.0, None, ALU.add))
                for _ in range(4):
                    link(TT(out, out, out, ALU.mult))

            exponential(dt, lam[:, 2, :], k_)
            link(TT(lrd, lr, dt, ALU.mult))
            exponential(par[:, 0, :], lrd, k_)
            early_unit(1)
            link(TT(th, li, dt, ALU.mult))

            def reduce_angle(out, x, k):
                link(TSC(k, x, 1.0 / TWO_PI, MAGIC, ALU.mult, ALU.add))
                link(TSC(k, k, MAGIC, None, ALU.subtract))
                link(STT(out=out, in0=k, scalar=-PI_A, in1=x, op0=ALU.mult, op1=ALU.add))
                link(STT(out=out, in0=k, scalar=-PI_B, in1=out, op0=ALU.mult, op1=ALU.add))
                link(STT(out=out, in0=k, scalar=-PI_C, in1=out, op0=ALU.mult, op1=ALU.add))
                link(TSC(out, out, PI_IN, -PI_IN, ALU.min, ALU.max))

            reduce_angle(r_, th, k_)
            link(TT(ang[:, 4, :, :], r_.unsqueeze(2).to_broadcast([P, TILES, 10]),
                    pw[:].unsqueeze(1).to_broadcast([P, TILES, 10]), ALU.mult))
            reduce_angle(ang[:, 0, :, :], ang[:, 4, :, :], ang[:, 5, :, :])
            link(STT(out=ang[:, 1, :, :], in0=ang[:, 0, :, :], scalar=-1.0, in1=ang[:, 0, :, :],
                     op0=ALU.mult, op1=ALU.max))
            TSC(ang[:, 1, :, :], ang[:, 1, :, :], -1.0, np.pi / 2, ALU.mult, ALU.add).then_inc(ang_ready, 1)
            early_unit(2)
            dve.wait_ge(sin_ready, 2)
            sin_p, cos_p = ang[:, 2, :, :], ang[:, 3, :, :]
            mag, ar, ai, nai = (par[:, i, :] for i in range(4))
            link(TT(ar, mag, cos_p[:, :, 0], ALU.mult))
            link(TT(ai, mag, sin_p[:, :, 0], ALU.mult))
            link(TSC(nai, ai, -1.0, None, ALU.mult))
            den, am1, t1, t2, cr, ci = (w1[:, i, :] for i in range(5, 11))
            link(TT(t1, lr, lr, ALU.mult))
            link(TT(t2, li, li, ALU.mult))
            link(TT(den, t1, t2, ALU.add))
            link(nc.vector.reciprocal(den, den))
            link(TSC(am1, ar, -1.0, None, ALU.add))
            link(TT(t1, lr, am1, ALU.mult))
            link(TT(t2, li, ai, ALU.mult))
            link(TT(cr, t1, t2, ALU.add))
            link(TT(cr, cr, den, ALU.mult))
            link(TT(t1, lr, ai, ALU.mult))
            link(TT(t2, li, am1, ALU.mult))
            link(TT(ci, t1, t2, ALU.subtract))
            link(TT(ci, ci, den, ALU.mult))
            crb = cr.unsqueeze(2).to_broadcast([P, TILES, GROUP])
            cib = ci.unsqueeze(2).to_broadcast([P, TILES, GROUP])
            link(TT(bbar[:, 0, :, :], bnat[:, 0, :, :], crb, ALU.mult))
            link(TT(bt[:, 0, :, :], bnat[:, 1, :, :], cib, ALU.mult))
            link(TT(bbar[:, 0, :, :], bbar[:, 0, :, :], bt[:, 0, :, :], ALU.subtract))
            link(TT(bbar[:, 1, :, :], bnat[:, 1, :, :], crb, ALU.mult))
            link(TT(bt[:, 1, :, :], bnat[:, 0, :, :], cib, ALU.mult))
            link(TT(bbar[:, 1, :, :], bbar[:, 1, :, :], bt[:, 1, :, :], ALU.add))
            link(TSC(cnat[:, 1, :, :], cnat[:, 1, :, :], -1.0, None, ALU.mult))
            link(nc.vector.memset(tabs[:, 0, :, :, 0:1], 1.0))
            link(nc.vector.memset(tabs[:, 1, :, :, 0:1], 0.0))
            for lev in range(5):
                d = 1 << lev
                shape = [P, TILES, 2, d]
                pc = cos_p.rearrange("p i (a k) -> p i a k", a=2)[:, :, :, lev:lev + 1].to_broadcast(shape)
                psn = sin_p.rearrange("p i (a k) -> p i a k", a=2)[:, :, :, lev:lev + 1].to_broadcast(shape)
                c_, s_ = tabs[:, 0, :, :, 0:d], tabs[:, 1, :, :, 0:d]
                co, so = tabs[:, 0, :, :, d:2 * d], tabs[:, 1, :, :, d:2 * d]
                u1, u2 = tt[:, 0, :, :, 0:d], tt[:, 1, :, :, 0:d]
                link(TT(co, c_, pc, ALU.mult))
                link(TT(u1, s_, psn, ALU.mult))
                link(TT(co, co, u1, ALU.subtract))
                link(TT(so, s_, pc, ALU.mult))
                link(TT(u2, c_, psn, ALU.mult))
                link(TT(so, so, u2, ALU.add))
            for c in range(3, FIRST_U + 1):
                early_unit(c)
            dve.wait_ge(turned, 1)
            first = ps[:, 3, 0:5 * KIWI].rearrange("p (t c) -> p t c", t=5)
            copy(ki_out[:, 0:5, :], first[:, :, 0:IDX_DIM]).then_inc(dve_read, 1)
            TSC(wis[:, 0:5, :], first[:, :, IDX_DIM:KIWI], N_IDX ** -0.5, None, ALU.mult)
            second = ps[:, 4, 0:3 * KIWI].rearrange("p (t c) -> p t c", t=3)
            copy(ki_out[:, 5:8, :], second[:, :, 0:IDX_DIM]).then_inc(dve_read, 1)
            TSC(wis[:, 5:8, :], second[:, :, IDX_DIM:KIWI], N_IDX ** -0.5, None, ALU.mult)
            third = ps[0:NS, 4, 3 * KIWI:4 * KIWI]
            copy(ki_out[0:NS, 8, :], third[:, 0:IDX_DIM]).then_inc(dve_read, 1)
            TSC(wis[0:NS, 8, :], third[:, IDX_DIM:KIWI], N_IDX ** -0.5, None, ALU.mult).then_inc(dve_read, 1)
            dve.wait_ge(dve_read, KW_READS)
            for ti, t in enumerate(IDX_TILES):
                sc = score[:, IDX_OFF[t]:IDX_OFF[t] + (t + 1) * P]
                for h in range(N_IDX):
                    m = ti * N_IDX + h
                    dve.wait_ge(act_read, m + 1)
                    wi = wis[:, t, h:h + 1]
                    r = rel[:, m % 2, 0:(t + 1) * P]
                    if h == 0:
                        TSC(sc, r, wi, None, ALU.mult).then_inc(acc_done, 1)
                    else:
                        dve.wait_ge(acc_done, m)
                        STT(out=sc, in0=r, scalar=wi, in1=sc, op0=ALU.mult, op1=ALU.add).then_inc(acc_done, 1)
                dve.wait_ge(acc_done, (ti + 1) * N_IDX)
                diag = sc[:, t * P:(t + 1) * P]
                link(TT(diag, diag, cmin[:], ALU.min))
            for c in range(FIRST_U + 1, FIRST_LOOP + 1):
                early_unit(c)

            with dve.Fori(0, LOOPS) as it:
                dve.sem_clear(loop_link)
                link = Link(dve, loop_link)

                def keep_eight(t):
                    sc = score[:, IDX_OFF[t]:IDX_OFF[t] + (t + 1) * P]
                    link(nc.vector.max(out=m8[:], in_=sc))
                    link(nc.vector.match_replace(out=sc, in_to_replace=m8[:], in_values=sc, imm_value=REPLACED))

                each = ROUNDS // LOOPS
                plan = {0: [7] * each, 1: [6] * each, 2: [5, 2] * each, 3: [4, 3] * each}
                for x in range(4):
                    tile = it * 4 + x
                    rounds = plan[x]
                    view = lambda a: tab[:, a, :].rearrange("p (a b) -> p a b", a=LO)
                    shape = [P, LO, LO]
                    low = lambda a: tabs[:, a, bass.ds(tile, 1), 0, :].to_broadcast(shape)
                    high = lambda a: tabs[:, a, bass.ds(tile, 1), 1, :].rearrange("p i a -> p a i").to_broadcast(shape)
                    g2 = g_[:, 0, :].rearrange("p (a b) -> p a b", a=LO)
                    g3 = g_[:, 1, :].rearrange("p (a b) -> p a b", a=LO)
                    TT(view(0), high(0), low(0), ALU.mult)
                    TT(g2, high(1), low(1), ALU.mult)
                    TT(view(1), high(0), low(1), ALU.mult)
                    link(TT(g3, high(1), low(0), ALU.mult))
                    TT(view(0), view(0), g2, ALU.subtract)
                    link(TT(view(1), view(1), g3, ALU.add))
                    early, later = len(rounds) // 4, 5 * len(rounds) // 8
                    for t in rounds[:early]:
                        keep_eight(t)
                    dve.wait_ge(x_mm, it * 12 + (3 * x + 3))
                    set_unit(link, ps[:, 3, 2 * NS:2 * NS + 4], (FIRST_LOOP + 2 * x + 1) % 4)
                    copy(xs, ps[:, 3, 0:2 * NS].rearrange("p (a n) -> p a n", a=2)).then_inc(dve_read, 1)
                    for n in range(2):
                        sl = slice(512 * n, 512 * n + 512)
                        xr, xi = ps[:, 4 + 2 * n, :], ps[:, 5 + 2 * n, :]
                        gr, gi = g_[:, 0, sl], g_[:, 1, sl]
                        c_, s_ = tab[:, 0, sl], tab[:, 1, sl]
                        TT(gr, xr, c_, ALU.mult)
                        link(TT(dt_, xi, s_, ALU.mult))
                        TT(gr, gr, dt_, ALU.add)
                        link(TT(gi, xi, c_, ALU.mult))
                        TT(dt_, xr, s_, ALU.mult).then_inc(dve_read, 1)
                        dve.wait_ge(dve_read, it * 24 + (KW_READS + 6 * x + n + 2))
                        link(TT(gi, gi, dt_, ALU.subtract))
                    ar, ai, nai = (par[:, k, bass.ds(tile, 1)] for k in (1, 2, 3))
                    for q in range(DEC_SEQ):
                        if q == 0:
                            pr, pi = (h0[:, a, :, bass.ds(tile, 1)].rearrange("p b i -> p (b i)") for a in range(2))
                        else:
                            pr, pi = (h_[:, a, SEQ + q - 1:TOK:DEC_SEQ] for a in range(2))
                        xr, xi = (xs[:, a, q:NS:DEC_SEQ] for a in range(2))
                        nr, ni = (h_[:, a, SEQ + q:TOK:DEC_SEQ] for a in range(2))
                        STT(out=nr, in0=pr, scalar=ar, in1=xr, op0=ALU.mult, op1=ALU.add)
                        link(STT(out=ni, in0=pi, scalar=ar, in1=xi, op0=ALU.mult, op1=ALU.add))
                        STT(out=nr, in0=pi, scalar=nai, in1=nr, op0=ALU.mult, op1=ALU.add)
                        link(STT(out=ni, in0=pr, scalar=ai, in1=ni, op0=ALU.mult, op1=ALU.add))
                    mag = par[:, 0, bass.ds(tile, 1)].to_broadcast([P, SEQ])
                    for a in range(2):
                        last = nc.vector.tensor_tensor_scan(out=g_[:, a, :], data0=mag, data1=g_[:, a, :], initial=0.0,
                                                            op0=ALU.mult, op1=ALU.add)
                        last.then_inc(g_ready, 1) if a == 1 else link(last)
                    for t in rounds[early:later]:
                        keep_eight(t)
                    dve.wait_ge(w_sized, it * 4 + (FIRST_LOOP + 2 + x))
                    set_unit(link, ps[:, 3, 0:4], (FIRST_LOOP + 2 * x + 2) % 4)
                    for t in rounds[later:]:
                        keep_eight(t)
                    for n, (t0, w) in enumerate(STEPS):
                        dve.wait_ge(y_mm, it * 12 + (3 * x + n + 1))
                        y, src = yacc[:, t0:t0 + w], ps[:, (6, 7, 4)[n], 0:w]
                        if x == 0:
                            last = STT(out=y, in0=uT[:, bass.ds(it, 1), t0:t0 + w].rearrange("p a n -> p (a n)"),
                                       scalar=dcol[:, bass.ds(it, 1)], in1=src, op0=ALU.mult, op1=ALU.add)
                        else:
                            last = TT(y, y, src, ALU.add)
                        last.then_inc(dve_read, 1)
                    dve.wait_ge(dve_read, it * 24 + (KW_READS + 6 * x + 6))
                    for a in range(2):
                        last = copy(h_last[:, a, :, bass.ds(tile, 1)].rearrange("p b i -> p (b i)"), h_[:, a, SEQ - 1:TOK:DEC_SEQ])
                    if x == 3:
                        last.then_inc(y_done, 1)
            dve.wait_ge(last_turned, 1)
            for n in range(2):
                copy(st_out[0:TILES, n, :], ps[0:TILES, 3, n * P:(n + 1) * P]).then_inc(last_copied, 1)
            for n in range(2):
                copy(st_out[:, 2 + n, :], ps[:, 5, n * P:(n + 1) * P]).then_inc(last_copied, 1)


def block_c(nc, io, v, sem, sb_in):
    ident, ps, z_dram, y_dram, mixT, kT, kv_tok = (v[n] for n in ("ident", "ps", "z_dram", "y_dram", "mixT", "kT", "kv_tok"))
    own = ExitStack()
    with own:
        sb = lambda name, shape: sb_in(own, name, shape)
        w_glu = sb("w_glu_sb", [P, 4, 2 * D_SSM])
        yT = sb("yT", [P, 4, TOK])
        vT = v["v_or_q"][:].rearrange("p (g n) -> p g n", g=N_KV)
        q_t, kmq, q_loaded = v["v_or_q"], v["kmq"], v["q_loaded"]
        qmT = sb("qmT", [P, 4, TOK])
        sg = sb("sg", [P, 2, 512])
        ag = sb("ag", [P, 512])
        mem_kv = sb("mem_kv", [P, 2, 2, D_MEM])
        mkT = yT[:, 0, 0:4 * N_MEM].rearrange("p (h n) -> p h n", h=4)
        pm = w_glu[:, 0:2, :].rearrange("p b (h n) -> p b h n", h=4)
        pmT = w_glu[:, 2:4, :].rearrange("p b (k h n) -> p b k h n", k=2, h=4)
        nmx = sb("nmx_c", [P, QT, 4])
        nb = sb("nb_c", [P, QT, 4])
        rs = sb("rs_c", [P, QT, 4])
        rinv = sb("rinv_c", [P, QT, 4])

        glu_loaded, kv_loaded, mem_loaded, gate_s_loaded, gate_m_loaded, gate_a_loaded = (
            sem(n) for n in ("glu_loaded", "kv_loaded", "mem_loaded", "gate_s_loaded", "gate_m_loaded", "gate_a_loaded"))
        glu_rest = sem("glu_rest")
        glu_mm, glu_sig, glu_used = sem("glu_mm"), sem("glu_sig"), sem("glu_used")
        kv_turned, kv_copied, kv_stored = sem("kv_turned"), sem("kv_copied"), sem("kv_stored_c")
        mk_turned, mk_copied = sem("mk_turned"), sem("mk_copied")
        s_mm, nb_ready, exp_done, p_ready = sem("s_mm_c"), sem("nb_ready_c"), sem("exp_done_c"), sem("p_ready_c")
        p_turned, p_copied = sem("p_turned_c"), [sem(f"p_copied_c{k}") for k in range(2)]
        o_mm, o_used, dve_link = sem("o_mm_c"), sem("o_used_c"), sem("dve_link_c")
        SCALE = HEAD_DIM ** -0.5
        GLU = [(c, n) for c in range(4) for n in range(3)]

        def pair(col):
            return z_dram[stored(col):stored(col) + 2].rearrange("c p n -> p c n")

        block = own.enter_context(nc.Block(name="mix_a"))

        @block.sync
        def _(sp):
            w_rows = io["w_glu"][0].rearrange("(k p) n -> p k n", p=P)
            sp.dma_start(yT[:], y_dram.rearrange("c p n -> p c n")).then_inc(glu_loaded, 16)
            for a in range(2):
                sp.dma_start(w_glu[:, :, a * D_SSM:a * D_SSM + P], w_rows[:, :, a * D_SSM:a * D_SSM + P]).then_inc(glu_loaded, 16)
            for a in range(2):
                rest = slice(a * D_SSM + P, (a + 1) * D_SSM)
                sp.dma_start(w_glu[:, :, rest], w_rows[:, :, rest]).then_inc(glu_rest, 16)
            for s in range(2):
                sp.dma_start(mixT[:, 8 + 2 * s:10 + 2 * s, :], pair(OFF_GS + SLAB * s)).then_inc(gate_s_loaded, 16)
            sp.dma_start(kT[:], pair(OFF_K)).then_inc(kv_loaded, 16)
            sp.dma_start(vT[:], pair(OFF_V)).then_inc(kv_loaded, 16)
            for n, name in enumerate(("out_mk", "out_mv")):
                src = io[name][0, 0].rearrange("(a p) h d -> p a (h d)", p=P)
                sp.dma_start(mem_kv[:, n, :, :], src).then_inc(mem_loaded, 16)
            for s in range(2):
                sp.dma_start(qmT[:, 2 * s:2 * s + 2, :], pair(OFF_QM + SLAB * s)).then_inc(mem_loaded, 16)
            for s in range(2):
                sp.dma_start(mixT[:, 12 + 2 * s:14 + 2 * s, :], pair(OFF_GM + SLAB * s)).then_inc(gate_m_loaded, 16)
            for s in range(4):
                sp.dma_start(mixT[:, 2 * s:2 * s + 2, :], pair(OFF_GA + SLAB * s)).then_inc(gate_a_loaded, 16)
            sp.wait_ge(gate_a_loaded, 64)
            sp.wait_ge(kv_copied, QT + 1)
            for t in range(2):
                load_queries(sp, queries(q_t), z_dram, t, q_loaded)
            for n, name in enumerate(("out_k", "out_v")):
                part = slice(n * 256, n * 256 + 256)
                dst = io[name + "_p"][0, 0].rearrange("(t p) h d -> p t (h d)", p=P)
                sp.dma_start(dst, kv_tok[:, 0:QT, part]).then_inc(kv_stored, 16)
                dst = io[name + "_s"][0].rearrange("b s h d -> (b s) (h d)")
                sp.dma_start(dst, kv_tok[0:NS, QT, part]).then_inc(kv_stored, 16)
            sp.wait_ge(kv_stored, 64)

        @block.gpsimd
        def _(pool):
            link = Link(pool, v["pool_link"])
            link(nc.gpsimd.iota(kmq[:], pattern=[[1, SEQ]], base=-(SEQ - P), channel_multiplier=-1,
                                allow_small_or_imprecise_dtypes=True))
            link(nc.gpsimd.affine_select(out=kmq[:], in_=kmq[:], compare_op=ALU.is_ge, fill=FAR, base=SEQ - P,
                                         pattern=[[-1, SEQ]], channel_multiplier=1))

            pool.wait_ge(kv_turned, QT + 1)
            for g in range(N_KV):
                link(nc.gpsimd.tensor_scalar(kT[:, g, 0:SEQ], kT[:, g, 0:SEQ], SCALE, None, ALU.mult))

        @block.tensor
        def _(pe):
            pe.wait_ge(glu_loaded, 48)
            for i, (c, n) in enumerate(GLU):
                t0, w = PIECES[n]
                if (c, n) == (1, 0):
                    pe.wait_ge(glu_rest, 32)
                if i >= 2:
                    pe.wait_ge(glu_used, i - 1)
                for a in range(2):
                    for k in range(4):
                        last = nc.tensor.matmul(ps[:, 2 * (i % 2) + a, 0:w], w_glu[:, k, a * D_SSM + c * P:a * D_SSM + (c + 1) * P],
                                                yT[:, k, t0:t0 + w], start=(k == 0), stop=(k == 3))
                last.then_inc(glu_mm, 1)
            pe.wait_ge(kv_loaded, 32)
            for t in range(QT + 1):
                n = P if t < QT else NS
                if t >= 2:
                    pe.wait_ge(kv_copied, t - 1)
                for a, src in enumerate((kT, kT, vT, vT)):
                    last = nc.tensor.transpose(ps[0:n, 4 + t % 2, a * P:(a + 1) * P], src[:, a % 2, t * P:t * P + n], ident[:])
                last.then_inc(kv_turned, 1)
            pe.wait_ge(mem_loaded, 64)
            for h in range(N_MEM_HEADS):
                for k in range(2):
                    last = nc.tensor.transpose(ps[:, 6 + h // 2, (2 * (h % 2) + k) * P:(2 * (h % 2) + k + 1) * P],
                                               mem_kv[:, 0, k, h * P:(h + 1) * P], ident[:])
            last.then_inc(mk_turned, 1)
            pe.wait_ge(mk_copied, 1)
            pe.wait_ge(glu_used, len(GLU))
            pe.wait_ge(kv_copied, QT + 1)
            for s in range(QT + 2):
                if s < QT:
                    if s >= 2:
                        pe.wait_ge(exp_done, 4 * (s - 1))
                    for h in range(N_MEM_HEADS):
                        last = nc.tensor.matmul(ps[:, 2 * (s % 2) + h // 2, (h % 2) * N_MEM:(h % 2 + 1) * N_MEM],
                                                qmT[:, h, s * P:(s + 1) * P], mkT[:, h, :], start=True, stop=True)
                    last.then_inc(s_mm, 1)
                if s >= 2:
                    u = s - 2
                    for k in range(2):
                        pe.wait_ge(p_copied[k], u + 1)
                    if u >= 2:
                        pe.wait_ge(o_used, u - 1)
                    for h in range(N_MEM_HEADS):
                        for k in range(2):
                            last = nc.tensor.matmul(ps[:, 6 + u % 2, h * P:(h + 1) * P], mem_kv[:, 1, k, h * P:(h + 1) * P],
                                                    pmT[:, u % 2, k, h, :], start=(k == 0), stop=(k == 1))
                    last.then_inc(o_mm, 1)
                if 1 <= s <= QT:
                    u = s - 1
                    pe.wait_ge(p_ready, u + 1)
                    for k in range(2):
                        if u >= 1:
                            pe.wait_ge(p_copied[k], u)
                        for h in range(N_MEM_HEADS):
                            last = nc.tensor.transpose(ps[:, 4 + k, h * P:(h + 1) * P], pm[:, u % 2, h, k * P:(k + 1) * P], ident[:])
                        last.then_inc(p_turned, 1)

        @block.scalar
        def _(act):
            for i, (c, n) in enumerate(GLU):
                w = PIECES[n][1]
                act.wait_ge(glu_mm, i + 1)
                if i >= 2:
                    act.wait_ge(glu_used, i - 1)
                nc.scalar.activation(sg[:, i % 2, 0:w], ps[:, 2 * (i % 2) + 1, 0:w], ACT.Sigmoid).then_inc(glu_sig, 1)
            for t in range(QT + 1):
                n = P if t < QT else NS
                act.wait_ge(kv_turned, t + 1)
                nc.scalar.activation(kv_tok[0:n, t, :], ps[0:n, 4 + t % 2, :], ACT.Copy).then_inc(kv_copied, 1)
            act.wait_ge(mk_turned, 1)
            nc.scalar.activation(yT[:, 0, 0:4 * N_MEM], ps[:, 6:8, :].rearrange("p a n -> p (a n)"), ACT.Copy).then_inc(mk_copied, 1)
            for s in range(QT + 1):
                if s < QT:
                    act.wait_ge(nb_ready, s + 1)
                    if s >= 2:
                        act.wait_ge(p_turned, 2 * (s - 1))
                    for h in range(N_MEM_HEADS):
                        nc.scalar.activation(pm[:, s % 2, h, :], ps[:, 2 * (s % 2) + h // 2, (h % 2) * N_MEM:(h % 2 + 1) * N_MEM],
                                             ACT.Exp, bias=nb[:, s, h:h + 1], scale=SCALE, accum_out=rs[:, s, h:h + 1]).then_inc(exp_done, 1)
                if s >= 1:
                    u = s - 1
                    act.wait_ge(p_turned, 2 * u + 1)
                    if u >= 2:
                        act.wait_ge(o_mm, u - 1)
                    nc.scalar.activation(pmT[:, u % 2, 0, :, :].rearrange("p h n -> p (h n)"), ps[:, 4, :], ACT.Copy).then_inc(p_copied[0], 1)

        @block.vector
        def _(dve):
            link = Link(dve, dve_link)
            TSC, TT = nc.vector.tensor_scalar, nc.vector.tensor_tensor
            dve.wait_ge(gate_s_loaded, 32)
            for i, (c, n) in enumerate(GLU):
                t0, w = PIECES[n]
                dve.wait_ge(glu_sig, i + 1)
                TT(ag[:, 0:w], ps[:, 2 * (i % 2), 0:w], sg[:, i % 2, 0:w], ALU.mult).then_inc(glu_used, 1)
                dve.wait_ge(glu_used, i + 1)
                o = mixT[:, 8 + c, t0:t0 + w]
                link(TT(o, o, ag[:, 0:w], ALU.mult))
            dve.wait_ge(gate_m_loaded, 32)
            for s in range(QT + 2):
                if s < QT:
                    dve.wait_ge(s_mm, s + 1)
                    src = ps[:, 2 * (s % 2):2 * (s % 2) + 2, :].rearrange("p a (h n) -> p (a h) n", h=2)
                    link(nc.vector.tensor_reduce(nmx[:, s, :], src, AX_X, ALU.max, negate=True))
                    TSC(nb[:, s, :], nmx[:, s, :], SCALE, None, ALU.mult).then_inc(nb_ready, 1)
                if 1 <= s <= QT:
                    u = s - 1
                    dve.wait_ge(exp_done, 4 * (u + 1))
                    link(nc.vector.reciprocal(rinv[:, u, :], rs[:, u, :]))
                    TT(pm[:, u % 2, :, :], pm[:, u % 2, :, :], rinv[:, u, :].unsqueeze(2).to_broadcast([P, 4, N_MEM]),
                       ALU.mult).then_inc(p_ready, 1)
                if s >= 2:
                    u = s - 2
                    dve.wait_ge(o_mm, u + 1)
                    o = mixT[:, 12:16, u * P:(u + 1) * P]
                    TT(o, o, ps[:, 6 + u % 2, :].rearrange("p (h n) -> p h n", h=4), ALU.mult).then_inc(o_used, 1)
                if 1 <= s <= QT:
                    u = s - 1
                    dve.wait_ge(p_turned, 2 * u + 2)
                    nc.vector.tensor_copy(pmT[:, u % 2, 1, :, :].rearrange("p h n -> p (h n)"), ps[:, 5, :]).then_inc(p_copied[1], 1)


def queries(room):
    return room[:, 0:2 * N_HEADS * P].rearrange("p (b h n) -> p b h n", b=2, h=N_HEADS)


def load_queries(eng, q_t, z_dram, t, q_loaded):
    for s in range(N_HEADS // 2):
        at = stored(OFF_Q + SLAB * s)
        src = z_dram[at:at + 2, :, t * P:(t + 1) * P].rearrange("c p n -> p c n")
        eng.dma_start(q_t[:, t % 2, 2 * s:2 * s + 2, :], src).then_inc(q_loaded[t % 2], 16)


def block_d(nc, io, v, sem, sb_in):
    ident, ps, z_dram, mixT, kT, kv_tok, score = (v[n] for n in ("ident", "ps", "z_dram", "mixT", "kT", "kv_tok", "score"))
    own = ExitStack()
    with own:
        sb = lambda name, shape: sb_in(own, name, shape)
        kmq, q_loaded = v["kmq"], v["q_loaded"]
        dist = sb("dist", [P, 3, SEQ])
        q_t = queries(v["v_or_q"])
        lg = sb("lg", [P, 2, SEQ])
        pr = sb("pr", [P, 2, GQA, SEQ])
        prT = sb("prT", [P, 2, GQA, P])
        inv_d = sb("inv_d", [P, 2, GQA, P])
        HEADS = QT * N_HEADS
        nmx = sb("nmx_d", [P, HEADS])
        rs = sb("rs_d", [P, HEADS])
        rinv = sb("rinv_d", [P, HEADS])

        dist_ready, pool_link = sem("dist_ready"), sem("pool_link_d")
        s_mm, s_read, nm_ready = sem("s_mm_d"), sem("s_read_d"), sem("nm_ready_d")
        exp_done, rinv_ready, p_ready = sem("exp_done_d"), sem("rinv_ready_d"), sem("p_ready_d")
        p_turned, p_copied = sem("p_turned_d"), [sem(f"p_copied_d{k}") for k in range(2)]
        o_mm, o_used, dve_link = sem("o_mm_d"), sem("o_used_d"), sem("dve_link_d")
        UNITS = [(t, g) for t in range(QT) for g in range(N_KV)]
        first_key_block = [sum(t + 1 for t, _ in UNITS[:u]) for u in range(len(UNITS) + 1)]

        def steps(u):
            kb = UNITS[u][0] + 1
            todo = []
            for k in range(kb):
                todo.append(("turn", k))
                if k:
                    todo.append(("value", k - 1))
            todo.append(("value", kb - 1))
            cut = [len(todo) * j // 4 for j in range(5)]
            return [todo[cut[j]:cut[j + 1]] for j in range(4)]

        block = own.enter_context(nc.Block(name="attend"))

        @block.sync
        def _(sp):
            for t in range(2, QT):
                sp.wait_ge(s_mm, N_HEADS * (t - 1))
                load_queries(sp, q_t, z_dram, t, q_loaded)
            sp.dma_start(v["pages"][:], io["page_table"].rearrange("b n -> (b n)").unsqueeze(0)).then_inc(v["pages_loaded"], 16)
            sp.wait_ge(v["pages_loaded"], 16)
            sp.wait_ge(dist_ready, len(IDX_TILES))
            for b in range(2):
                load_keys(sp, io, v, b)

        @block.gpsimd
        def _(pool):
            link = Link(pool, pool_link)
            def prepare(t):
                n = (t + 1) * P
                if t >= IDX_TILES[0] + 3:
                    pool.wait_ge(s_read, N_HEADS * (t - 2))
                d = dist[:, t % 3, 0:n]
                link(nc.gpsimd.tensor_scalar(d, score[:, IDX_OFF[t]:IDX_OFF[t] + n], CUT, FAR, ALU.is_ge, ALU.mult))
                nc.gpsimd.tensor_tensor(d, d, kmq[:, SEQ - n:SEQ], ALU.add).then_inc(dist_ready, 1)

            for t in IDX_TILES:
                prepare(t)
            B, S = DEC_BATCH, DEC_SEQ
            lateT, qrow, rm32, spread, slope = (v[n] for n in ("lateT", "qrow", "rm32", "spread", "slope"))
            A = nc.gpsimd.affine_select
            link(nc.gpsimd.iota(qrow[:].rearrange("p (b q) -> p b q", q=S), pattern=[[0, B], [1, S]], base=0,
                                channel_multiplier=0, allow_small_or_imprecise_dtypes=True))
            link(nc.gpsimd.memset(lateT[:], 3e38))
            link(A(out=lateT[:], in_=lateT[:], compare_op=ALU.is_ge, fill=INVALID, base=0, pattern=[[0, B], [1, S]], channel_multiplier=-1))
            link(nc.gpsimd.memset(rm32[:], 1.0))
            link(A(out=rm32[:], in_=rm32[:], compare_op=ALU.is_ge, fill=0.0, base=0, pattern=[[-S, B]], channel_multiplier=1))
            link(A(out=rm32[:], in_=rm32[:], compare_op=ALU.is_ge, fill=0.0, base=S - 1, pattern=[[S, B]], channel_multiplier=-1))
            for j in range(4):
                link(nc.gpsimd.tensor_copy(spread[:, j, :], ident[0:NS, 0:NS]))
                for g in range(N_KV):
                    link(nc.gpsimd.memset(slope[NS * j:NS * (j + 1), g:g + 1], 2.0 ** (-8.0 * (GQA * g + j + 1) / N_HEADS)))
            link(nc.gpsimd.iota(v["dist_e"][:], pattern=[[1, PAST_LEN + S]], base=-PAST_LEN, channel_multiplier=0, allow_small_or_imprecise_dtypes=True))

        @block.tensor
        def _(pe):
            def turn(u, k):
                gk = first_key_block[u] + k
                if gk >= 2:
                    pe.wait_ge(p_copied[gk % 2], gk // 2)
                for j in range(GQA):
                    last = nc.tensor.matmul(ps[:, 4 + gk % 2, j * P:(j + 1) * P], pr[:, u % 2, j, k * P:(k + 1) * P],
                                            inv_d[:, u % 2, j, :], start=True, stop=True)
                last.then_inc(p_turned, 1)

            def value(u, k):
                t, g = UNITS[u]
                gk = first_key_block[u] + k
                pe.wait_ge(p_copied[gk % 2], gk // 2 + 1)
                if k == 0 and u >= 2:
                    pe.wait_ge(o_used, u - 1)
                v_ = kv_tok[:, k, 256 + g * P:256 + (g + 1) * P]
                nc.tensor.matmul(ps[:, 6 + u % 2, :], v_, prT[:, gk % 2, :, :].rearrange("p j n -> p (j n)"),
                                 start=(k == 0), stop=(k == t)).then_inc(o_mm, 1)

            for s in range(len(UNITS) + 1):
                todo = steps(s - 1) if s else [[]] * 4
                for j in range(GQA):
                    if s < len(UNITS):
                        t, g = UNITS[s]
                        hh = GQA * s + j
                        if g == 0 and j == 0:
                            pe.wait_ge(q_loaded[t % 2], 64 * (t // 2 + 1))
                        if hh >= 2:
                            pe.wait_ge(s_read, hh - 1)
                        for x0 in range(0, (t + 1) * P, 512):
                            w = min(512, (t + 1) * P - x0)
                            last = nc.tensor.matmul(ps[:, 2 * (hh % 2) + x0 // 512, 0:w], q_t[:, t % 2, GQA * g + j, :],
                                                    kT[:, g, x0:x0 + w], start=True, stop=True)
                        last.then_inc(s_mm, 1)
                    if s and j == 0:
                        pe.wait_ge(p_ready, GQA * s)
                    for kind, k in todo[j]:
                        (turn if kind == "turn" else value)(s - 1, k)

        def copy_turned(eng, copy, u, todo, parity):
            for kind, k in todo:
                gk = first_key_block[u] + k
                if kind == "turn" and gk % 2 == parity:
                    eng.wait_ge(p_turned, gk + 1)
                    if gk >= 2:
                        eng.wait_ge(o_mm, gk - 1)
                    copy(prT[:, parity, :, :].rearrange("p j n -> p (j n)"), ps[:, 4 + parity, :]).then_inc(p_copied[parity], 1)

        @block.scalar
        def _(act):
            def diagonal(hh):
                act.wait_ge(rinv_ready, hh + 1)
                nc.scalar.activation(inv_d[:, (hh // GQA) % 2, hh % GQA, :], ident[:], ACT.Copy, scale=rinv[:, hh:hh + 1]).then_inc(p_ready, 1)

            for s in range(len(UNITS) + 1):
                todo = steps(s - 1) if s else [[]] * 4
                for j in range(GQA):
                    if s < len(UNITS):
                        n = (UNITS[s][0] + 1) * P
                        hh = GQA * s + j
                        act.wait_ge(nm_ready, hh + 1)
                        if j == 0 and s >= 2:
                            act.wait_ge(p_turned, first_key_block[s - 1])
                        nc.scalar.activation(pr[:, s % 2, j, 0:n], lg[:, hh % 2, 0:n], ACT.Exp, bias=nmx[:, hh:hh + 1],
                                             accum_out=rs[:, hh:hh + 1]).then_inc(exp_done, 1)
                        if j:
                            diagonal(hh - 1)
                    copy_turned(act, nc.scalar.copy, s - 1, todo[j], 0)
                if s < len(UNITS):
                    diagonal(GQA * s + 3)

        @block.vector
        def _(dve):
            link = Link(dve, dve_link)

            def invert(hh):
                dve.wait_ge(exp_done, hh + 1)
                nc.vector.reciprocal(rinv[:, hh:hh + 1], rs[:, hh:hh + 1]).then_inc(rinv_ready, 1)

            for s in range(len(UNITS) + 1):
                todo = steps(s - 1) if s else [[]] * 4
                for j in range(GQA):
                    if s < len(UNITS):
                        t, g = UNITS[s]
                        n = (t + 1) * P
                        hh = GQA * s + j
                        if g == 0 and j == 0 and t in IDX_TILES:
                            dve.wait_ge(dist_ready, t - IDX_TILES[0] + 1)
                        away = dist[:, t % 3, 0:n] if t in IDX_TILES else kmq[:, SEQ - n:SEQ]
                        dve.wait_ge(s_mm, hh + 1)
                        src = ps[:, 2 * (hh % 2):2 * (hh % 2) + 2, :].rearrange("p a n -> p (a n)")[:, 0:n]
                        if hh >= 2:
                            dve.wait_ge(exp_done, hh - 1)
                        nc.vector.scalar_tensor_tensor(out=lg[:, hh % 2, 0:n], in0=away,
                                                       scalar=2.0 ** (-8.0 * (GQA * g + j + 1) / N_HEADS), in1=src,
                                                       op0=ALU.mult, op1=ALU.add).then_inc(s_read, 1)
                        dve.wait_ge(s_read, hh + 1)
                        nc.vector.tensor_reduce(nmx[:, hh:hh + 1], lg[:, hh % 2, 0:n], AX_X, ALU.max, negate=True).then_inc(nm_ready, 1)
                        if j:
                            invert(hh - 1)
                    copy_turned(dve, nc.vector.tensor_copy, s - 1, todo[j], 1)
                if s < len(UNITS):
                    invert(GQA * s + 3)
                if s:
                    u = s - 1
                    t, g = UNITS[u]
                    dve.wait_ge(o_mm, first_key_block[u + 1])
                    o = mixT[:, GQA * g:GQA * (g + 1), t * P:(t + 1) * P]
                    nc.vector.tensor_tensor(o, o, ps[:, 6 + u % 2, :].rearrange("p (j n) -> p j n", j=GQA), ALU.mult).then_inc(o_used, 1)


def page_of(eng, io, v, b, n):
    at = b * (PAST_LEN // PAGE) + n
    return bass.ds(eng.value_load(v["pages"][0:1, at:at + 1], min_val=0, max_val=io["cache_k"].shape[1] - 1), 1)


def keys_room(v):
    score = v["score"]
    return (score[:, 0:2048].rearrange("p (b n d) -> p b n d", b=2, n=PAST_LEN // PAGE),
            score[:, 2048:4096].rearrange("p (b n d) -> p b n d", b=2, n=2), v["ki_in"])


def load_keys(eng, io, v, b):
    k_in, mk_in, ki_in = keys_room(v)
    loaded = v["k_loaded"][b % 2]
    for n in range(PAST_LEN // PAGE):
        page = page_of(eng, io, v, b, n)
        eng.dma_start(ki_in[:, b % 2, n, :], io["cache_kidx"][0, page].rearrange("a p d -> (a p) d")).then_inc(loaded, 16)
        eng.dma_start(k_in[:, b % 2, n, :], io["cache_k"][0, page].rearrange("a p h d -> (a p) (h d)")).then_inc(loaded, 16)
    eng.dma_start(mk_in[:, b % 2, :, :], io["cache_mem_k"][0, b].rearrange("(a p) h d -> p a (h d)", p=P)).then_inc(loaded, 16)


def block_e(nc, io, v, sem, sb_in):
    ident, ps, z_dram, mixT, kT = (v[n] for n in ("ident", "ps", "z_dram", "mixT", "kT"))
    wis, qi_s, kiT, score = (v[n] for n in ("wis", "qi_s", "kiT", "score"))
    B, S = DEC_BATCH, DEC_SEQ
    PAGES = PAST_LEN // PAGE
    KEYS = PAST_LEN + S
    BLOCKS = PAGES + 1
    own = ExitStack()
    with own:
        sb = lambda name, shape, dt=F32: sb_in(own, name, shape, dt)
        pages, lateT, qrow, rm32, spread, slope, dist = (v[n] for n in ("pages", "lateT", "qrow", "rm32", "spread", "slope", "dist_e"))
        k_in, mk_in, ki_in = keys_room(v)
        v_all = sb("v_all", [P, B, PAGES, 256])
        v_new = sb("v_new", [S, B, 256])
        mv_all = sb("mv_all", [P, B, 2, D_MEM])
        key_room = sb("key_room", [P, 3 * PAST_LEN])
        oT = kT[:].rearrange("p g n -> p (g n)")[0:4 * S, 0:N_KV * B * P]
        kbT = key_room[:, 0:N_KV * PAST_LEN].rearrange("p (g n) -> p g n", g=N_KV)
        kibT = key_room[:, N_KV * PAST_LEN:]
        mkbT = sb("mkbT", [P, 4, N_MEM])
        q_s = sb("q_s", [P, N_HEADS, NS])
        qm_s = sb("qm_s", [P, 4, NS])
        spare = v["y_room"][:, KT * TOK:]
        wi_all = spare[:, 0:NS * N_IDX].rearrange("p (b s h) -> p b s h", b=B, s=S)
        wi_b = spare[:, NS * N_IDX:2 * NS * N_IDX].rearrange("p (b a c s) -> p b a c s", b=B, a=2, s=S)
        r_ = sb("r_", [P, BLOCKS, 2 * N_IDX // 2, S])
        sT = sb("sT", [P, BLOCKS, B, S])
        SEL = KEYS + 8
        sel = sb("sel", [NS, SEL])
        m8 = sb("m8_e", [NS, 8])
        qcol = sb("qcol", [NS, 1])
        rmask = sb("rmask", [P, B])
        acc = sb("acc_e", [P, N_KV, KEYS])
        acc_m = sb("acc_m", [P, N_MEM])
        pT = key_room[:, 0:N_KV * BLOCKS * P].rearrange("p (g n b j q) -> p g n b j q", g=N_KV, n=BLOCKS, j=4, b=B)
        pmT = sb("pmT_e", [P, 2, 4, B, S])
        sm = sb("sm_e", [P, 3, 4])

        pages_loaded, const_ready = v["pages_loaded"], sem("const_ready_e")
        small_loaded, wi_written, wi_loaded = sem("small_loaded"), sem("wi_written"), sem("wi_loaded")
        k_loaded = v["k_loaded"]
        v_loaded = sem("v_loaded_e")
        k_turned, k_copied = sem("k_turned_e"), sem("k_copied_e")
        i_mm, i_read, s_mm, s_read = sem("i_mm"), sem("i_read"), sem("s_mm_e"), sem("s_read_e")
        dve_link, rows_made, rows_used = sem("dve_link_e"), sem("rows_made"), sem("rows_used")
        score_turned, chosen, spread_done = sem("score_turned"), sem("chosen"), sem("spread_done")
        scores_sT, logits, exp_done, p_ready = sem("scores_sT"), sem("logits_e"), sem("exp_done_e"), sem("p_ready_e")
        p_turned, p_copied, o_mm = sem("p_turned_e"), sem("p_copied_e"), sem("o_mm_e")
        mix_summed, o_copied, o_turned = sem("mix_summed"), sem("o_copied"), sem("o_turned")
        absolute = spare[:, 2 * NS * N_IDX:2 * NS * N_IDX + SEQ // 2].bitcast(BF16)
        wi_dram = nc.dram_tensor("wi_scratch", (NS, N_IDX), F32, kind="Internal").ap()

        block = own.enter_context(nc.Block(name="sample"))

        @block.sync
        def _(sp):
            sp.dma_start(wi_dram, wis[0:NS, QT, :]).then_inc(wi_written, 16)
            for s in range(4):
                at = stored(OFF_Q + SLAB * s)
                sp.dma_start(q_s[:, 2 * s:2 * s + 2, :], z_dram[at:at + 2, :, SEQ:TOK].rearrange("c p n -> p c n")).then_inc(small_loaded, 16)
            for s in range(2):
                at = stored(OFF_QM + SLAB * s)
                sp.dma_start(qm_s[:, 2 * s:2 * s + 2, :], z_dram[at:at + 2, :, SEQ:TOK].rearrange("c p n -> p c n")).then_inc(small_loaded, 16)
            sp.dma_start(v_new[:], io["out_v_s"][0].rearrange("b s h d -> s b (h d)")).then_inc(small_loaded, 16)
            sp.wait_ge(wi_written, 16)
            sp.dma_start(spare[:, 0:NS * N_IDX], wi_dram.rearrange("t h -> (t h)").partition_broadcast(P)).then_inc(wi_loaded, 16)
            for b in range(2, B):
                sp.wait_ge(k_turned, 3 * (b - 1))
                load_keys(sp, io, v, b)
            sp.wait_ge(k_turned, 3 * B)
            sp.dma_start(w_slab(score), w_out_slab(io, 0)).then_inc(v["w_first"], 16)

        @block.gpsimd
        def _(pool):
            pool.wait_ge(small_loaded, 7 * 16)
            for q in (q_s, qm_s):
                last = nc.gpsimd.tensor_scalar(q[:], q[:], HEAD_DIM ** -0.5, None, ALU.mult)
            last.then_inc(const_ready, 1)
            for b in range(B):
                for n in range(PAGES):
                    src = io["cache_v"][0, page_of(pool, io, v, b, n)].rearrange("a p h d -> (a p) (h d)")
                    pool.dma_start(v_all[:, b, n, :], src).then_inc(v_loaded, 16)
                pool.dma_start(mv_all[:, b, :, :], io["cache_mem_v"][0, b].rearrange("(a p) h d -> p a (h d)", p=P)).then_inc(v_loaded, 16)

        @block.tensor
        def _(pe):
            nc.tensor.transpose(ps[0:NS, 7, 0:1], qrow[:], ident[0:1, 0:1])
            nc.tensor.matmul(ps[:, 7, 8:8 + B], spread[:].rearrange("k j n -> k (j n)"), rm32[:], start=True, stop=True).then_inc(rows_made, 1)
            pe.wait_ge(rows_used, 1)
            for b in range(B):
                pe.wait_ge(k_loaded[b % 2], (2 * PAGES + 1) * 16 * (b // 2 + 1))
                if b:
                    pe.wait_ge(k_copied, 3 * b)
                for n in range(PAGES):
                    last = nc.tensor.transpose(ps[0:IDX_DIM, 0, n * P:(n + 1) * P], ki_in[:, b % 2, n, :], ident[:])
                last.then_inc(k_turned, 1)
                for g in range(N_KV):
                    if b:
                        pe.wait_ge(s_read, 4 * b)
                    for n in range(PAGES):
                        last = nc.tensor.transpose(ps[:, 1 + g, n * P:(n + 1) * P], k_in[:, b % 2, n, g * P:(g + 1) * P], ident[:])
                last.then_inc(k_turned, 1)
                for h in range(4):
                    for n in range(2):
                        last = nc.tensor.transpose(ps[:, 3 + h // 2, (2 * (h % 2) + n) * P:(2 * (h % 2) + n + 1) * P],
                                                   mk_in[:, b % 2, n, h * P:(h + 1) * P], ident[:])
                last.then_inc(k_turned, 1)
                pe.wait_ge(k_copied, 3 * b + 1)
                if b:
                    pe.wait_ge(i_read, 2 * b)
                for n in range(BLOCKS):
                    for a in range(2):
                        half = slice(a * IDX_DIM, (a + 1) * IDX_DIM)
                        keys = kibT[half, n * P:(n + 1) * P] if n < PAGES else kiT[half, a, SEQ + S * b:SEQ + S * (b + 1)]
                        m = P if n < PAGES else S
                        col = 64 + 32 * n
                        last = nc.tensor.matmul(ps[0:m, 5 + a, col:col + 32], keys, qi_s[half, :, S * b:S * (b + 1)], start=True, stop=True)
                last.then_inc(i_mm, 1)
                pe.wait_ge(k_copied, 3 * b + 3)
                if b == 0:
                    pe.wait_ge(const_ready, 1)
                for g in range(N_KV):
                    q = q_s[:, GQA * g:GQA * (g + 1), :].rearrange("p j n -> p (j n)")
                    nc.tensor.matmul(ps[:, 1 + g, :], q, kbT[:, g, :], start=True, stop=True)
                    last = nc.tensor.matmul(ps[:, 4, g * S:(g + 1) * S], q, kT[:, g, SEQ + S * b:SEQ + S * (b + 1)], start=True, stop=True)
                for h in range(4):
                    last = nc.tensor.matmul(ps[NS * h:NS * (h + 1), 7, 0:N_MEM], qm_s[:, h, :], mkbT[:, h, :], start=True, stop=True)
                last.then_inc(s_mm, 1)
            pe.wait_ge(scores_sT, 1)
            pe.wait_ge(s_read, 4 * B)
            for n in range(BLOCKS):
                m = P if n < PAGES else S
                out = ps[0:NS, 0, n * P:(n + 1) * P] if n < PAGES else ps[0:NS, 1, 0:S]
                last = nc.tensor.transpose(out, sT[0:m, n, :, :].rearrange("p b q -> p (b q)"), ident[0:m, 0:m])
            last.then_inc(score_turned, 1)
            pe.wait_ge(p_ready, 1)
            for n in range(2):
                last = nc.tensor.transpose(ps[:, 6, n * P:(n + 1) * P], acc_m[:, n * P:(n + 1) * P], ident[:])
            last.then_inc(p_turned, 1)
            pe.wait_ge(v_loaded, (PAGES + 1) * B * 16)
            pe.wait_ge(p_copied, 1)
            for h in range(4):
                for b in range(B):
                    for n in range(2):
                        last = nc.tensor.matmul(ps[:, 7, h * NS + S * b:h * NS + S * (b + 1)], mv_all[:, b, n, h * P:(h + 1) * P],
                                                pmT[:, n, h, b, :], start=(n == 0), stop=(n == 1))
            last.then_inc(o_mm, 1)
            pe.wait_ge(chosen, 1)
            rows = spread[:].rearrange("k j n -> k (j n)")
            nc.tensor.matmul(ps[:, 2, :], rows, sel[:, 0:PAST_LEN], start=True, stop=True)
            nc.tensor.matmul(ps[:, 3, 0:S], rows, sel[:, PAST_LEN:KEYS], start=True, stop=True).then_inc(spread_done, 1)
            for g in range(N_KV):
                pe.wait_ge(p_ready, 2 + g)
                for n in range(BLOCKS):
                    w = P if n < PAGES else S
                    out = ps[:, 4 + 2 * g, n * P:(n + 1) * P] if n < PAGES else ps[0:S, 5 - 4 * g, 0:P]
                    last = nc.tensor.transpose(out, acc[:, g, n * P:n * P + w], ident[:])
                last.then_inc(p_turned, 1)
            pe.wait_ge(p_copied, 3)
            for g in range(N_KV):
                for b in range(B):
                    for n in range(BLOCKS):
                        m = P if n < PAGES else S
                        vals = v_all[:, b, n, g * P:(g + 1) * P] if n < PAGES else v_new[:, b, g * P:(g + 1) * P]
                        last = nc.tensor.matmul(ps[0:4 * S, 2 * g + b // 4, (b % 4) * P:(b % 4 + 1) * P],
                                                pT[0:m, g, n, b, :, :].rearrange("p j q -> p (j q)"), vals,
                                                start=(n == 0), stop=(n == BLOCKS - 1))
                last.then_inc(o_mm, 1)
            for g in range(N_KV):
                pe.wait_ge(o_copied, g + 1)
                for b in range(B):
                    at = g * B + b
                    last = nc.tensor.transpose(ps[:, 4, at * 4 * S:(at + 1) * 4 * S], oT[:, at * P:(at + 1) * P], ident[0:4 * S, 0:4 * S])
            last.then_inc(o_turned, 1)

        @block.scalar
        def _(act):
            for b in range(B):
                act.wait_ge(k_turned, 3 * b + 1)
                if b:
                    act.wait_ge(i_mm, b)
                nc.scalar.copy(kibT[0:IDX_DIM, :], ps[0:IDX_DIM, 0, :])
                nc.scalar.copy(kibT[IDX_DIM:P, :], ps[0:IDX_DIM, 0, :]).then_inc(k_copied, 1)
                act.wait_ge(k_turned, 3 * b + 2)
                if b:
                    act.wait_ge(s_mm, b)
                nc.scalar.copy(key_room[:, 0:N_KV * PAST_LEN], ps[:, 1:3, :].rearrange("p g n -> p (g n)")).then_inc(k_copied, 1)
                act.wait_ge(k_turned, 3 * b + 3)
                nc.scalar.copy(mkbT[:].rearrange("p h n -> p (h n)"), ps[:, 3:5, :].rearrange("p g n -> p (g n)")).then_inc(k_copied, 1)
                for k in range(KT // B * b, KT // B * (b + 1)):
                    if k:
                        act.wait_ge(mix_summed, k)
                    nc.scalar.activation(absolute, mixT[:, k, 0:SEQ], ACT.Abs, accum_out=v["mix_size"][:, k:k + 1]).then_inc(mix_summed, 1)
            act.wait_ge(logits, 1)
            nc.scalar.activation(acc_m[:], acc_m[:], ACT.Exp, bias=sm[:, 0, 2:3], accum_out=sm[:, 1, 2:3]).then_inc(exp_done, 1)
            act.wait_ge(p_turned, 1)
            nc.scalar.copy(pmT[:].rearrange("p n h b q -> p (n h b q)"), ps[:, 6, 0:2 * P]).then_inc(p_copied, 1)
            for g in range(N_KV):
                act.wait_ge(logits, 2 + g)
                nc.scalar.activation(acc[:, g, :], acc[:, g, :], ACT.Exp, bias=sm[:, 0, g:g + 1], accum_out=sm[:, 1, g:g + 1]).then_inc(exp_done, 1)
            for g in range(N_KV):
                act.wait_ge(p_turned, 2 + g)
                for n in range(BLOCKS):
                    m = P if n < PAGES else S
                    src = ps[:, 4 + 2 * g, n * P:(n + 1) * P] if n < PAGES else ps[0:S, 5 - 4 * g, 0:P]
                    last = nc.scalar.copy(pT[0:m, g, n, :, :, :].rearrange("p b j q -> p j b q"), src.rearrange("p (j b q) -> p j b q", j=4, b=B))
                last.then_inc(p_copied, 1)
            for g in range(N_KV):
                act.wait_ge(o_mm, 2 + g)
                nc.scalar.copy(oT[:, g * B * P:(g + 1) * B * P], ps[0:4 * S, 2 * g:2 * g + 2, :].rearrange("p a n -> p (a n)")).then_inc(o_copied, 1)

        @block.vector
        def _(dve):
            link = Link(dve, dve_link)
            TSC, TT, STT = nc.vector.tensor_scalar, nc.vector.tensor_tensor, nc.vector.scalar_tensor_tensor
            copy = nc.vector.tensor_copy
            dve.wait_ge(rows_made, 1)
            link(copy(qcol[:], ps[0:NS, 7, 0:1]))
            copy(rmask[:], ps[:, 7, 8:8 + B]).then_inc(rows_used, 1)
            dve.wait_ge(rows_used, 1)
            dve.wait_ge(wi_loaded, 16)
            for a in range(2):
                src = wi_all.rearrange("p b s (c a) -> p b s c a", a=2)
                for c in range(N_IDX // 2):
                    last = copy(wi_b[:, :, a, c, :], src[:, :, :, c, a])
            link(last)
            for b in range(B):
                dve.wait_ge(i_mm, b + 1)
                for rows, blocks in ((slice(0, P), slice(0, PAGES)), (slice(0, S), slice(PAGES, BLOCKS))):
                    n = blocks.stop - blocks.start
                    src = ps[rows, 5:7, 64 + blocks.start * 32:64 + blocks.stop * 32].rearrange("p a (n x) -> p a n x", n=n)
                    r = r_[rows, blocks, :, :]
                    last = TSC(r.rearrange("p n (a c) q -> p a n (c q)", a=2), src, IDX_DIM ** -0.5, 0.0, ALU.mult, ALU.max)
                    last.then_inc(i_read, 1)
                    dve.wait_ge(i_read, 2 * b + (1 if n > 1 else 2))
                    wb_ = wi_b[rows, b, :, :, :].rearrange("p a c q -> p (a c) q").unsqueeze(1).to_broadcast([rows.stop, n, N_IDX, S])
                    link(TT(r, r, wb_, ALU.mult))
                    link(nc.vector.tensor_reduce(sT[rows, blocks, b, :], r.rearrange("p n c q -> p n q c"), AX_X, ALU.add))
                dve.wait_ge(s_mm, b + 1)
                rm = rmask[:, b:b + 1]
                for out, src in ((acc[:, :, 0:PAST_LEN], ps[:, 1:3, :]), (acc[:, :, PAST_LEN:KEYS], ps[:, 4, 0:2 * S].rearrange("p (g n) -> p g n", g=2)),
                                 (acc_m[:], ps[:, 7, 0:N_MEM])):
                    if b == 0:
                        last = TSC(out, src, rm, None, ALU.mult)
                    else:
                        last = STT(out=out, in0=src, scalar=rm, in1=out, op0=ALU.mult, op1=ALU.add)
                    last.then_inc(s_read, 1)
                copy(sm[:, 2, 3:4], rm).then_inc(s_read, 1)
                dve.wait_ge(s_read, 4 * b + 4)
            TT(sT[0:S, PAGES, :, :], sT[0:S, PAGES, :, :], lateT[:], ALU.min).then_inc(scores_sT, 1)

            def invert(k, group, p):
                dve.wait_ge(exp_done, k + 1)
                link(nc.vector.reciprocal(sm[:, 2, group:group + 1], sm[:, 1, group:group + 1]))
                TSC(p, p, sm[:, 2, group:group + 1], None, ALU.mult).then_inc(p_ready, 1)

            nc.vector.tensor_reduce(sm[:, 0, 2:3], acc_m[:], AX_X, ALU.max, negate=True).then_inc(logits, 1)
            dve.wait_ge(score_turned, 1)
            link(nc.vector.memset(sel[:, KEYS:SEL], PAD))
            link(copy(sel[:, 0:PAST_LEN], ps[0:NS, 0, :]))
            link(copy(sel[:, PAST_LEN:KEYS], ps[0:NS, 1, 0:S]))
            invert(0, 2, acc_m[:])
            for n in range(TOPK_S // 8 + 1):
                link(nc.vector.max(out=m8[:], in_=sel[:]))
                if n == TOPK_S // 8:
                    link(nc.vector.memset(m8[:, TOPK_S % 8:8], PAD))
                link(nc.vector.match_replace(out=sel[:], in_to_replace=m8[:], in_values=sel[:], imm_value=REPLACED))
            s_ = sel[:, 0:KEYS]
            link(TSC(s_, s_, CUT, FAR, ALU.is_ge, ALU.mult))
            link(TT(s_, s_, dist[0:NS, :], ALU.add))
            TSC(s_, s_, qcol[:], None, ALU.subtract).then_inc(chosen, 1)
            dve.wait_ge(spread_done, 1)
            link(copy(dist[:, 0:PAST_LEN], ps[:, 2, :]))
            link(copy(dist[:, PAST_LEN:KEYS], ps[:, 3, 0:S]))
            for g in range(N_KV):
                link(STT(out=acc[:, g, :], in0=dist[:], scalar=slope[:, g:g + 1], in1=acc[:, g, :], op0=ALU.mult, op1=ALU.add))
                nc.vector.tensor_reduce(sm[:, 0, g:g + 1], acc[:, g, :], AX_X, ALU.max, negate=True).then_inc(logits, 1)
            for g in range(N_KV):
                invert(1 + g, g, acc[:, g, :])
            dve.wait_ge(o_mm, 1)
            o = mixT[:, 12:16, SEQ:TOK]
            TT(o, o, ps[:, 7, 0:P].rearrange("p (h n) -> p h n", h=4), ALU.mult)
            dve.wait_ge(o_turned, 1)
            for g in range(N_KV):
                o = mixT[:, GQA * g:GQA * (g + 1), SEQ:TOK].rearrange("p j (b q) -> p j b q", b=B)
                src = ps[:, 4, g * B * 4 * S:(g + 1) * B * 4 * S].rearrange("p (b j q) -> p j b q", b=B, j=4)
                TT(o, o, src, ALU.mult)


def w_slab(place):
    return place[:, 0:KT * SLAB].rearrange("p (k n) -> p k n", k=KT)


def w_out_slab(io, s):
    return io["w_out"][0].rearrange("(k p) n -> p k n", p=P)[:, :, s * SLAB:(s + 1) * SLAB]


def block_f(nc, io, v, sem, sb_in):
    ps, mixT, score, ones, mix_size, w_first = (v[n] for n in ("ps", "mixT", "score", "ones", "mix_size", "w_first"))
    own = ExitStack()
    with own:
        sb = lambda name, shape, dt=F32: sb_in(own, name, shape, dt)
        NSLAB = D_MODEL // SLAB
        m16 = sb("m16", [P, 2, KT, TOK], F16)
        w16 = sb("w16_f", [P, 2, 2, KT, SLAB], F16)
        raw = w_slab(score)
        x_in = sb("x_f", [P, QT + 1, SLAB])
        y = v["y_room"][:].rearrange("p (t n) -> p t n", t=QT + 1)
        g_b = v["kiT"][:].rearrange("p a n -> p (a n)")[:, 0:D_MODEL]
        sq = v["qi_s"][:].rearrange("p c n -> p (c n)").bitcast(BF16).rearrange("p (a n) -> p a n", a=2)
        size = sb("size_f", [P, 2])
        unit = sb("unit_f", [P, 3, 3])
        ss = sb("ss_f", [P, QT + 1, NSLAB])
        st = sb("st_f", [P, QT + 1, 4])

        w_loaded, w_sized, w_summed, m_high, m_low, w_high, w_split, unit_ready, act_link = (
            sem(n) for n in ("w_o_loaded", "w_o_sized", "w_o_summed", "m_high", "m_low", "w_o_high", "w_o_split", "unit_ready_f", "unit_scaled_f"))
        x_loaded, g_loaded = sem("x_again"), sem("g_f_loaded")
        y_mm, banks_free, y_sq, ms_ready, rt_ready, fin = (sem(n) for n in ("yo_mm", "banks_free", "yo_sq", "ms_f", "rt_f", "fin_f"))
        dve_link, loop_link, stored_y = sem("dve_link_f"), sem("loop_link_f"), sem("stored_y")

        RING = 6
        TILES_F = QT + 1

        def rows(t):
            return P if t < QT else NS

        def low_of_first(pool, q):
            k = slice(4 * q, 4 * q + 4)
            pool.wait_ge(w_high, q + 1)
            nc.gpsimd.tensor_tensor(w16[:, 0, 1, k, :], raw[:, k, :], w16[:, 0, 0, k, :], ALU.subtract).then_inc(w_split, 1)

        def bank(b, t):
            return (TILES_F * b + t) % RING

        def slab(ap, s):
            return ap.rearrange("p (s n) -> p s n", n=SLAB)[:, bass.ds(s, 1), :].rearrange("p a n -> p (a n)")

        block = own.enter_context(nc.Block(name="out"))

        @block.sync
        def _(sp):
            for s in range(NSLAB):
                if s:
                    sp.wait_ge(w_split, 4 * s)
                    sp.dma_start(raw, w_out_slab(io, s)).then_inc(w_loaded, 16)
                    sp.wait_ge(banks_free, TILES_F * s + RING)
                cols = slice(s * SLAB, (s + 1) * SLAB)
                sp.dma_start(x_in[:, 0:QT, :], io["x_prompt"][0, :, cols].rearrange("(t p) n -> p t n", p=P)).then_inc(x_loaded, 16)
                sp.dma_start(x_in[0:NS, QT, :], io["x_sample"].rearrange("b s d -> (b s) d")[:, cols]).then_inc(x_loaded, 16)
                if s == 0:
                    sp.dma_start(g_b, io["g_final"].partition_broadcast(P)).then_inc(g_loaded, 16)
            for t in range(TILES_F):
                sp.wait_ge(fin, t + 1)
                dst = io["out_y_p"][0, t * P:(t + 1) * P, :] if t < QT else io["out_y_s"].rearrange("b s d -> (b s) d")
                sp.dma_start(dst, y[0:rows(t), t, :]).then_inc(stored_y, 16)
            sp.wait_ge(stored_y, 16 * TILES_F)

        @block.tensor
        def _(pe):
            def sum_sizes(s, b):
                pe.wait_ge(w_summed, s + 1)
                nc.tensor.matmul(ps[:, 7, 0:1], ones[:], size[:, b:b + 1], start=True, stop=True).then_inc(w_sized, 1)

            pe.wait_ge(unit_ready, 1)
            nc.tensor.matmul(ps[:, 6, 0:1], ones[:], mix_size[:, KT + 1:KT + 2], start=True, stop=True).then_inc(w_sized, 1)
            pe.wait_ge(w_summed, 1)
            nc.tensor.matmul(ps[:, 7, 0:1], ones[:], size[:, 0:1], start=True, stop=True).then_inc(w_sized, 1)
            def slab_products(s, b, more=True):
                for t in range(TILES_F):
                    pe.wait_ge(banks_free, TILES_F * s + (t + 1))
                    for k in range(KT):
                        if t == 0 and k % 4 == 0:
                            pe.wait_ge(w_split, 4 * s + (k // 4 + 1))
                        if t == 0 and b == 0:
                            pe.wait_ge(m_low, k + 1)
                        for j, (mp, wp) in enumerate(((0, 0), (0, 1), (1, 0))):
                            last = nc.tensor.matmul(ps[0:rows(t), bank(b, t), 0:SLAB], m16[:, mp, k, t * P:t * P + rows(t)],
                                                    w16[:, b, wp, k, :], start=(k == 0 and j == 0), stop=(k == KT - 1 and j == 2))
                    last.then_inc(y_mm, 1)
                    if t == 3 and more:
                        sum_sizes(s + 1, 1 - b)

            with pe.Fori(0, NSLAB // 2 - 1) as it:
                for b in range(2):
                    slab_products(it * 2 + b, b)
            slab_products(NSLAB - 2, 0)
            slab_products(NSLAB - 1, 1, more=False)

        @block.vector
        def _(dve):
            link = Link(dve, dve_link)
            TSC, TT, STT = nc.vector.tensor_scalar, nc.vector.tensor_tensor, nc.vector.scalar_tensor_tensor
            dve.sem_inc(banks_free, RING)
            dve.wait_ge(w_summed, 1)
            nc.vector.tensor_reduce(mix_size[:, KT + 1:KT + 2], mix_size[:, 0:KT + 1], AX_X, ALU.max).then_inc(unit_ready, 1)
            dve.wait_ge(w_sized, 1)
            link(TSC(unit[:, 0, 0:1], ps[:, 6, 0:1], M_SHIFT, TINY, ALU.mult, ALU.max))
            nc.vector.reciprocal(unit[:, 0, 1:2], unit[:, 0, 0:1]).then_inc(unit_ready, 1)

            def set_unit(link, s, b):
                dve.wait_ge(w_sized, s + 2)
                u = [unit[:, 1 + b, i:i + 1] for i in range(3)]
                link(TSC(u[0], ps[:, 7, 0:1], W_SHIFT, TINY, ALU.mult, ALU.max))
                nc.vector.reciprocal(u[1], u[0])
                TT(u[2], u[0], unit[:, 0, 0:1], ALU.mult).then_inc(unit_ready, 1)

            def split_low(s, b, q):
                k = slice(4 * q, 4 * q + 4)
                dve.wait_ge(w_high, 4 * s + (q + 1))
                TT(w16[:, b, 1, k, :], raw[:, k, :], w16[:, b, 0, k, :], ALU.subtract).then_inc(w_split, 1)

            set_unit(link, 0, 0)
            for q in range(4):
                for k in range(4 * q, 4 * q + 4):
                    dve.wait_ge(m_high, k + 1)
                    STT(out=m16[:, 1, k, :], in0=mixT[:, k, :], scalar=unit[:, 0, 1:2], in1=m16[:, 0, k, :],
                        op0=ALU.mult, op1=ALU.subtract).then_inc(m_low, 1)

            def add(s, b, t):
                dve.wait_ge(y_mm, TILES_F * s + (t + 1))
                if t == 0:
                    dve.wait_ge(x_loaded, 32 * s + 32)
                n = rows(t)
                STT(out=slab(y[0:n, t, :], s), in0=ps[0:n, bank(b, t), 0:SLAB], scalar=unit[0:n, 1 + b, 2:3],
                    in1=x_in[0:n, t, :], op0=ALU.mult, op1=ALU.add).then_inc(banks_free, 1)

            def finish(t):
                n = rows(t)
                dve.wait_ge(y_sq, 2 + TILES_F * (NSLAB - 1) + t + 1)
                link(nc.vector.tensor_reduce(st[0:n, t, 0:1], ss[0:n, t, :], AX_X, ALU.add))
                TSC(st[0:n, t, 1:2], st[0:n, t, 0:1], 1.0 / D_MODEL, EPS, ALU.mult, ALU.add).then_inc(ms_ready, 1)
                dve.wait_ge(rt_ready, t + 1)
                link(nc.vector.reciprocal(st[0:n, t, 3:4], st[0:n, t, 2:3]))
                STT(out=y[0:n, t, :], in0=y[0:n, t, :], scalar=st[0:n, t, 3:4], in1=g_b[0:n, :],
                    op0=ALU.mult, op1=ALU.mult).then_inc(fin, 1)

            dve.wait_ge(m_low, KT)
            def slab_adds(link, s, b):
                for t in range(TILES_F):
                    add(s, b, t)
                    if t == 4:
                        set_unit(link, s + 1, 1 - b)
                    if t >= 5:
                        split_low(s + 1, 1 - b, t - 5)

            with dve.Fori(0, NSLAB // 2 - 1) as it:
                dve.sem_clear(loop_link)
                in_loop = Link(dve, loop_link)
                for b in range(2):
                    slab_adds(in_loop, it * 2 + b, b)
            slab_adds(link, NSLAB - 2, 0)
            dve.wait_ge(g_loaded, 16)
            for t in range(TILES_F):
                add(NSLAB - 1, 1, t)
                if t:
                    finish(t - 1)
            finish(QT)

        @block.gpsimd
        def _(pool):
            pool.wait_ge(unit_ready, 3)
            for q in range(4):
                k = slice(4 * q, 4 * q + 4)
                nc.gpsimd.tensor_scalar(raw[:, k, :], raw[:, k, :], unit[:, 1, 1:2], None, ALU.mult).then_inc(act_link, 1)
                if q:
                    low_of_first(pool, q - 1)
            low_of_first(pool, 3)

        @block.scalar
        def _(act):
            act.sem_inc(y_sq, 2)

            def sum_absolutes(s, b):
                nc.scalar.activation(w16[:, b, 1, :, :].bitcast(BF16), raw, ACT.Abs, accum_out=size[:, b:b + 1]).then_inc(w_summed, 1)

            def split_high(s, b, q):
                k = slice(4 * q, 4 * q + 4)
                nc.scalar.activation(raw[:, k, :], raw[:, k, :], ACT.Copy, scale=unit[:, 1 + b, 1:2]).then_inc(act_link, 1)
                act.wait_ge(act_link, 4 * s + (q + 1))
                nc.scalar.activation(w16[:, b, 0, k, :], raw[:, k, :], ACT.Copy).then_inc(w_high, 1)

            def square(s, b, t):
                act.wait_ge(banks_free, TILES_F * s + (t + 1 + RING))
                act.wait_ge(y_sq, TILES_F * s + (t + 1))
                n = rows(t)
                nc.scalar.activation(sq[0:n, (TILES_F * b + t) % 2, :], slab(y[0:n, t, :], s), ACT.Square,
                                     accum_out=ss[0:n, t, bass.ds(s, 1)]).then_inc(y_sq, 1)

            def slab_squares(s, b):
                for t in range(TILES_F):
                    square(s, b, t)
                    if t == 0:
                        act.wait_ge(w_loaded, 16 * s + 16)
                        sum_absolutes(s + 1, 1 - b)
                    if t == 4:
                        act.wait_ge(unit_ready, s + 4)
                    if 4 <= t < 8:
                        split_high(s + 1, 1 - b, t - 4)

            nc.scalar.activation(m16[:, 0, 0, 0:KT * NS].bitcast(BF16).rearrange("p (k n) -> p k n", k=KT), mixT[:, :, SEQ:TOK], ACT.Abs,
                                 accum_out=mix_size[:, KT:KT + 1])
            act.wait_ge(w_first, 16)
            sum_absolutes(0, 0)
            act.wait_ge(unit_ready, 2)
            for q in range(4):
                for k in range(4 * q, 4 * q + 4):
                    nc.scalar.activation(m16[:, 0, k, :], mixT[:, k, :], ACT.Copy, scale=unit[:, 0, 1:2]).then_inc(m_high, 1)
                act.wait_ge(act_link, q + 1)
                nc.scalar.activation(w16[:, 0, 0, 4 * q:4 * q + 4, :], raw[:, 4 * q:4 * q + 4, :], ACT.Copy).then_inc(w_high, 1)
            with act.Fori(0, NSLAB // 2 - 1) as it:
                for b in range(2):
                    slab_squares(it * 2 + b, b)
            slab_squares(NSLAB - 2, 0)
            for t in range(TILES_F):
                square(NSLAB - 1, 1, t)
                act.wait_ge(ms_ready, t + 1)
                n = rows(t)
                nc.scalar.activation(st[0:n, t, 2:3], st[0:n, t, 1:2], ACT.Sqrt).then_inc(rt_ready, 1)


_INS = ["x_prompt", "x_sample", "mem_prompt", "cache_k", "cache_v", "cache_kidx", "cache_mem_k", "cache_mem_v",
        "state_ssm_re", "state_ssm_im", "page_table", "g_norm", "w_in", "g_mem", "w_mem_kv", "lam_re", "lam_im",
        "log_dt", "b_re", "b_im", "c_re", "c_im", "d_skip", "w_glu", "w_out", "g_final"]
_OUTS = {
    "out_y_p": (1, SEQ, D_MODEL), "out_y_s": (DEC_BATCH, DEC_SEQ, D_MODEL),
    "out_k_p": (1, 1, SEQ, N_KV, HEAD_DIM), "out_v_p": (1, 1, SEQ, N_KV, HEAD_DIM), "out_kidx_p": (1, 1, SEQ, IDX_DIM),
    "out_mk": (1, 1, N_MEM, N_MEM_HEADS, HEAD_DIM), "out_mv": (1, 1, N_MEM, N_MEM_HEADS, HEAD_DIM),
    "out_ssm_re_p": (1, 1, GROUPS, STATE), "out_ssm_im_p": (1, 1, GROUPS, STATE),
    "out_k_s": (1, DEC_BATCH, DEC_SEQ, N_KV, HEAD_DIM), "out_v_s": (1, DEC_BATCH, DEC_SEQ, N_KV, HEAD_DIM),
    "out_kidx_s": (1, DEC_BATCH, DEC_SEQ, IDX_DIM),
    "out_ssm_re_s": (1, DEC_BATCH, GROUPS, STATE), "out_ssm_im_s": (1, DEC_BATCH, GROUPS, STATE),
}


def kernel(**inputs):
    import numpy as _np
    import concourse.bacc as _bacc
    from concourse import mybir as _mybir
    from concourse.bass_utils import run_bass_kernel_spmd as _run

    nc = _bacc.Bacc("TRN2", target_bir_lowering=False, num_devices=1)
    arrays, io = {}, {}
    for name in _INS:
        a = _np.ascontiguousarray(inputs[name])
        arrays[f"in_{name}_dram"] = a
        io[name] = nc.dram_tensor(f"in_{name}_dram", a.shape, _mybir.dt.from_np(a.dtype), kind="ExternalInput").ap()
    for name, shape in _OUTS.items():
        io[name] = nc.dram_tensor(f"{name}_dram", shape, F32, kind="ExternalOutput").ap()
    build_program(nc, io)
    r = _run(nc, [arrays], core_ids=[0])
    return tuple(r.results[0][f"{name}_dram"] for name in _OUTS)
```
